# Optimizing a Trainium2 kernel written in Bass

```python
import math
import jax, jax.numpy as jnp
from jax import lax
import numpy as np

D_MODEL = 1024
BATCH = 1
SEQ = 128
DEPTH = 2
DEC_BATCH = 1
DEC_SEQ = 256
PAST_LEN = 128

GRID_W = 64
EPS = 1e-6
SSD_HEADS = 16
SSD_HEAD_DIM = 64
D_INNER = SSD_HEADS * SSD_HEAD_DIM
SSD_GROUPS = 2
HEADS_PER_GROUP = SSD_HEADS // SSD_GROUPS
SSD_STATE = 128
SSD_CONV = 3
SSD_CHUNK = 128
CONV_CH = D_INNER + 2 * SSD_GROUPS * SSD_STATE
MLA_HEADS = 16
Q_LORA = 384
KV_LORA = 256
QK_NOPE = 64
ROPE_DIM = 32
V_DIM = 64
ROPE_THETA = 10000.0
Q_BLOCK = 128
ATTN_SCALE = (QK_NOPE + ROPE_DIM) ** -0.5
FFT_GROUPS = 4
FFT_GROUP_W = 256
FFT_W = FFT_GROUPS * FFT_GROUP_W
D_FF = 2816
FFN_CONV = 3
N_BRANCH = 3
OFF_XBC = D_INNER
OFF_DT = OFF_XBC + CONV_CH
OFF_QD = OFF_DT + 2 * SSD_HEADS
OFF_KVD = OFF_QD + Q_LORA
OFF_FFT = OFF_KVD + KV_LORA + ROPE_DIM
IN_COLS = OFF_FFT + FFT_W

kernel_name = "hybrid_ssd_mla_fnet_diffusion_step"

def rms_norm(x, g):
    xf = x.astype(jnp.float32)
    y = xf * lax.rsqrt(jnp.mean(xf * xf, axis=-1, keepdims=True) + EPS)
    return (y * g.astype(jnp.float32)).astype(x.dtype)

def adaln_params(cvec, w, b):
    m = jax.nn.silu(cvec) @ w + b
    return jnp.split(m[:, None, :], 6, axis=-1)

def dwconv_centred(x, w, b):
    k = w.shape[0]
    y = lax.conv_general_dilated(x, w[:, None, :].astype(x.dtype), (1,), [(k // 2, k // 2)],
                                 dimension_numbers=("NWC", "WIO", "NWC"),
                                 feature_group_count=x.shape[-1])
    return y + b

def rope_2d(x):
    n = x.shape[1]
    rows = n // GRID_W
    row = jnp.repeat(jnp.arange(rows), GRID_W)
    col = jnp.tile(jnp.arange(GRID_W), rows)
    quarter = ROPE_DIM // 4
    inv = ROPE_THETA ** (-jnp.arange(quarter, dtype=jnp.float32) / quarter)
    bshape = (n,) + (1,) * (x.ndim - 3) + (quarter,)

    def rot(xa, pos):
        ang = (pos.astype(jnp.float32)[:, None] * inv).reshape(bshape)
        cos, sin = jnp.cos(ang).astype(x.dtype), jnp.sin(ang).astype(x.dtype)
        x1, x2 = jnp.split(xa, 2, axis=-1)
        return jnp.concatenate([x1 * cos - x2 * sin, x1 * sin + x2 * cos], axis=-1)

    x_row, x_col = jnp.split(x, 2, axis=-1)
    return jnp.concatenate([rot(x_row, row), rot(x_col, col)], axis=-1)

def ssd_scan(x, dt, a, bm, cm, h0):
    b, l, g, e, p = x.shape
    n = bm.shape[-1]
    nc = l // SSD_CHUNK
    f32 = jnp.float32
    xdt = (x.astype(f32) * dt[..., None]).reshape(b, nc, SSD_CHUNK, g, e, p)
    bc = bm.astype(f32).reshape(b, nc, SSD_CHUNK, g, n)
    cc = cm.astype(f32).reshape(b, nc, SSD_CHUNK, g, n)
    a_cum = jnp.cumsum((dt * a).reshape(b, nc, SSD_CHUNK, g, e), axis=2)
    lower = jnp.tril(jnp.ones((SSD_CHUNK, SSD_CHUNK), bool))[:, :, None, None]
    seg = a_cum[:, :, :, None] - a_cum[:, :, None, :]
    decay = jnp.where(lower, jnp.exp(jnp.where(lower, seg, 0.0)), 0.0)
    cb = jnp.einsum("bcign,bcjgn->bcijg", cc, bc)
    y_diag = jnp.einsum("bcijg,bcijge,bcjgep->bcigep", cb, decay, xdt)
    to_end = jnp.exp(a_cum[:, :, -1:] - a_cum)
    chunk_states = jnp.einsum("bcjgn,bcjge,bcjgep->bcgepn", bc, to_end, xdt)
    chunk_decay = jnp.exp(a_cum[:, :, -1])

    def step(h, inp):
        s, d = inp
        return h * d[..., None, None] + s, h

    h_last, h_enter = lax.scan(step, h0.astype(f32),
                               (jnp.moveaxis(chunk_states, 1, 0), jnp.moveaxis(chunk_decay, 1, 0)))
    h_enter = jnp.moveaxis(h_enter, 0, 1)
    y_off = jnp.einsum("bcign,bcige,bcgepn->bcigep", cc, jnp.exp(a_cum), h_enter)
    y = (y_diag + y_off).reshape(b, l, g, e, p)
    return y.astype(x.dtype), h_last.astype(x.dtype)

def flip_seq(t):
    return jnp.flip(t, axis=1)

def ssd_branch(z, xbc, dt_raw, h0, lw):
    b, l, _ = z.shape
    f32 = jnp.float32
    xbc = jax.nn.silu(dwconv_centred(xbc, lw["conv_ssd_w"], lw["conv_ssd_b"]))
    xs = xbc[..., :D_INNER].reshape(b, l, SSD_GROUPS, HEADS_PER_GROUP, SSD_HEAD_DIM)
    bm = xbc[..., D_INNER:D_INNER + SSD_GROUPS * SSD_STATE].reshape(b, l, SSD_GROUPS, SSD_STATE)
    cm = xbc[..., D_INNER + SSD_GROUPS * SSD_STATE:].reshape(b, l, SSD_GROUPS, SSD_STATE)
    dt = jax.nn.softplus(dt_raw.astype(f32).reshape(b, l, 2, SSD_GROUPS, HEADS_PER_GROUP)
                         + lw["dt_bias"].astype(f32).reshape(2, SSD_GROUPS, HEADS_PER_GROUP))
    a = -jnp.exp(lw["a_log"].astype(f32)).reshape(2, SSD_GROUPS, HEADS_PER_GROUP)
    h0 = h0.reshape(b, 2, SSD_GROUPS, HEADS_PER_GROUP, SSD_HEAD_DIM, SSD_STATE)
    y_f, h_f = ssd_scan(xs, dt[:, :, 0], a[0], bm, cm, h0[:, 0])
    y_b, h_b = ssd_scan(flip_seq(xs), flip_seq(dt[:, :, 1]), a[1], flip_seq(bm), flip_seq(cm), h0[:, 1])
    y = y_f + flip_seq(y_b) + lw["d_skip"].reshape(SSD_GROUPS, HEADS_PER_GROUP, 1) * xs
    y = rms_norm(y.reshape(b, l, D_INNER) * jax.nn.silu(z), lw["g_ssd_norm"])
    h_final = jnp.stack([h_f, h_b], axis=1).reshape(b, 2, SSD_HEADS, SSD_HEAD_DIM, SSD_STATE)
    return y @ lw["w_ssd_out"], h_final

def mla_attend(q_nope, q_pe, ckv, kpe, w_kv_up):
    b, lq = q_nope.shape[:2]
    kv = jnp.einsum("bkr,rhd->bkhd", ckv, w_kv_up.reshape(KV_LORA, MLA_HEADS, QK_NOPE + V_DIM))
    k_nope, v = kv[..., :QK_NOPE], kv[..., QK_NOPE:]
    nb = lq // Q_BLOCK

    def to_blocks(t):
        return jnp.moveaxis(t.reshape((b, nb, Q_BLOCK) + t.shape[2:]), 1, 0)

    def one_block(args):
        qn, qp = args
        s = (jnp.einsum("bqhd,bkhd->bhqk", qn, k_nope)
             + jnp.einsum("bqhr,bkr->bhqk", qp, kpe))
        pr = jax.nn.softmax(s.astype(jnp.float32) * ATTN_SCALE, axis=-1).astype(v.dtype)
        return jnp.einsum("bhqk,bkhd->bqhd", pr, v)

    o = lax.map(one_block, (to_blocks(q_nope), to_blocks(q_pe)))
    return jnp.moveaxis(o, 0, 1).reshape(b, lq, MLA_HEADS * V_DIM)

def fourier_branch(f):
    b, l, _ = f.shape
    fg = f.astype(jnp.float32).reshape(b, l, FFT_GROUPS, FFT_GROUP_W)
    mixed = jnp.fft.fft2(fg, axes=(1, 3), norm="ortho").real
    return mixed.reshape(b, l, FFT_W).astype(f.dtype)

def token_mixing(h, lw, ctx):
    b, l, _ = h.shape
    proj = h @ lw["w_in"]
    z = proj[..., :OFF_XBC]
    xbc = proj[..., OFF_XBC:OFF_DT]
    dt_raw = proj[..., OFF_DT:OFF_QD]
    q_down = proj[..., OFF_QD:OFF_KVD]
    kv_down = proj[..., OFF_KVD:OFF_FFT]
    f_in = proj[..., OFF_FFT:]
    q = (rms_norm(q_down, lw["g_q_norm"]) @ lw["w_q_up"]).reshape(b, l, MLA_HEADS, QK_NOPE + ROPE_DIM)
    q_nope, q_pe = q[..., :QK_NOPE], q[..., QK_NOPE:]
    ckv = rms_norm(kv_down[..., :KV_LORA], lw["g_kv_norm"])
    kpe = kv_down[..., KV_LORA:]
    if ctx is None:
        h0 = jnp.zeros((b, 2, SSD_HEADS, SSD_HEAD_DIM, SSD_STATE), h.dtype)
        keys_ckv, keys_kpe = ckv, kpe
    else:
        ckv_ctx, kpe_ctx, h0 = ctx
        q_pe = rope_2d(q_pe)
        keys_ckv = jnp.concatenate([ckv, ckv_ctx.astype(ckv.dtype)], axis=1)
        keys_kpe = jnp.concatenate([rope_2d(kpe), kpe_ctx.astype(kpe.dtype)], axis=1)
    o_mla = mla_attend(q_nope, q_pe, keys_ckv, keys_kpe, lw["w_kv_up"]) @ lw["w_mla_out"]
    o_ssd, h_final = ssd_branch(z, xbc, dt_raw, h0, lw)
    o_fft = fourier_branch(f_in) @ lw["w_fft_out"]
    gates = jax.nn.sigmoid(h @ lw["w_gate"] + lw["b_gate"])
    g_ssd, g_mla, g_fft = jnp.split(gates, N_BRANCH, axis=-1)
    out = (g_ssd * o_ssd + g_mla * o_mla + g_fft * o_fft) @ lw["w_o"]
    return out, (ckv, kpe, h_final)

def conv_mlp(h, lw):
    u = dwconv_centred(h @ lw["w_up"], lw["conv_ffn_w"], lw["conv_ffn_b"])
    a, g = jnp.split(u, 2, axis=-1)
    return (jax.nn.silu(a) * g) @ lw["w_down"]

def trunk_layer(x, cvec, lw, ctx):
    sh1, sc1, g1, sh2, sc2, g2 = adaln_params(cvec, lw["w_ada"], lw["b_ada"])
    h = rms_norm(x, lw["g_pre_mix"]) * (1 + sc1) + sh1
    mix, ctx_out = token_mixing(h, lw, ctx)
    x = x + g1 * rms_norm(mix, lw["g_post_mix"])
    h = rms_norm(x, lw["g_pre_ffn"]) * (1 + sc2) + sh2
    x = x + g2 * rms_norm(conv_mlp(h, lw), lw["g_post_ffn"])
    return x, ctx_out

def setup_inputs(seed: int = 0) -> dict:
    key = jax.random.key(seed)
    keys = iter(jax.random.split(key, 64))
    L, D = DEPTH, D_MODEL

    def normal(shape, scale):
        return jax.random.normal(next(keys), shape, jnp.float32) * scale

    def gain(shape):
        return 1.0 + normal(shape, 0.05)

    dt0 = jnp.exp(jax.random.uniform(next(keys), (L, 2, SSD_HEADS), jnp.float32,
                                     math.log(1e-3), math.log(1e-1)))
    dt_bias = dt0 + jnp.log(-jnp.expm1(-dt0))
    a_log = jnp.log(jax.random.uniform(next(keys), (L, 2, SSD_HEADS), jnp.float32, 1.0, 16.0))
    return {
        "x_prompt": normal((BATCH, SEQ, D), 1.0),
        "x_sample": normal((DEC_BATCH, DEC_SEQ, D), 1.0),
        "cache_ckv": normal((DEC_BATCH, L, PAST_LEN, KV_LORA), 1.0),
        "cache_kpe": normal((DEC_BATCH, L, PAST_LEN, ROPE_DIM), 1.0),
        "state_ssm": normal((DEC_BATCH, L, 2, SSD_HEADS, SSD_HEAD_DIM, SSD_STATE), 0.3),
        "c": normal((DEC_BATCH, D), 1.0),
        "c_ctx": normal((D,), 1.0),
        "w_ada": normal((L, D, 6 * D), 0.5 * D ** -0.5),
        "b_ada": normal((L, 6 * D), 0.01),
        "g_pre_mix": gain((L, D)),
        "g_post_mix": gain((L, D)),
        "g_pre_ffn": gain((L, D)),
        "g_post_ffn": gain((L, D)),
        "w_in": normal((L, D, IN_COLS), D ** -0.5),
        "w_gate": normal((L, D, N_BRANCH * D), D ** -0.5),
        "b_gate": normal((L, N_BRANCH * D), 0.01),
        "w_o": normal((L, D, D), D ** -0.5),
        "conv_ssd_w": normal((L, SSD_CONV, CONV_CH), SSD_CONV ** -0.5),
        "conv_ssd_b": normal((L, CONV_CH), 0.01),
        "dt_bias": dt_bias,
        "a_log": a_log,
        "d_skip": gain((L, SSD_HEADS)),
        "g_ssd_norm": gain((L, D_INNER)),
        "w_ssd_out": normal((L, D_INNER, D), D_INNER ** -0.5),
        "g_q_norm": gain((L, Q_LORA)),
        "w_q_up": normal((L, Q_LORA, MLA_HEADS * (QK_NOPE + ROPE_DIM)), Q_LORA ** -0.5),
        "g_kv_norm": gain((L, KV_LORA)),
        "w_kv_up": normal((L, KV_LORA, MLA_HEADS * (QK_NOPE + V_DIM)), KV_LORA ** -0.5),
        "w_mla_out": normal((L, MLA_HEADS * V_DIM, D), (MLA_HEADS * V_DIM) ** -0.5),
        "w_fft_out": normal((L, FFT_W, D), FFT_W ** -0.5),
        "w_up": normal((L, D, 2 * D_FF), D ** -0.5),
        "conv_ffn_w": normal((L, FFN_CONV, 2 * D_FF), FFN_CONV ** -0.5),
        "conv_ffn_b": normal((L, 2 * D_FF), 0.01),
        "w_down": normal((L, D_FF, D), D_FF ** -0.5),
    }

def reference(x_prompt, x_sample, cache_ckv, cache_kpe, state_ssm, c, c_ctx,
              w_ada, b_ada, g_pre_mix, g_post_mix, g_pre_ffn, g_post_ffn,
              w_in, w_gate, b_gate, w_o, conv_ssd_w, conv_ssd_b, dt_bias, a_log, d_skip,
              g_ssd_norm, w_ssd_out, g_q_norm, w_q_up, g_kv_norm, w_kv_up, w_mla_out,
              w_fft_out, w_up, conv_ffn_w, conv_ffn_b, w_down):
    params = {
        "w_ada": w_ada, "b_ada": b_ada, "g_pre_mix": g_pre_mix, "g_post_mix": g_post_mix,
        "g_pre_ffn": g_pre_ffn, "g_post_ffn": g_post_ffn, "w_in": w_in, "w_gate": w_gate,
        "b_gate": b_gate, "w_o": w_o, "conv_ssd_w": conv_ssd_w, "conv_ssd_b": conv_ssd_b,
        "dt_bias": dt_bias, "a_log": a_log, "d_skip": d_skip, "g_ssd_norm": g_ssd_norm,
        "w_ssd_out": w_ssd_out, "g_q_norm": g_q_norm, "w_q_up": w_q_up, "g_kv_norm": g_kv_norm,
        "w_kv_up": w_kv_up, "w_mla_out": w_mla_out, "w_fft_out": w_fft_out, "w_up": w_up,
        "conv_ffn_w": conv_ffn_w, "conv_ffn_b": conv_ffn_b, "w_down": w_down,
    }
    y_prompt, y_sample = x_prompt, x_sample
    ckv_list, kpe_list, ssm_list = [], [], []
    c_context = c_ctx[None, :]
    for i in range(DEPTH):
        lw = {name: arr[i] for name, arr in params.items()}
        y_prompt, (ckv, kpe, ssm) = trunk_layer(y_prompt, c_context, lw, None)
        ckv_list.append(ckv)
        kpe_list.append(kpe)
        ssm_list.append(ssm)
        y_sample, _ = trunk_layer(y_sample, c, lw,
                                  (cache_ckv[:, i], cache_kpe[:, i], state_ssm[:, i]))
    new_ckv = jnp.stack(ckv_list, axis=1)
    new_kpe = jnp.stack(kpe_list, axis=1)
    new_ssm = jnp.stack(ssm_list, axis=1)
    return (y_prompt, y_sample, new_ckv, new_kpe, new_ssm)


_drawn_inputs = setup_inputs


def setup_inputs(seed=0):
    import zlib

    import numpy as np

    out = dict(_drawn_inputs(seed))
    spreads = {}
    factors = {'cache_ckv': 3.454,
     'cache_kpe': 6.627,
     'g_post_mix': 2.748,
     'g_post_ffn': 2.867,
     'b_gate': 8.0,
     'conv_ssd_b': 3.471,
     'd_skip': 8.0,
     'g_ssd_norm': 3.654,
     'g_q_norm': 8.0,
     'conv_ffn_b': 8.0}
    for name, (base, spread) in spreads.items():
        noise = np.random.default_rng([zlib.crc32(name.encode()), seed]).standard_normal(out[name].shape)
        drawn = base * np.exp(spread * noise) if base else spread * noise
        out[name] = __import__('jax').numpy.asarray(drawn.astype(out[name].dtype))
    for name, factor in factors.items():
        out[name] = (out[name] * factor).astype(out[name].dtype)
    return out
```

```python
from contextlib import ExitStack

import numpy as np

import concourse.bass as bass
from concourse import mybir

F32 = mybir.dt.float32
F32R = mybir.dt.float32r
ALU = mybir.AluOpType
ACT = mybir.ActivationFunctionType
AX = mybir.AxisListType

P = 128
LAYERS = 2
CTX, LAT, PAST = 128, 256, 128
T = CTX + LAT
KEYS = T + PAST
D = 1024
DB = D // P
HEADS = 16
HALF = HEADS // 2
HD = 64
STATE = 128
ROPE = 32
QL, KVL = 384, 256
QB, KVB = QL // P, KVL // P
XBC_B = 12
FF_B = 22
FF_H = FF_B // 2
GROUP_W = 256
GROUPS = 4
EPS = 1e-6
ATTN_SCALE = float((HD + ROPE) ** -0.5)
SEGS = ((0, CTX), (CTX, T))
CHUNKS = T // P

RING = 4
AHEAD = 2
STAGES = {}
TILES = 0
for _name, _count in (("ada", 48), ("proj", 18), ("z", 8), ("out_ssd", 16), ("heads0", 8), ("heads1", 8),
                      ("out_mla", 16), ("f", 8), ("out_fft", 16), ("w_o", 8),
                      ("up0", 22), ("down0", 11), ("up1", 22), ("down1", 11)):
    STAGES[_name] = (TILES, _count)
    TILES += _count
TURNS = TILES // RING
assert TILES % RING == 0

PARAMS = {}
N_PARAMS = 0
for _name, _count in (("b_ada", 48), ("g_pre_mix", 8), ("g_post_mix", 8), ("g_pre_ffn", 8), ("g_post_ffn", 8),
                      ("b_gate", 24), ("conv_w", 36), ("conv_b", 12), ("ffn_w", 132), ("ffn_b", 44),
                      ("d_skip", 8), ("g_ssd", 8), ("g_q", 3), ("g_kv", 2), ("dt_bias", 32), ("a_log", 32)):
    PARAMS[_name] = (N_PARAMS, _count)
    N_PARAMS += _count

CONSTS = {}
N_CONSTS = 0
for _name, _count in (("ident", 128), ("tri", 256), ("ones", 128), ("rope", T), ("dft_ch", 2 * 512),
                      ("dft_lat", 2 * 2 * 256), ("dft_ctx", 2 * 128)):
    CONSTS[_name] = (N_CONSTS, _count)
    N_CONSTS += _count
N_KEPT = CONSTS["dft_ch"][0]
N_DFT = N_CONSTS - N_KEPT


class Signal:

    def __init__(self, sem, per_layer):
        self.sem, self.per_layer = sem, per_layer

    def at(self, layer, n):
        return layer * self.per_layer + n


DVE_LINKS = 45
ACT_LINKS = 0


def build_program(nc, a_x, a_cond, a_state, a_ckv, a_kpe, a_params, a_consts, a_weights,
                  o_x, o_ckv, o_kpe, o_state):
    ctx = ExitStack()
    with ctx:
        def sb(name, shape, dt=F32):
            return ctx.enter_context(nc.sbuf_tensor(name, shape, dt))

        def sem(name):
            return ctx.enter_context(nc.semaphore(name))

        def signal(name, per_layer):
            return Signal(sem(name), per_layer)

        consts = sb("consts", [P, N_KEPT])
        params = sb("params", [P, N_PARAMS])
        raw = sb("raw", [P, RING, 1024])
        w_hi = sb("w_hi", [P, AHEAD, 1024], F32R)
        w_lo = sb("w_lo", [P, AHEAD, 1024], F32R)
        x = sb("x", [P, DB, T])
        cond = sb("cond", [P, DB, 2])
        c_parts = sb("c_parts", [P, DB, 4], F32R)
        fold = sb("fold", [4, 2])
        mod = sb("mod", [P, 48, 2])
        coef = sb("coef", [P, 6, DB, 2])
        h_hi = sb("h_hi", [P, DB, T], F32R)
        h_lo = sb("h_lo", [P, DB, T], F32R)
        in_hi = sb("in_hi", [P, DB * T + KVB * KEYS + QB * T], F32R)
        in_lo = sb("in_lo", [P, DB * T + KVB * KEYS + QB * T], F32R)
        y_hi, y_lo = (v[:, 0:FF_H * T].rearrange("p (k n) -> p k n", k=FF_H) for v in (in_hi, in_lo))
        kvq_hi, kvq_lo = (v[:, DB * T:] for v in (in_hi, in_lo))
        wide = sb("wide", [P, DB, T])
        mix = sb("mix", [P, DB, T])
        root = sb("root", [P, T])
        rstd = sb("rstd", [P, T])
        conv = sb("conv", [P, AHEAD, T])
        gate = sb("gate", [P, T])
        gated = sb("gated", [P, T])
        kpe = sb("kpe", [96, KEYS])
        kpe_raw = sb("kpe_raw", [96, CTX])
        low = mix[:, 0:KVB + QB, :]
        ckv = sb("ckv", [P, KVB, KEYS])
        stat = sb("stat", [P, 64])
        region = sb("region", [P, 12 * 1024])

        def view(at, shape):
            n = int(np.prod(shape))
            v = region[:, at:at + n]
            names = [chr(97 + i) for i in range(len(shape))]
            if len(shape) == 1:
                return v
            return v.rearrange(f"p ({' '.join(names)}) -> p {' '.join(names)}",
                               **dict(zip(names[1:], shape[1:])))

        K1 = HEADS * HD
        tok_major = "p k n -> p (k n)"
        mod_rows = region[0:4, 0:48 * P]
        xbc = view(0, [XBC_B, T])
        b_tok = view(4608, [CHUNKS, 256])
        cbm = view(5376, [2, CHUNKS * 2, P])
        xdt = view(6912, [2, K1])
        decay = view(8960, [2 * HALF, P])
        h_state = view(8960, [2, K1])
        x_end = view(6912, [K1])
        scaled = view(6912 + 1024, [K1])
        xs_tok = mix[:, :, :].rearrange(tok_major).rearrange("p (c n) -> p c n", c=CHUNKS)
        y_tok = wide[:, :, :].rearrange(tok_major).rearrange("p (c n) -> p c n", c=CHUNKS)
        q_t = view(0, [HALF, T])
        k_t = view(3072, [HALF, KEYS])
        v_tok = view(7168, [4, 512])
        prob = view(9216, [2, 2, T])
        prob_t = view(10752, [2, T])
        rot = view(11520, [2, T])
        o_tok = y_tok
        f_ch = view(0, [CHUNKS, GROUPS, 512])
        dft = view(12288 - N_DFT, [N_DFT])

        dts = sb("dts", [P, 12, CHUNKS * 32])
        dt_t = gated[0:32, :]

        ps = ctx.enter_context(nc.psum_tensor("ps", [P, 8, 512], F32))
        flat = ps[:, :, :].rearrange("p b n -> p (b n)")

        def const(name):
            at, n = CONSTS[name]
            return consts[:, at:at + n] if at < N_KEPT else dft[:, at - N_KEPT:at - N_KEPT + n]

        def param(name, i=0, n=1):
            at = PARAMS[name][0]
            return params[:, at + i:at + i + n]

        ident = const("ident")
        ones = const("ones")
        tri = [const("tri")[:, 0:P], const("tri")[:, P:2 * P]]
        dft_ch = const("dft_ch").rearrange("p (k n) -> p k n", k=2)
        dft_lat = const("dft_lat").rearrange("p (k s n) -> p k s n", k=2, s=2)
        dft_ctx = const("dft_ctx").rearrange("p (s n) -> p s n", s=2)
        rope = const("rope")
        ckv_hi = kvq_hi[:, 0:KVB * KEYS].rearrange("p (k n) -> p k n", k=KVB)
        ckv_lo = kvq_lo[:, 0:KVB * KEYS].rearrange("p (k n) -> p k n", k=KVB)
        q_hi = kvq_hi[:, KVB * KEYS:].rearrange("p (k n) -> p k n", k=QB)
        q_lo = kvq_lo[:, KVB * KEYS:].rearrange("p (k n) -> p k n", k=QB)

        loaded = sem("loaded")
        stored = sem("stored")
        arrived = [Signal(sem(f"arrived{j}"), 16 * TURNS) for j in range(RING)]
        hi_made = signal("hi_made", TILES)
        lo_made = signal("lo_made", TILES)
        used = signal("used", TILES)
        taken = signal("taken", TILES)
        ready = sem("ready")
        c_split = sem("c_split")
        pool_marks, pe_marks, dve_marks = sem("pool_marks"), sem("pe_marks"), sem("dve_marks")
        squares = signal("squares", 7)
        sums = signal("sums", 7)
        roots = signal("roots", 7)
        mod_made = signal("mod_made", 1)
        h_value = signal("h_value", 2 * DB)
        h_hi_made = signal("h_hi_made", 2 * DB)
        h_lo_made = signal("h_lo_made", 2 * DB)
        kvq_value = signal("kvq_value", 5)
        kvq_hi_made = signal("kvq_hi_made", 5)
        kvq_lo_made = signal("kvq_lo_made", 5)
        y_value = signal("y_value", 2 * DB)
        y_hi_made = signal("y_hi_made", 4 * DB + FF_B)
        y_lo_made = signal("y_lo_made", 4 * DB + FF_B)
        conv_mid = signal("conv_mid", XBC_B + 2 * FF_B)
        conv_left = signal("conv_left", XBC_B + 2 * FF_B)
        conv_done = signal("conv_done", XBC_B + 2 * FF_B)
        silu_done = signal("silu_done", XBC_B + FF_B + DB)
        ag_value = signal("ag_value", FF_B)
        misc_copied = signal("misc_copied", 1)
        cache_in = signal("cache_in", 32)
        params_in = signal("params_in", 16)
        caches_free = signal("caches_free", 1)
        kpe_ready = signal("kpe_ready", 3)
        kpe_spread = signal("kpe_spread", 1)
        ckv_ready = signal("ckv_ready", 1)
        transposed = signal("transposed", CHUNKS)
        tok_ready = signal("tok_ready", CHUNKS)
        dt_ready = signal("dt_ready", 1)
        acum_sums = signal("acum_sums", 1)
        exps_ready = signal("exps_ready", 1)
        cb_made = signal("cb_made", 1)
        xdt_ready = signal("xdt_ready", CHUNKS)
        rows_made = signal("rows_made", 2 * CHUNKS)
        segs_ready = signal("segs_ready", 2 * CHUNKS)
        decay_ready = signal("decay_ready", 2 * CHUNKS)
        masked = signal("masked", 2 * CHUNKS)
        y_diag = signal("y_diag", 2 * CHUNKS)
        y_taken = signal("y_taken", 1 * CHUNKS)
        state_in = signal("state_in", 16)
        state_free = signal("state_free", 1)
        ends_ready = signal("ends_ready", 4)
        states_made = signal("states_made", 4)
        states_taken = signal("states_taken", 4)
        off_ready = signal("off_ready", 4)
        off_made = signal("off_made", 4)
        off_taken = signal("off_taken", 4)
        new_state = signal("new_state", 2)
        state_out = signal("state_out", 32)
        y_turned = signal("y_turned", DB)
        y_back = signal("y_back", DB)
        gate_made = signal("gate_made", 3 * DB)
        q_plain = signal("q_plain", HALF)
        q_rot = signal("q_rot", 3 * HALF)
        k_even = signal("k_even", 4)
        k_odd = signal("k_odd", 4)
        v_ready = signal("v_ready", 4)
        N_PAIR = 2 * CHUNKS * (HALF // 2)
        scored = signal("scored", N_PAIR)
        maxed = signal("maxed", 2 * N_PAIR)
        exped = signal("exped", N_PAIR)
        p_turned = signal("p_turned", 2 * N_PAIR)
        p_back = signal("p_back", 2 * N_PAIR)
        o_made = signal("o_made", N_PAIR)
        o_taken = signal("o_taken", 4 * CHUNKS)
        o_turned = signal("o_turned", DB)
        dft_in = signal("dft_in", 16)
        f_ready = signal("f_ready", DB)
        ch_made = signal("ch_made", CHUNKS * GROUPS)
        ch_taken = signal("ch_taken", CHUNKS * GROUPS)
        pos_made = signal("pos_made", DB)
        wo_ready = signal("wo_ready", DB)
        down_made = signal("down_made", 2)
        down_taken = signal("down_taken", 2)
        x_ready = signal("x_ready", 1)
        x_mid = signal("x_mid", 1)
        dt_abs = signal("dt_abs", 1)
        dt_exp = signal("dt_exp", 2)
        to_end = signal("to_end", 1)
        mixed = signal("mixed", 1 + 2 * DB)
        dve_chain = signal("dve_chain", DVE_LINKS)
        act_chain = signal("act_chain", ACT_LINKS)

        def through(eng, stage, body):
            t, count = STAGES[stage]
            first, end = t, t + count
            while t % RING and t < end:
                body(t, t // RING, t % RING, t - first)
                t += 1
            turns = (end - t) // RING
            if turns > 1:
                with eng.Fori(0, turns) as r:
                    for j in range(RING):
                        body(r * RING + (t + j), r + t // RING, j, r * RING + (t + j - first))
                t += turns * RING
            while t < end:
                body(t, t // RING, t % RING, t - first)
                t += 1

        def at_tile(slot, name="raw"):
            return raw[:, slot % RING, :]

        def settle(eng, mark):
            eng.sem_inc(mark, 1)

        def after(dve):
            settle(dve, dve_marks)
            return dve.engine_nop()

        def spread(ap, n):
            return ap.unsqueeze(2).broadcast_to([ap.shape[0], ap.shape[1], n])

        def repeat(ap, n):
            return ap.unsqueeze(1).broadcast_to([ap.shape[0], n, ap.shape[1]])

        def ssd(pe, L):
            for c in range(CHUNKS):
                at = (0, 3, 0)[c] * 512
                if c == 2:
                    pe.wait_ge(tok_ready.sem, tok_ready.at(L, 1))
                cols = slice(c * P, (c + 1) * P)
                for b in range(10):
                    pe.transpose(flat[:, at + b * P:at + (b + 1) * P], xbc[:, b, cols], ident)
                m = pe.transpose(flat[:, at + 10 * P:at + 10 * P + 32], dt_t[:, cols], ident[0:32, 0:32])
                m.then_inc(transposed.sem, 1)
            for c in range(CHUNKS):
                cols = slice(c * P, (c + 1) * P)
                for g in range(2):
                    m = pe.matmul(flat[:, 6 * 512 + (2 * c + g) * P:6 * 512 + (2 * c + g + 1) * P],
                                  xbc[:, 8 + g, cols], xbc[:, 10 + g, cols], start=True, stop=True)
            m.then_inc(cb_made.sem, 1)
            pe.wait_ge(dt_ready.sem, dt_ready.at(L, 1))
            pe.wait_ge(tok_ready.sem, tok_ready.at(L, CHUNKS))
            dta = dts[:, 1, :].rearrange("p (c d h) -> p c d h", c=CHUNKS, d=2)
            for d in range(2):
                pe.matmul(ps[:, 3, d * 48:(d + 1) * 48], tri[d], dta[:, :, d, :], start=True, stop=True)
            pe.matmul(ps[:, 3, 96:192], ones, dts[:, 1, :], start=True, stop=True).then_inc(acum_sums.sem, 1)
            pe.wait_ge(exps_ready.sem, exps_ready.at(L, 1))

            def rows(i):
                c, g = i // 2, i % 2
                if i:
                    pe.wait_ge(segs_ready.sem, segs_ready.at(L, i))
                for d in range(2):
                    for h in range(HALF):
                        one = dts[:, 1, c * 32 + d * 16 + g * HALF + h:c * 32 + d * 16 + g * HALF + h + 1]
                        m = pe.matmul(flat[:, 4 * 512 + (d * HALF + h) * P:4 * 512 + (d * HALF + h + 1) * P],
                                      one.broadcast_to([P, P]), tri[d], start=True, stop=True)
                m.then_inc(rows_made.sem, 1)

            pe.wait_ge(xdt_ready.sem, xdt_ready.at(L, 1))
            rows(0)
            for i in range(2 * CHUNKS):
                c, g = i // 2, i % 2
                if i + 1 < 2 * CHUNKS:
                    rows(i + 1)
                if g == 0 and c:
                    pe.wait_ge(y_taken.sem, y_taken.at(L, c))
                pe.wait_ge(xdt_ready.sem, xdt_ready.at(L, c + 1))
                pe.wait_ge(masked.sem, masked.at(L, i + 1))
                for h in range(HALF):
                    for d in range(2):
                        m = pe.matmul(ps[:, g, h * HD:(h + 1) * HD], decay[:, d * HALF + h, :],
                                      xdt[:, d, (g * HALF + h) * HD:(g * HALF + h + 1) * HD],
                                      start=(d == 0), stop=(d == 1))
                m.then_inc(y_diag.sem, 1)
            n_state = n_off = 0
            for d, c, what in SSD_STEPS:
                if what == "state":
                    pe.wait_ge(ends_ready.sem, ends_ready.at(L, n_state + 1))
                    for g in range(2):
                        m = pe.matmul(ps[:, 2 + g, :], b_tok[:, c, g * P:(g + 1) * P],
                                      x_end[:, g * 512:(g + 1) * 512], start=True, stop=True)
                    n_state += 1
                    m.then_inc(states_made.sem, 1)
                else:
                    pe.wait_ge(off_ready.sem, off_ready.at(L, n_off + 1))
                    for g in range(2):
                        m = pe.matmul(ps[:, 4 + g, :], xbc[:, 10 + g, c * P:(c + 1) * P],
                                      h_state[:, d, g * 512:(g + 1) * 512], start=True, stop=True)
                    n_off += 1
                    m.then_inc(off_made.sem, 1)
            pe.wait_ge(off_taken.sem, off_taken.at(L, 4))
            for b in range(DB):
                if b >= 4:
                    pe.wait_ge(y_back.sem, y_back.at(L, b - 3))
                for c in range(CHUNKS):
                    m = pe.transpose(ps[:, 4 + b % 4, c * P:(c + 1) * P], y_tok[:, c, b * P:(b + 1) * P], ident)
                m.then_inc(y_turned.sem, 1)

        def attention(pe, L, half, product, weights, tile_in):
            t0 = STAGES[f"heads{half}"][0]
            for i in range(4):
                t = t0 + i
                tile_in(L, t)
                if half == 0 and i == 0:
                    pe.wait_ge(kvq_lo_made.sem, kvq_lo_made.at(L, 5))
                for hh in range(2):
                    m = product(ps[:, 2 * (t % AHEAD) + hh, 0:T],
                                [(*weights(t, hh * QB + kk), q_hi[:, kk, :], q_lo[:, kk, :]) for kk in range(QB)])
                m.then_inc(used.sem, 1)
            for i in range(2):
                t = t0 + 4 + i
                tile_in(L, t)
                for b in range(2):
                    m = product(ps[:, 2 * (t % AHEAD) + b, :],
                                [(*weights(t, b * KVB + kk), ckv_hi[:, kk, :], ckv_lo[:, kk, :]) for kk in range(KVB)])
                m.then_inc(used.sem, 1)
            for i in range(2):
                t = t0 + 6 + i
                tile_in(L, t)
                for s in range(KEYS // P):
                    cols = slice(s * P, (s + 1) * P)
                    parts = []
                    for kk in range(KVB):
                        wh, wl = weights(t, 0, n=256, at=kk * 256)
                        parts.append((ckv_hi[:, kk, cols], ckv_lo[:, kk, cols], wh, wl))
                    m = product(ps[:, 2 * (t % AHEAD) + s // 2, (s % 2) * 256:(s % 2 + 1) * 256], parts)
                m.then_inc(used.sem, 1)
            pe.wait_ge(taken.sem, taken.at(L, t0 + 8 + AHEAD))
            pe.wait_ge(v_ready.sem, v_ready.at(L, 2 * half + 2))
            pe.wait_ge(kpe_spread.sem, kpe_spread.at(L, 1))

            pairs = [(qt, hp) for qt in range(CHUNKS) for hp in range(HALF // 2)]
            base = half * len(pairs)

            def scores(i):
                qt, hp = pairs[i]
                if i >= 2:
                    pe.wait_ge(exped.sem, exped.at(L, base + i - 1))
                lo, hi = (0, CTX) if qt == 0 else (CTX, KEYS)
                for hh in range(2):
                    h = 2 * hp + hh
                    m = pe.matmul(ps[:, 4 + 2 * (i % 2) + hh, 0:hi - lo], q_t[0:96, h, qt * P:(qt + 1) * P],
                                  k_t[0:96, h, lo:hi], start=True, stop=True)
                m.then_inc(scored.sem, 1)

            scores(0)
            for i, (qt, hp) in enumerate(pairs):
                if i + 1 < len(pairs):
                    scores(i + 1)
                n = 1 if qt == 0 else 3
                pe.wait_ge(exped.sem, exped.at(L, base + i + 1))
                for hh in range(2):
                    if base + i:
                        pe.wait_ge(p_back.sem, p_back.at(L, 2 * (base + i) + hh - 1))
                    for s in range(n):
                        m = pe.transpose(ps[:, hh, s * P:(s + 1) * P], prob[:, i % 2, hh, s * P:(s + 1) * P], ident)
                    m.then_inc(p_turned.sem, 1)
                for hh in range(2):
                    h = 2 * hp + hh
                    if hp == 0 and hh == 0 and base + i >= 4:
                        pe.wait_ge(o_taken.sem, o_taken.at(L, 2 * ((base + i) // 4) - 1))
                    pe.wait_ge(p_back.sem, p_back.at(L, 2 * (base + i) + hh + 1))
                    for s in range(n):
                        ks = 0 if qt == 0 else 1 + s
                        m = pe.matmul(ps[:, 2 + qt % 2, h * HD:(h + 1) * HD], prob_t[:, hh, s * P:(s + 1) * P],
                                      v_tok[:, ks, h * HD:(h + 1) * HD], start=(s == 0), stop=(s == n - 1))
                m.then_inc(o_made.sem, 1)
            pe.wait_ge(o_taken.sem, o_taken.at(L, 2 * CHUNKS * (half + 1)))

        def fourier(pe, L):
            pe.wait_ge(f_ready.sem, f_ready.at(L, DB))
            pe.wait_ge(dft_in.sem, dft_in.at(L, 16))
            for i in range(CHUNKS * GROUPS):
                c, g = i // GROUPS, i % GROUPS
                if i >= 4:
                    pe.wait_ge(ch_taken.sem, ch_taken.at(L, i - 3))
                for kk in range(2):
                    m = pe.matmul(ps[:, 4 + i % 4, :], wide[:, 2 * g + kk, c * P:(c + 1) * P], dft_ch[:, kk, :],
                                  start=(kk == 0), stop=(kk == 1))
                m.then_inc(ch_made.sem, 1)
            pe.wait_ge(ch_taken.sem, ch_taken.at(L, CHUNKS * GROUPS))
            for b in range(DB):
                g, w = b // 2, (b % 2) * P
                if b >= 4:
                    pe.wait_ge(y_lo_made.sem, y_lo_made.at(L, 2 * DB + b - 3))
                for s in range(2):
                    pe.matmul(ps[:, 4 + b % 4, 0:CTX], f_ch[:, 0, g, s * 256 + w:s * 256 + w + P], dft_ctx[:, s, :],
                              start=(s == 0), stop=(s == 1))
                for i in range(4):
                    c, s = i // 2, i % 2
                    m = pe.matmul(ps[:, 4 + b % 4, CTX:T], f_ch[:, 1 + c, g, s * 256 + w:s * 256 + w + P],
                                  dft_lat[:, c, s, :], start=(i == 0), stop=(i == 3))
                m.then_inc(pos_made.sem, 1)

        SSD_STEPS = [(0, 0, "state"), (1, 0, "state"),
                     (0, 1, "off"), (0, 1, "state"), (0, 2, "off"),
                     (1, 2, "off"), (1, 2, "state"), (1, 1, "off")]

        def up_stage(eng, half, body):
            t, count = STAGES[f"up{half}"]
            first, end = t, t + count
            def one(t, turn, j, k, par, i):
                body(t, turn, j, k, par == 0, i)
            while t % RING and t < end:
                one(t, t // RING, t % RING, t - first, (t - first) % 2, (t - first) // 2)
                t += 1
            turns = (end - t) // RING
            with eng.Fori(0, turns) as r:
                for j in range(RING):
                    k0 = t + j - first
                    one(r * RING + (t + j), r + t // RING, j, r * RING + k0, k0 % 2, r * (RING // 2) + k0 // 2)
            t += turns * RING
            while t < end:
                one(t, t // RING, t % RING, t - first, (t - first) % 2, (t - first) // 2)
                t += 1

        def sub_stage(eng, first, count, body):
            t, end = first, first + count
            while t % RING and t < end:
                body(t, t // RING, t % RING, t - first)
                t += 1
            turns = (end - t) // RING
            if turns:
                with eng.Fori(0, turns) as r:
                    for j in range(RING):
                        body(r * RING + (t + j), r + t // RING, j, r * RING + (t + j - first))
                t += turns * RING
            while t < end:
                body(t, t // RING, t % RING, t - first)
                t += 1

        def lagged(eng, first, count, body):
            for t in range(first, first + RING):
                body(t, t // RING, t % RING, t - first)
            sub_stage(eng, first + RING, count - RING, lambda t, turn, j, k: body(t, turn, j, k + RING))

        def param_at(name, k, step, i):
            at = PARAMS[name][0]
            start = k * step + (at + i)
            return params[:, bass.ds(start, 1)]

        def gates(L, act, refill, stage, branch):
            def body(t, turn, j, k, i, is_gate):
                refill(L, t, turn, j)
                if is_gate:
                    act.wait_ge(taken.sem, taken.at(L, t + AHEAD))
                    act.activation(gate[:, :], ps[:, 2 * (j % 2), 0:T], ACT.Sigmoid,
                                   bias=param_at("b_gate", i + branch * DB, 1, 0)).then_inc(gate_made.sem, 1)
            pairs(act, stage, body)

        def pairs(eng, stage, body):
            t, count = STAGES[stage]
            first, end = t, t + count
            while t % RING and t < end:
                body(t, t // RING, t % RING, t - first, (t - first) // 2, (t - first) % 2 == 0)
                t += 1
            turns = (end - t) // RING
            with eng.Fori(0, turns) as r:
                for j in range(RING):
                    k0 = t + j - first
                    body(r * RING + (t + j), r + t // RING, j, r * RING + k0, r * (RING // 2) + k0 // 2, k0 % 2 == 0)
            t += turns * RING
            while t < end:
                body(t, t // RING, t % RING, t - first, (t - first) // 2, (t - first) % 2 == 0)
                t += 1

        def ssd_act(L, act, link):
            act.wait_ge(kvq_lo_made.sem, kvq_lo_made.at(L, 5))
            for c in range(CHUNKS):
                at = (0, 3, 0)[c] * 512
                act.wait_ge(transposed.sem, transposed.at(L, c + 1))
                act.activation(xs_tok[:, c, :], flat[:, at:at + 1024], ACT.Copy)
                act.activation(b_tok[:, c, :], flat[:, at + 1024:at + 1280], ACT.Copy)
                act.activation(dts[:, 0, c * 32:(c + 1) * 32], flat[:, at + 1280:at + 1312], ACT.Copy)\
                   .then_inc(tok_ready.sem, 1)
            act.wait_ge(dt_abs.sem, dt_abs.at(L, 1))
            act.activation(dts[:, 3, :], dts[:, 2, :], ACT.Exp, scale=-1.0)
            act.activation(dts[:, 4, 0:32], param("a_log", 0, 32), ACT.Exp).then_inc(dt_exp.sem, 1)
            act.wait_ge(to_end.sem, to_end.at(L, 1))
            act.activation(dts[:, 8, :], dts[:, 6, :], ACT.Exp)
            act.activation(dts[:, 9, :], dts[:, 7, :], ACT.Exp)
            act.activation(dts[:, 10, :], ps[:, 3, 96:192], ACT.Exp).then_inc(dt_exp.sem, 1)
            for i in range(2 * CHUNKS):
                act.wait_ge(segs_ready.sem, segs_ready.at(L, i + 1))
                act.activation(decay[:, :, :], decay[:, :, :], ACT.Exp).then_inc(decay_ready.sem, 1)

        def attention_act(L, act, refill, half):
            t0 = STAGES[f"heads{half}"][0]
            for i in range(4):
                t = t0 + i
                refill(L, t, t // RING, t % RING)
                act.activation(q_t[0:64, 2 * i:2 * i + 2, :], ps[0:64, 2 * (t % 2):2 * (t % 2) + 2, 0:T], ACT.Copy)\
                   .then_inc(q_plain.sem, 1)
            for i in range(2):
                t = t0 + 4 + i
                refill(L, t, t // RING, t % RING)
                act.activation(k_t[0:64, 4 * i:4 * i + 4:2, :], ps[0:64, 2 * (t % 2):2 * (t % 2) + 2, :], ACT.Copy)\
                   .then_inc(k_even.sem, 1)
            for i in range(2):
                t = t0 + 6 + i
                refill(L, t, t // RING, t % RING)
                b = 2 * (t % 2)
                act.activation(v_tok[:, :, i * 256:(i + 1) * 256],
                               flat[:, b * 512:b * 512 + 1024].rearrange("p (s n) -> p s n", s=4), ACT.Copy)\
                   .then_inc(v_ready.sem, 1)
            n = CHUNKS * HALF // 2
            for i in range(n):
                qt, hp = i // 4, i % 4
                width = CTX if qt == 0 else KEYS - CTX
                act.wait_ge(maxed.sem, maxed.at(L, 2 * (half * n + i + 1)))
                if half * n + i >= 2:
                    act.wait_ge(p_turned.sem, p_turned.at(L, 2 * (half * n + i - 1)))
                for hh in range(2):
                    m = act.activation(prob[:, i % 2, hh, 0:width], ps[:, 4 + 2 * (i % 2) + hh, 0:width], ACT.Exp,
                                       bias=stat[:, 2 * (i % 4) + hh:2 * (i % 4) + hh + 1], scale=ATTN_SCALE,
                                       accum_out=stat[:, 16 + (qt % 2) * 8 + 2 * hp + hh:17 + (qt % 2) * 8 + 2 * hp + hh])
                m.then_inc(exped.sem, 1)

        def y_los(L, n, value):
            dve = nc.vector
            for k in range(DB):
                dve.wait_ge(y_hi_made.sem, y_hi_made.at(L, n * DB + k + 1))
                dve.tensor_tensor(y_lo[:, k, :], value(k), y_hi[:, k, :].bitcast(F32), ALU.subtract)\
                   .then_inc(y_lo_made.sem, 1)

        def merge(L, stage, branch):
            dve = nc.vector

            def body(t, turn, j, k, i, is_gate):
                dve.wait_ge(hi_made.sem, hi_made.at(L, t + AHEAD + 1))
                dve.tensor_tensor(w_lo[:, j % AHEAD, :], raw[:, (j + AHEAD) % RING, :],
                                  w_hi[:, j % AHEAD, :].bitcast(F32), ALU.subtract).then_inc(lo_made.sem, 1)
                if is_gate:
                    dve.wait_ge(gate_made.sem, gate_made.at(L, i + branch * DB + 1))
                    after(dve).then_inc(taken.sem, 1)
                    return
                dve.wait_ge(used.sem, used.at(L, t + 1))
                bank = ps[:, 2 * (j % 2), 0:T]
                if branch == 0:
                    dve.tensor_tensor(mix[:, i, :], gate[:, :], bank, ALU.mult).then_inc(taken.sem, 1)
                else:
                    dve.wait_ge(mixed.sem, mixed.at(L, i + (1 + (branch - 1) * DB)))
                    dve.tensor_tensor(gated[:, :], gate[:, :], bank, ALU.mult).then_inc(taken.sem, 1)
                    dve.wait_ge(taken.sem, taken.at(L, t + 1 + AHEAD))
                    dve.tensor_tensor(mix[:, i, :], mix[:, i, :], gated[:, :], ALU.add).then_inc(mixed.sem, 1)
            pairs(dve, stage, body)
            if branch == 0:
                after(dve).then_inc(mixed.sem, 1)

        def ssd_dve(L, dve, link):
            n = CHUNKS * 32
            dt, dta, mag, e, ea_log, s2, acum, end = (dts[:, i, :] for i in (0, 1, 2, 3, 4, 5, 6, 7))
            exp_a, exp_end, exp_all, poly = (dts[:, i, :] for i in (8, 9, 10, 11))

            def per_head(ap):
                return ap.rearrange("p (c n) -> p c n", c=CHUNKS)
            dve.wait_ge(tok_ready.sem, tok_ready.at(L, CHUNKS))
            link(L, dve.tensor_tensor(per_head(dt), per_head(dt), repeat(param("dt_bias", 0, 32), CHUNKS), ALU.add))
            link(L, dve.tensor_scalar(mag, dt, -1.0, None, ALU.mult))
            dve.tensor_tensor(mag, mag, dt, ALU.max).then_inc(dt_abs.sem, 1)
            dve.wait_ge(dt_exp.sem, dt_exp.at(L, 1))
            link(L, dve.tensor_scalar(s2, e, 2.0, None, ALU.add))
            link(L, dve.reciprocal(s2, s2))
            link(L, dve.tensor_tensor(e, e, s2, ALU.mult))
            link(L, dve.tensor_tensor(s2, e, e, ALU.mult))
            link(L, dve.tensor_scalar(poly, s2, 1.0 / 17, None, ALU.mult))
            for q in (15, 13, 11, 9, 7, 5, 3):
                link(L, dve.scalar_tensor_tensor(out=poly, in0=poly, scalar=1.0 / q, in1=s2, op0=ALU.add, op1=ALU.mult))
            link(L, dve.scalar_tensor_tensor(out=poly, in0=poly, scalar=1.0, in1=e, op0=ALU.add, op1=ALU.mult))
            link(L, dve.tensor_scalar(dt, dt, 0.0, None, ALU.max))
            link(L, dve.scalar_tensor_tensor(out=dt, in0=poly, scalar=2.0, in1=dt, op0=ALU.mult, op1=ALU.add))
            dve.scalar_tensor_tensor(out=per_head(dta), in0=per_head(dt), scalar=-1.0,
                                     in1=repeat(ea_log[:, 0:32], CHUNKS), op0=ALU.mult, op1=ALU.mult)\
               .then_inc(dt_ready.sem, 1)
            dve.wait_ge(cb_made.sem, cb_made.at(L, 1))
            for d in range(2):
                m = dve.tensor_tensor(cbm[:, d, :, :], flat[:, 6 * 512:6 * 512 + 768].rearrange("p (i n) -> p i n", n=P),
                                      repeat(tri[d], 2 * CHUNKS), ALU.mult)
            link(L, m)
            dve.wait_ge(acum_sums.sem, acum_sums.at(L, 1))
            for d in range(2):
                m = dve.tensor_copy(acum.rearrange("p (c d h) -> p c d h", c=CHUNKS, d=2)[:, :, d, :],
                                    ps[:, 3, d * 48:(d + 1) * 48].rearrange("p (c h) -> p c h", c=CHUNKS))
            m.then_inc(exps_ready.sem, 1)
            dve.wait_ge(exps_ready.sem, exps_ready.at(L, 1))
            dve.tensor_tensor(end, ps[:, 3, 96:192], acum, ALU.subtract).then_inc(to_end.sem, 1)

            def heads(v):
                return v.rearrange("p (h n) -> p h n", n=HD)

            for i in range(2 * CHUNKS):
                c, g = i // 2, i % 2
                if g == 0:
                    if c:
                        dve.wait_ge(y_diag.sem, y_diag.at(L, 2 * c))
                        dve.tensor_copy(y_tok[:, c - 1, :], flat[:, 0:1024]).then_inc(y_taken.sem, 1)
                    for d in range(2):
                        m = dve.tensor_tensor(heads(xdt[:, d, :]), heads(xs_tok[:, c, :]),
                                              spread(dts[:, 0, c * 32 + d * 16:c * 32 + d * 16 + 16], HD), ALU.mult)
                    m.then_inc(xdt_ready.sem, 1)
                dve.wait_ge(rows_made.sem, rows_made.at(L, i + 1))
                if i:
                    dve.wait_ge(y_diag.sem, y_diag.at(L, i))
                for d in range(2):
                    for h in range(HALF):
                        at = c * 32 + d * 16 + g * HALF + h
                        r = d * HALF + h
                        m = dve.tensor_scalar(decay[:, r, :], flat[:, 4 * 512 + r * P:4 * 512 + (r + 1) * P],
                                              acum[:, at:at + 1], 0.0, ALU.subtract, ALU.min)
                m.then_inc(segs_ready.sem, 1)
                dve.wait_ge(decay_ready.sem, decay_ready.at(L, i + 1))
                for d in range(2):
                    m = dve.tensor_tensor(decay[:, d * HALF:(d + 1) * HALF, :], decay[:, d * HALF:(d + 1) * HALF, :],
                                          repeat(cbm[:, d, 2 * c + g, :], HALF), ALU.mult)
                m.then_inc(masked.sem, 1)
            dve.wait_ge(y_diag.sem, y_diag.at(L, 2 * CHUNKS))
            dve.tensor_copy(y_tok[:, CHUNKS - 1, :], flat[:, 0:1024]).then_inc(y_taken.sem, 1)
            dve.wait_ge(dt_exp.sem, dt_exp.at(L, 2))
            n_state = n_off = 0
            for d, c, what in SSD_STEPS:
                cols = slice(c * 32 + d * 16, c * 32 + d * 16 + 16)
                if what == "state":
                    link(L, dve.tensor_tensor(poly[:, 0:16], dts[:, 0, cols], exp_end[:, cols], ALU.mult))
                    dve.tensor_tensor(heads(x_end), heads(xs_tok[:, c, :]), spread(poly[:, 0:16], HD), ALU.mult)\
                       .then_inc(ends_ready.sem, 1)
                    n_state += 1
                    dve.wait_ge(states_made.sem, states_made.at(L, n_state))
                    if c == 0:
                        dve.tensor_copy(h_state[:, d, :], flat[:, 1024:2048]).then_inc(new_state.sem, 1)
                        after(dve).then_inc(states_taken.sem, 1)
                    else:
                        link(L, dve.tensor_tensor(heads(h_state[:, d, :]), heads(h_state[:, d, :]),
                                                  spread(exp_all[:, c * 32 + d * 16:c * 32 + d * 16 + 16], HD), ALU.mult))
                        link(L, dve.tensor_tensor(h_state[:, d, :], h_state[:, d, :], flat[:, 1024:2048], ALU.add))
                        after(dve).then_inc(off_ready.sem, 1)
                else:
                    if n_off == 0 or n_off == 2:
                        dve.wait_ge(state_in.sem, state_in.at(L, 16))
                        after(dve).then_inc(off_ready.sem, 1)
                    n_off += 1
                    dve.wait_ge(off_made.sem, off_made.at(L, n_off))
                    link(L, dve.tensor_tensor(heads(scaled), heads(flat[:, 2048:3072]), spread(exp_a[:, cols], HD), ALU.mult))
                    dve.tensor_tensor(y_tok[:, c, :], y_tok[:, c, :], scaled, ALU.add).then_inc(off_taken.sem, 1)
                    dve.wait_ge(off_taken.sem, off_taken.at(L, n_off))
            for b in range(DB):
                dve.wait_ge(y_turned.sem, y_turned.at(L, b + 1))
                dve.scalar_tensor_tensor(out=mix[:, b, :], in0=xbc[:, b, :], scalar=param("d_skip", b),
                                         in1=ps[:, 4 + b % 4, 0:T], op0=ALU.mult, op1=ALU.add).then_inc(y_back.sem, 1)

        def attention_dve(L, dve, link, split, tick_taken, half):
            t0 = STAGES[f"heads{half}"][0]
            for i in range(4):
                t = t0 + i
                split(L, t, t // RING, t % RING)
                dve.wait_ge(q_plain.sem, q_plain.at(L, 4 * half + i + 1))
                b = 2 * (t % 2)
                n = 3 * (4 * half + i)
                if n:
                    dve.wait_ge(q_rot.sem, q_rot.at(L, n))
                dve.tensor_tensor(rot[64:96, :, :], ps[96:128, b:b + 2, 0:T], repeat(rope[96:128, :], 2), ALU.mult)\
                   .then_inc(q_rot.sem, 1)
                dve.tensor_tensor(q_t[64:96, 2 * i:2 * i + 2, :], ps[64:96, b:b + 2, 0:T], repeat(rope[64:96, :], 2),
                                  ALU.mult).then_inc(q_rot.sem, 1)
                dve.wait_ge(q_rot.sem, q_rot.at(L, n + 2))
                tick_taken()
                dve.tensor_tensor(q_t[64:96, 2 * i:2 * i + 2, :], q_t[64:96, 2 * i:2 * i + 2, :], rot[64:96, :, :],
                                  ALU.add).then_inc(q_rot.sem, 1)
            for i in range(2):
                t = t0 + 4 + i
                split(L, t, t // RING, t % RING)
                dve.wait_ge(k_even.sem, k_even.at(L, 2 * half + i + 1))
                b = 2 * (t % 2)
                dve.tensor_copy(k_t[0:64, 4 * i + 1:4 * i + 4:2, :], ps[64:128, b:b + 2, :]).then_inc(taken.sem, 1)
            for i in range(2):
                t = t0 + 6 + i
                split(L, t, t // RING, t % RING)
                dve.wait_ge(v_ready.sem, v_ready.at(L, 2 * half + i + 1))
                tick_taken()
            n = CHUNKS * HALF // 2

            def maxima(i):
                qt = i // 4
                width = CTX if qt == 0 else KEYS - CTX
                m0 = half * n + i
                at = 2 * (i % 4)
                dve.wait_ge(scored.sem, scored.at(L, m0 + 1))
                if m0 >= 4:
                    dve.wait_ge(exped.sem, exped.at(L, m0 - 3))
                b = 4 + 2 * (i % 2)
                dve.tensor_reduce(stat[:, at:at + 2], ps[:, b:b + 2, 0:width], AX.X, ALU.max).then_inc(maxed.sem, 1)
                dve.wait_ge(maxed.sem, maxed.at(L, 2 * m0 + 1))
                dve.tensor_scalar(stat[:, at:at + 2], stat[:, at:at + 2], -ATTN_SCALE, None, ALU.mult)\
                   .then_inc(maxed.sem, 1)

            maxima(0)
            for i in range(n):
                qt, hp = i // 4, i % 4
                width = CTX if qt == 0 else KEYS - CTX
                if i + 1 < n:
                    maxima(i + 1)
                m0 = half * n + i
                for hh in range(2):
                    dve.wait_ge(p_turned.sem, p_turned.at(L, 2 * m0 + hh + 1))
                    if m0:
                        dve.wait_ge(o_made.sem, o_made.at(L, m0))
                    dve.tensor_copy(prob_t[:, hh, 0:width], ps[:, hh, 0:width]).then_inc(p_back.sem, 1)
                if hp == 3:
                    dve.wait_ge(exped.sem, exped.at(L, m0 + 1))
                    sums_ = stat[:, 16 + (qt % 2) * 8:24 + (qt % 2) * 8]
                    dve.reciprocal(stat[:, 32:40], sums_).then_inc(o_taken.sem, 1)
                    done = 2 * CHUNKS * half + 2 * qt
                    dve.wait_ge(o_taken.sem, o_taken.at(L, done + 1))
                    dve.wait_ge(o_made.sem, o_made.at(L, m0 + 1))
                    dve.tensor_tensor(o_tok[:, qt, half * 512:(half + 1) * 512].rearrange("p (h n) -> p h n", n=HD),
                                      ps[:, 2 + qt % 2, :].rearrange("p (h n) -> p h n", n=HD),
                                      spread(stat[:, 32:40], HD), ALU.mult).then_inc(o_taken.sem, 1)

        block = ctx.enter_context(nc.Block())


        @block.sync
        def _(sp):
            total = LAYERS * TILES
            for t in range(RING):
                sp.dma_start(raw[:, t, :], a_weights[t]).then_inc(arrived[t].sem, 16)
            with sp.Fori(0, total // RING - 1) as r:
                for j in range(RING):
                    sp.wait_ge(lo_made.sem, r * RING + (j + 1))
                    sp.dma_start(raw[:, j, :], a_weights[r * RING + (RING + j)]).then_inc(arrived[j].sem, 16)
            for j in range(AHEAD):
                sp.wait_ge(lo_made.sem, total - RING + j + 1)
                sp.dma_start(raw[:, j, :], a_weights[j]).then_inc(arrived[j].sem, 16)

        @block.gpsimd
        def _(pool):
            pool.dma_start(consts[:, :], a_consts[:, 0:N_KEPT]).then_inc(loaded, 16)
            pool.dma_start(x[:, :, :], a_x).then_inc(loaded, 16)
            pool.dma_start(cond[:, :, :], a_cond).then_inc(loaded, 16)
            with pool.Fori(0, LAYERS) as L:
                pool.wait_ge(caches_free.sem, caches_free.at(L, 1))
                settle(pool, pool_marks)
                pool.dma_start(params[:, :], a_params[L]).then_inc(params_in.sem, 16)
                pool.dma_start(ckv[:, :, T:KEYS], a_ckv[L]).then_inc(cache_in.sem, 16)
                pool.dma_start(kpe[64:96, T:KEYS], a_kpe[L]).then_inc(cache_in.sem, 16)
                pool.wait_ge(misc_copied.sem, misc_copied.at(L, 1))
                settle(pool, pool_marks)
                pool.dma_start(o_kpe[L], kpe_raw[64:96, :]).then_inc(stored, 16)
                pool.wait_ge(ckv_ready.sem, ckv_ready.at(L, 1))
                settle(pool, pool_marks)
                pool.dma_start(o_ckv[L], ckv[:, :, 0:CTX]).then_inc(stored, 16)
                for d in range(2):
                    pool.wait_ge(new_state.sem, new_state.at(L, d + 1))
                    settle(pool, pool_marks)
                    pool.dma_start(o_state[L, d], h_state[:, d, :]).then_inc(state_out.sem, 16)
                pool.wait_ge(state_out.sem, state_out.at(L, 32))
                settle(pool, pool_marks)
                pool.dma_start(h_state[:, :, :], a_state[L]).then_inc(state_in.sem, 16)
                pool.wait_ge(y_back.sem, y_back.at(L, DB))
                pool.wait_ge(kpe_ready.sem, kpe_ready.at(L, 3))
                pool.wait_ge(cache_in.sem, cache_in.at(L, 32))
                settle(pool, pool_marks)
                pool.tensor_copy(k_t[64:96, :, :], repeat(kpe[64:96, :], HALF)).then_inc(kpe_spread.sem, 1)
                pool.wait_ge(o_taken.sem, o_taken.at(L, 4 * CHUNKS))
                settle(pool, pool_marks)
                pool.dma_start(dft, a_consts[:, N_KEPT:]).then_inc(dft_in.sem, 16)
            pool.wait_ge(x_ready.sem, LAYERS * x_ready.per_layer)
            pool.dma_start(o_x, x[:, :, :]).then_inc(stored, 16)
            pool.wait_ge(stored, 16 * (2 * LAYERS + 1))
            pool.wait_ge(state_out.sem, LAYERS * 32)
            for j in range(AHEAD):
                pool.wait_ge(arrived[j].sem, 16 * (LAYERS * TURNS + 1))

        @block.tensor
        def _(pe):
            def product(out, blocks, first=True, last=True):
                for i, (ah, al, bh, bl) in enumerate(blocks):
                    start, stop = first and i == 0, last and i == len(blocks) - 1
                    pe.matmul(out, ah, bh, start=start, stop=False)
                    pe.matmul(out, ah, bl, start=False, stop=False)
                    m = pe.matmul(out, al, bh, start=False, stop=stop)
                return m

            def weights(j, k, n=P, at=None):
                lo = k * P if at is None else at
                return w_hi[:, j % AHEAD, lo:lo + n], w_lo[:, j % AHEAD, lo:lo + n]

            def tile_in(L, t):
                pe.wait_ge(lo_made.sem, lo_made.at(L, t + 1))
                pe.wait_ge(taken.sem, taken.at(L, t + 1))

            def bank(j):
                return 2 * (j % AHEAD)

            def project(L, stage, hi, lo, n=T):
                def body(t, turn, j, k):
                    tile_in(L, t)
                    product(ps[:, bank(j), 0:n], [(*weights(j, kk), hi[:, kk, 0:n], lo[:, kk, 0:n])
                                                  for kk in range(DB)]).then_inc(used.sem, 1)
                through(pe, stage, body)

            def norm_sum(L, n, blocks, sq):
                pe.wait_ge(squares.sem, squares.at(L, n))
                for kk in range(blocks):
                    m = pe.matmul(ps[:, 7, 0:T], ones, sq[:, kk, :], start=(kk == 0), stop=(kk == blocks - 1))
                m.then_inc(sums.sem, 1)

            def out_project(L, stage):
                def body(t, turn, j, k):
                    tile_in(L, t)
                    hi, lo = (h_hi, h_lo) if j % 2 == 0 else (y_hi, y_lo)
                    product(ps[:, bank(j), 0:T], [(*weights(j, kk), hi[:, kk, :], lo[:, kk, :])
                                                  for kk in range(DB)]).then_inc(used.sem, 1)
                assert STAGES[stage][0] % 2 == 0
                through(pe, stage, body)

            pe.wait_ge(loaded, 48)
            pe.wait_ge(c_split, 3)
            with pe.Fori(0, LAYERS) as L:
                norm_sum(L, 1, DB, wide)

                def ada(t, turn, j, k):
                    tile_in(L, t)
                    for kk in range(DB):
                        hi, lo = weights(j, kk)
                        pe.matmul(ps[0:4, bank(j), 0:P], c_parts[:, kk, :], hi, start=(kk == 0), stop=False)
                        m = pe.matmul(ps[0:4, bank(j), 0:P], c_parts[:, kk, :], lo, start=False, stop=(kk == DB - 1))
                    m.then_inc(used.sem, 1)
                through(pe, "ada", ada)
                pe.wait_ge(taken.sem, taken.at(L, STAGES["ada"][1] + AHEAD))
                for k in range(48):
                    m = pe.matmul(ps[:, 4, 2 * k:2 * k + 2], mod_rows[:, k * P:(k + 1) * P], fold[:, :],
                                  start=True, stop=True)
                m.then_inc(mod_made.sem, 1)
                pe.wait_ge(h_lo_made.sem, h_lo_made.at(L, DB))
                settle(pe, pe_marks)
                project(L, "proj", h_hi, h_lo)
                norm_sum(L, 2, KVB, wide)
                norm_sum(L, 3, QB, wide)
                ssd(pe, L)
                project(L, "z", h_hi, h_lo)
                norm_sum(L, 4, DB, wide)
                pe.wait_ge(y_lo_made.sem, y_lo_made.at(L, DB))
                out_project(L, "out_ssd")
                attention(pe, L, 0, product, weights, tile_in)
                attention(pe, L, 1, product, weights, tile_in)
                pe.wait_ge(o_taken.sem, o_taken.at(L, 4 * CHUNKS))
                for b in range(DB):
                    if b >= 4:
                        pe.wait_ge(y_lo_made.sem, y_lo_made.at(L, DB + b - 3))
                    for c in range(CHUNKS):
                        m = pe.transpose(ps[:, 4 + b % 4, c * P:(c + 1) * P], o_tok[:, c, b * P:(b + 1) * P], ident)
                    m.then_inc(o_turned.sem, 1)
                pe.wait_ge(y_lo_made.sem, y_lo_made.at(L, 2 * DB))
                out_project(L, "out_mla")
                project(L, "f", h_hi, h_lo)
                fourier(pe, L)
                pe.wait_ge(y_lo_made.sem, y_lo_made.at(L, 3 * DB))
                out_project(L, "out_fft")
                pe.wait_ge(y_lo_made.sem, y_lo_made.at(L, 4 * DB))
                project(L, "w_o", y_hi, y_lo)
                norm_sum(L, 5, DB, mix)
                norm_sum(L, 6, DB, mix)
                pe.wait_ge(h_lo_made.sem, h_lo_made.at(L, 2 * DB))
                for half in range(2):
                    if half:
                        pe.wait_ge(down_taken.sem, down_taken.at(L, 1))
                    project(L, f"up{half}", h_hi, h_lo)
                    pe.wait_ge(taken.sem, taken.at(L, STAGES[f"down{half}"][0] + AHEAD))

                    def down(t, turn, j, k, half=half):
                        pe.wait_ge(lo_made.sem, lo_made.at(L, t + 1))
                        pe.wait_ge(y_lo_made.sem, y_lo_made.at(L, 4 * DB + half * FF_H + 1 + k))
                        for b in range(DB):
                            wh, wl = weights(j, b)
                            m = product(ps[:, b, 0:T], [(wh, wl, y_hi[:, k, :], y_lo[:, k, :])],
                                        first=(k == 0), last=(k == FF_H - 1))
                        m.then_inc(used.sem, 1)
                    t0 = STAGES[f"down{half}"][0]
                    for k in range(FF_H):
                        down(t0 + k, (t0 + k) // RING, (t0 + k) % RING, k)
                    m = pe.matmul(ps[0:1, 7, 510:511], ones[:, 0:1], ones[:, 0:1], start=True, stop=True)
                    m.then_inc(down_made.sem, 1)
                pe.wait_ge(down_taken.sem, down_taken.at(L, 2))
                norm_sum(L, 7, DB, mix)

        @block.scalar
        def _(act):
            steps = [0]

            def link(L, ins):
                steps[0] += 1
                ins.then_inc(act_chain.sem, 1)
                act.wait_ge(act_chain.sem, act_chain.at(L, steps[0]))

            def refill(L, t, turn, j):
                act.wait_ge(used.sem, used.at(L, t + 1))
                nxt = (j + AHEAD) % RING
                act.wait_ge(arrived[nxt].sem, arrived[nxt].at(L, 16 * (turn + (j + AHEAD) // RING + 1)))
                act.activation(w_hi[:, j % AHEAD, :], raw[:, nxt, :], ACT.Copy).then_inc(hi_made.sem, 1)

            def idle(L, stage):
                through(act, stage, lambda t, turn, j, k: refill(L, t, turn, j))

            def norm(L, n, src, width, sq):
                act.activation(sq, src, ACT.Square).then_inc(squares.sem, 1)
                act.wait_ge(sums.sem, sums.at(L, n))
                act.activation(root[:, :], ps[:, 7, 0:T], ACT.Sqrt, scale=1.0 / width, bias=eps[:, 0:1]).then_inc(roots.sem, 1)

            eps = stat[:, 63:64]
            act.wait_ge(loaded, 48)
            act.wait_ge(ready, 1)
            act.activation(cond[:, :, :], cond[:, :, :], ACT.Silu).then_inc(c_split, 1)
            act.wait_ge(c_split, 1)
            act.activation(c_parts[:, :, 0:2], cond[:, :, :], ACT.Copy).then_inc(ready, 1)
            for t in range(AHEAD):
                act.wait_ge(arrived[t].sem, 16)
                act.activation(w_hi[:, t, :], raw[:, t, :], ACT.Copy).then_inc(hi_made.sem, 1)
            with act.Fori(0, LAYERS) as L:
                act.wait_ge(params_in.sem, params_in.at(L, 16))
                norm(L, 1, x[:, :, :], D, wide[:, :, :])
                idle(L, "ada")
                for k in range(DB):
                    act.wait_ge(h_value.sem, h_value.at(L, k + 1))
                    act.activation(h_hi[:, k, :], wide[:, k, :], ACT.Copy).then_inc(h_hi_made.sem, 1)

                def centre(L, j, w_name, b_name, k):
                    act.activation(conv[:, j % 2, :], ps[:, 2 * (j % 2), 0:T], ACT.Identity,
                                   scale=param_at(w_name, k, 3, 1), bias=param_at(b_name, k, 1, 0))\
                       .then_inc(conv_mid.sem, 1)

                def xbc_silu(j, k):
                    act.wait_ge(conv_done.sem, conv_done.at(L, k + 1))
                    act.activation(xbc[:, k, :], conv[:, j % 2, :], ACT.Silu).then_inc(silu_done.sem, 1)

                def proj(t, turn, j, k):
                    refill(L, t, turn, j)
                    if not (isinstance(k, int) and k < 2):
                        act.wait_ge(silu_done.sem, silu_done.at(L, k - 1))
                    centre(L, j, "conv_w", "conv_b", k)
                    if not (isinstance(k, int) and k == 0):
                        xbc_silu(j + 1, k - 1)
                t0 = STAGES["proj"][0]
                lagged(act, t0, XBC_B, proj)
                for k in range(XBC_B, 18):
                    t = t0 + k
                    refill(L, t, t // RING, t % RING)
                    if k == XBC_B:
                        xbc_silu(k - 1, k - 1)
                        bank = ps[:, 2 * (t % 2), :]
                        act.activation(dt_t[:, :], bank[0:32, 0:T], ACT.Copy)
                        act.activation(kpe_raw[64:96, :], bank[64:96, 0:CTX], ACT.Copy).then_inc(misc_copied.sem, 1)
                act.wait_ge(taken.sem, taken.at(L, t0 + 18 + AHEAD))
                norm(L, 2, low[:, 0:KVB, :], KVL, wide[:, 0:KVB, :])
                act.wait_ge(kvq_value.sem, kvq_value.at(L, 2))
                act.wait_ge(cache_in.sem, cache_in.at(L, 32))
                for k in range(KVB):
                    act.activation(ckv_hi[:, k, :], ckv[:, k, :], ACT.Copy).then_inc(kvq_hi_made.sem, 1)
                norm(L, 3, low[:, KVB:, :], QL, wide[:, 0:QB, :])
                act.wait_ge(kvq_value.sem, kvq_value.at(L, 5))
                for k in range(QB):
                    act.activation(q_hi[:, k, :], low[:, KVB + k, :], ACT.Copy).then_inc(kvq_hi_made.sem, 1)
                ssd_act(L, act, link)

                def z_tile(t, turn, j, k):
                    refill(L, t, turn, j)
                    act.activation(conv[:, j % 2, :], ps[:, 2 * (j % 2), 0:T], ACT.Silu).then_inc(silu_done.sem, 1)
                through(act, "z", z_tile)
                act.wait_ge(y_value.sem, y_value.at(L, DB))
                norm(L, 4, mix[:, :, :], D, wide[:, :, :])
                act.wait_ge(y_value.sem, y_value.at(L, 2 * DB))
                for k in range(DB):
                    act.activation(y_hi[:, k, :], mix[:, k, :], ACT.Copy).then_inc(y_hi_made.sem, 1)
                gates(L, act, refill, "out_ssd", 0)

                attention_act(L, act, refill, 0)
                attention_act(L, act, refill, 1)
                for b in range(DB):
                    act.wait_ge(o_turned.sem, o_turned.at(L, b + 1))
                    act.activation(y_hi[:, b, :], ps[:, 4 + b % 4, 0:T], ACT.Copy).then_inc(y_hi_made.sem, 1)
                gates(L, act, refill, "out_mla", 1)

                def f_tile(t, turn, j, k):
                    refill(L, t, turn, j)
                    act.activation(wide[:, k, :], ps[:, 2 * (j % 2), 0:T], ACT.Copy).then_inc(f_ready.sem, 1)
                through(act, "f", f_tile)
                for i in range(CHUNKS * GROUPS):
                    act.wait_ge(ch_made.sem, ch_made.at(L, i + 1))
                    act.activation(f_ch[:, i // GROUPS, i % GROUPS, :], ps[:, 4 + i % 4, :], ACT.Copy)\
                       .then_inc(ch_taken.sem, 1)
                for b in range(DB):
                    act.wait_ge(pos_made.sem, pos_made.at(L, b + 1))
                    act.activation(y_hi[:, b, :], ps[:, 4 + b % 4, 0:T], ACT.Copy).then_inc(y_hi_made.sem, 1)
                gates(L, act, refill, "out_fft", 2)
                act.wait_ge(mixed.sem, mixed.at(L, 1 + 2 * DB))
                for k in range(DB):
                    act.activation(y_hi[:, k, :], mix[:, k, :], ACT.Copy).then_inc(y_hi_made.sem, 1)

                def wo_tile(t, turn, j, k):
                    refill(L, t, turn, j)
                    act.activation(wide[:, k, :], ps[:, 2 * (j % 2), 0:T], ACT.Copy).then_inc(wo_ready.sem, 1)
                through(act, "w_o", wo_tile)
                act.wait_ge(wo_ready.sem, wo_ready.at(L, DB))
                act.wait_ge(y_lo_made.sem, y_lo_made.at(L, 4 * DB))
                norm(L, 5, wide[:, :, :], D, mix[:, :, :])
                act.wait_ge(x_mid.sem, x_mid.at(L, 1))
                norm(L, 6, x[:, :, :], D, mix[:, :, :])
                for k in range(DB):
                    act.wait_ge(h_value.sem, h_value.at(L, DB + k + 1))
                    act.activation(h_hi[:, k, :], wide[:, k, :], ACT.Copy).then_inc(h_hi_made.sem, 1)
                for half in range(2):
                    base = half * FF_B

                    def finish(j, k, a, i, half=half, base=base):
                        if a:
                            act.wait_ge(conv_done.sem, conv_done.at(L, k + (XBC_B + base + 1)))
                            act.activation(gate[:, :], conv[:, j % 2, :], ACT.Silu).then_inc(silu_done.sem, 1)
                        else:
                            act.wait_ge(ag_value.sem, ag_value.at(L, i + (half * FF_H + 1)))
                            act.activation(y_hi[:, i, :], gated[:, :], ACT.Copy).then_inc(y_hi_made.sem, 1)

                    def up(t, turn, j, k, a, i, half=half, base=base):
                        refill(L, t, turn, j)
                        first = isinstance(k, int)
                        if a and not (first and k < 2):
                            act.wait_ge(silu_done.sem, silu_done.at(L, i + (XBC_B + DB + half * FF_H)))
                        if not a and not (first and k < 2):
                            act.wait_ge(ag_value.sem, ag_value.at(L, i + half * FF_H))
                        centre(L, j, "ffn_w", "ffn_b", k + base)
                        if not (first and k == 0):
                            finish(j + 1, k - 1, not a, i if not a else i - 1)
                    up_stage(act, half, up)
                    finish(STAGES[f"up{half}"][0] + FF_B - 1, FF_B - 1, False, FF_H - 1)
                    t0 = STAGES[f"down{half}"][0]
                    for k in range(FF_H):
                        refill(L, t0 + k, (t0 + k) // RING, (t0 + k) % RING)
                act.wait_ge(down_taken.sem, down_taken.at(L, 2))
                norm(L, 7, wide[:, :, :], D, mix[:, :, :])
                act.wait_ge(x_ready.sem, x_ready.at(L, 1))
            assert steps[0] == ACT_LINKS, steps

        @block.vector
        def _(dve):
            steps = [0]

            def link(L, ins):
                steps[0] += 1
                ins.then_inc(dve_chain.sem, 1)
                dve.wait_ge(dve_chain.sem, dve_chain.at(L, steps[0]))

            def split(L, t, turn, j):
                dve.wait_ge(hi_made.sem, hi_made.at(L, t + AHEAD + 1))
                dve.tensor_tensor(w_lo[:, j % AHEAD, :], raw[:, (j + AHEAD) % RING, :],
                                  w_hi[:, j % AHEAD, :].bitcast(F32), ALU.subtract).then_inc(lo_made.sem, 1)

            def lo_part(out, value, hi):
                return dve.tensor_tensor(out, value, hi.bitcast(F32), ALU.subtract)

            def tick_taken():
                after(dve).then_inc(taken.sem, 1)

            def norm(L, n):
                dve.wait_ge(roots.sem, roots.at(L, n))
                link(L, dve.reciprocal(rstd[:, :], root[:, :]))

            def modulate(L, which):
                for k in range(DB):
                    for s, (lo, hi) in enumerate(SEGS):
                        m = dve.tensor_scalar(wide[:, k, lo:hi], wide[:, k, lo:hi], coef[:, 3 * which, k, s:s + 1],
                                              coef[:, 3 * which + 1, k, s:s + 1], ALU.mult, ALU.add)
                    m.then_inc(h_value.sem, 1)
                for k in range(DB):
                    dve.wait_ge(h_hi_made.sem, h_hi_made.at(L, which * DB + k + 1))
                    lo_part(h_lo[:, k, :], wide[:, k, :], h_hi[:, k, :]).then_inc(h_lo_made.sem, 1)

            def residual(L, which, signal_):
                link(L, dve.tensor_tensor(wide[:, :, :], wide[:, :, :], repeat(rstd[:, :], DB), ALU.mult))
                for k in range(DB):
                    for s, (lo, hi) in enumerate(SEGS):
                        m = dve.scalar_tensor_tensor(out=x[:, k, lo:hi], in0=wide[:, k, lo:hi],
                                                     scalar=coef[:, 3 * which + 2, k, s:s + 1], in1=x[:, k, lo:hi],
                                                     op0=ALU.mult, op1=ALU.add)
                m.then_inc(signal_.sem, 1)

            def taps(L, n, j, w_name, k, last):
                dve.wait_ge(conv_mid.sem, conv_mid.at(L, n + 1))
                bank, buf = ps[:, 2 * (j % 2), :], conv[:, j % 2, :]
                for lo, hi in SEGS:
                    m = dve.scalar_tensor_tensor(out=buf[:, lo + 1:hi], in0=bank[:, lo:hi - 1],
                                                 scalar=param_at(w_name, k, 3, 0), in1=buf[:, lo + 1:hi],
                                                 op0=ALU.mult, op1=ALU.add)
                m.then_inc(conv_left.sem, 1)
                dve.wait_ge(conv_left.sem, conv_left.at(L, n + 1))
                for lo, hi in SEGS:
                    m = dve.scalar_tensor_tensor(out=buf[:, lo:hi - 1], in0=bank[:, lo + 1:hi],
                                                 scalar=param_at(w_name, k, 3, 2), in1=buf[:, lo:hi - 1],
                                                 op0=ALU.mult, op1=ALU.add)
                m.then_inc(conv_done.sem, 1)
                dve.wait_ge(conv_done.sem, conv_done.at(L, n + 1))
                tick_taken()

            dve.wait_ge(loaded, 48)
            dve.memset(stat[:, 63:64], EPS).then_inc(ready, 1)
            dve.wait_ge(ready, 2)
            lo_part(c_parts[:, :, 2:4], cond[:, :, :], c_parts[:, :, 0:2]).then_inc(c_split, 1)
            dve.tensor_copy(fold[:, :], ident[0:4, 0:2]).then_inc(ready, 1)
            dve.wait_ge(ready, 3)
            dve.tensor_tensor(fold[:, :], fold[:, :], ident[0:4, 2:4], ALU.add).then_inc(c_split, 1)
            for t in range(AHEAD):
                dve.wait_ge(hi_made.sem, t + 1)
                dve.tensor_tensor(w_lo[:, t, :], raw[:, t, :], w_hi[:, t, :].bitcast(F32), ALU.subtract)\
                   .then_inc(lo_made.sem, 1)
            for _ in range(AHEAD):
                tick_taken()
            after(dve).then_inc(caches_free.sem, 1)

            with dve.Fori(0, LAYERS) as L:
                dve.wait_ge(params_in.sem, params_in.at(L, 16))
                settle(dve, dve_marks)

                def ada(t, turn, j, k):
                    split(L, t, turn, j)
                    dve.wait_ge(used.sem, used.at(L, t + 1))
                    dve.tensor_copy(mod_rows[:, bass.ds(k * P, P)], ps[0:4, 2 * (j % 2), 0:P]).then_inc(taken.sem, 1)
                norm(L, 1)
                link(L, dve.tensor_tensor(wide[:, :, :], x[:, :, :], repeat(rstd[:, :], DB), ALU.mult))
                settle(dve, dve_marks)
                through(dve, "ada", ada)
                dve.wait_ge(mod_made.sem, mod_made.at(L, 1))
                link(L, dve.tensor_tensor(mod[:, :, :], ps[:, 4, 0:96].rearrange("p (k s) -> p k s", s=2),
                                          spread(param("b_ada", 0, 48), 2), ALU.add))
                for which, (pre, post) in enumerate((("g_pre_mix", "g_post_mix"), ("g_pre_ffn", "g_post_ffn"))):
                    shift, scale, g = (mod[:, (3 * which + i) * DB:(3 * which + i + 1) * DB, :] for i in range(3))
                    dve.scalar_tensor_tensor(out=coef[:, 3 * which, :, :], in0=scale, scalar=1.0,
                                             in1=spread(param(pre, 0, DB), 2), op0=ALU.add, op1=ALU.mult)
                    dve.tensor_copy(coef[:, 3 * which + 1, :, :], shift)
                    m = dve.tensor_tensor(coef[:, 3 * which + 2, :, :], g, spread(param(post, 0, DB), 2), ALU.mult)
                link(L, m)
                modulate(L, 0)

                def conv_tile(t, turn, j, k):
                    split(L, t, turn, j)
                    taps(L, k, j, "conv_w", k, None)
                t0 = STAGES["proj"][0]
                sub_stage(dve, t0, XBC_B, conv_tile)
                t = t0 + XBC_B
                j = t % RING
                split(L, t, t // RING, j)
                dve.wait_ge(misc_copied.sem, misc_copied.at(L, 1))
                bank = ps[:, 2 * (j % 2), :]
                dve.tensor_tensor(gated[64:96, :], bank[32:64, 0:T], rope[32:64, :], ALU.mult).then_inc(kpe_ready.sem, 1)
                dve.tensor_tensor(kpe[64:96, 0:T], bank[64:96, 0:T], rope[64:96, :], ALU.mult).then_inc(kpe_ready.sem, 1)
                dve.wait_ge(kpe_ready.sem, kpe_ready.at(L, 2))
                tick_taken()
                dve.tensor_tensor(kpe[64:96, 0:T], kpe[64:96, 0:T], gated[64:96, :], ALU.add).then_inc(kpe_ready.sem, 1)
                for k in range(KVB + QB):
                    t = t0 + XBC_B + 1 + k
                    j = t % RING
                    split(L, t, t // RING, j)
                    dve.wait_ge(used.sem, used.at(L, t + 1))
                    dve.tensor_copy(low[:, k, :], ps[:, 2 * (j % 2), 0:T]).then_inc(taken.sem, 1)
                norm(L, 2)
                for k in range(KVB):
                    link(L, dve.scalar_tensor_tensor(out=ckv[:, k, 0:T], in0=low[:, k, :], scalar=param("g_kv", k),
                                             in1=rstd[:, :], op0=ALU.mult, op1=ALU.mult))
                after(dve).then_inc(ckv_ready.sem, 1)
                for k in range(KVB):
                    after(dve).then_inc(kvq_value.sem, 1)
                for k in range(KVB):
                    dve.wait_ge(kvq_hi_made.sem, kvq_hi_made.at(L, k + 1))
                    lo_part(ckv_lo[:, k, :], ckv[:, k, :], ckv_hi[:, k, :]).then_inc(kvq_lo_made.sem, 1)
                norm(L, 3)
                for k in range(QB):
                    dve.scalar_tensor_tensor(out=low[:, KVB + k, :], in0=low[:, KVB + k, :], scalar=param("g_q", k),
                                             in1=rstd[:, :], op0=ALU.mult, op1=ALU.mult).then_inc(kvq_value.sem, 1)
                for k in range(QB):
                    dve.wait_ge(kvq_hi_made.sem, kvq_hi_made.at(L, KVB + k + 1))
                    lo_part(q_lo[:, k, :], low[:, KVB + k, :], q_hi[:, k, :]).then_inc(kvq_lo_made.sem, 1)
                ssd_dve(L, dve, link)

                def z_tile(t, turn, j, k):
                    split(L, t, turn, j)
                    dve.wait_ge(silu_done.sem, silu_done.at(L, XBC_B + k + 1))
                    dve.tensor_tensor(mix[:, k, :], mix[:, k, :], conv[:, j % 2, :], ALU.mult).then_inc(y_value.sem, 1)
                    tick_taken()
                through(dve, "z", z_tile)
                norm(L, 4)
                for k in range(DB):
                    dve.scalar_tensor_tensor(out=mix[:, k, :], in0=mix[:, k, :], scalar=param("g_ssd", k),
                                             in1=rstd[:, :], op0=ALU.mult, op1=ALU.mult).then_inc(y_value.sem, 1)
                y_los(L, 0, lambda k: mix[:, k, :])
                merge(L, "out_ssd", 0)

                attention_dve(L, dve, link, split, tick_taken, 0)
                attention_dve(L, dve, link, split, tick_taken, 1)
                y_los(L, 1, lambda k: ps[:, 4 + k % 4, 0:T])
                merge(L, "out_mla", 1)
                through(dve, "f", lambda t, turn, j, k: (split(L, t, turn, j),
                                                        dve.wait_ge(f_ready.sem, f_ready.at(L, k + 1)),
                                                        tick_taken()))
                y_los(L, 2, lambda k: ps[:, 4 + k % 4, 0:T])
                merge(L, "out_fft", 2)
                y_los(L, 3, lambda k: mix[:, k, :])
                through(dve, "w_o", lambda t, turn, j, k: (split(L, t, turn, j),
                                                          dve.wait_ge(wo_ready.sem, wo_ready.at(L, k + 1)),
                                                          tick_taken()))
                norm(L, 5)
                residual(L, 0, x_mid)
                dve.wait_ge(x_mid.sem, x_mid.at(L, 1))
                norm(L, 6)
                link(L, dve.tensor_tensor(wide[:, :, :], x[:, :, :], repeat(rstd[:, :], DB), ALU.mult))
                modulate(L, 1)

                for half in range(2):
                    def ag_lo(i, half=half):
                        dve.wait_ge(y_hi_made.sem, y_hi_made.at(L, i + (4 * DB + half * FF_H + 1)))
                        lo_part(y_lo[:, i, :], gated[:, :], y_hi[:, i, :]).then_inc(y_lo_made.sem, 1)

                    def up(t, turn, j, k, a, i, half=half):
                        split(L, t, turn, j)
                        taps(L, k + (XBC_B + half * FF_B), j, "ffn_w", k + half * FF_B, None)
                        if a:
                            if not (isinstance(i, int) and i == 0):
                                ag_lo(i - 1)
                        else:
                            if not (isinstance(i, int) and i == 0):
                                dve.wait_ge(y_lo_made.sem, y_lo_made.at(L, i + (4 * DB + half * FF_H)))
                            dve.wait_ge(silu_done.sem, silu_done.at(L, i + (XBC_B + DB + half * FF_H + 1)))
                            dve.tensor_tensor(gated[:, :], gate[:, :], conv[:, j % 2, :], ALU.mult)\
                               .then_inc(ag_value.sem, 1)
                    up_stage(dve, half, up)
                    ag_lo(FF_H - 1)
                    t0 = STAGES[f"down{half}"][0]
                    for k in range(FF_H):
                        split(L, t0 + k, (t0 + k) // RING, (t0 + k) % RING)
                        tick_taken()
                    dve.wait_ge(down_made.sem, down_made.at(L, half + 1))
                    if half == 0:
                        dve.tensor_copy(wide[:, :, :], ps[:, :, 0:T]).then_inc(down_taken.sem, 1)
                        dve.wait_ge(down_taken.sem, down_taken.at(L, 1))
                    else:
                        dve.tensor_tensor(wide[:, :, :], wide[:, :, :], ps[:, :, 0:T], ALU.add)\
                           .then_inc(down_taken.sem, 1)
                norm(L, 7)
                residual(L, 1, x_ready)
                dve.wait_ge(x_ready.sem, x_ready.at(L, 1))
                after(dve).then_inc(caches_free.sem, 1)
            assert steps[0] == DVE_LINKS, steps


def dft(n, scale):
    i = np.arange(n)
    angle = 2 * np.pi * ((i[:, None] * i[None, :]) % n) / n
    return np.cos(angle) * scale, np.sin(angle) * scale


def rope_swap():
    q = ROPE // 4
    i = np.arange(ROPE)
    second = (i // q) % 2 == 1
    return np.where(second, i - q, i + q), np.where(second, 1.0, -1.0)


def constant_tables():
    out = np.zeros((P, N_CONSTS), np.float32)

    def put(name, value):
        at, n = CONSTS[name]
        out[:, at:at + n] = np.asarray(value, np.float64).reshape(P, n)
    i = np.arange(P)
    put("ident", np.eye(P))
    put("tri", np.concatenate([i[:, None] <= i[None, :], i[:, None] >= i[None, :]], 1))
    put("ones", np.ones((P, P)))
    c, s = dft(GROUP_W, GROUP_W ** -0.5)
    put("dft_ch", np.concatenate([c, s], 1).reshape(2, P, 512).transpose(1, 0, 2))
    c, s = dft(LAT, LAT ** -0.5)
    put("dft_lat", np.stack([c, -s], 1).reshape(2, P, 2, LAT).transpose(1, 0, 2, 3))
    c, s = dft(CTX, CTX ** -0.5)
    put("dft_ctx", np.stack([c, -s], 1))
    quarter = ROPE // 4
    inv = (10000.0 ** (-np.arange(quarter, dtype=np.float32) / quarter)).astype(np.float32)
    t = np.arange(LAT)
    pos = np.stack([t // 64, t % 64]).astype(np.float32)
    f = np.arange(ROPE)
    angle = (pos[f // (2 * quarter)] * inv[f % quarter][:, None]).astype(np.float32).astype(np.float64)
    _, sign = rope_swap()
    table = np.zeros((P, T))
    cos = np.concatenate([np.ones((ROPE, CTX)), np.cos(angle)], 1)
    sin = np.concatenate([np.zeros((ROPE, CTX)), np.sin(angle) * sign[:, None]], 1)
    table[32:64], table[64:96], table[96:128] = sin, cos, sin
    put("rope", table)
    return out


def pack_weights(w):
    tiles = np.zeros((LAYERS * TILES, P, 1024), np.float32)
    swap, _ = rope_swap()
    o_xbc, o_dt, o_q, o_kv, o_f = 1024, 1024 + 1536, 1024 + 1536 + 32, 1024 + 1536 + 32 + QL, \
        1024 + 1536 + 32 + QL + KVL + ROPE
    for layer in range(LAYERS):
        w_in, w_gate, w_up = w["w_in"][layer], w["w_gate"][layer], w["w_up"][layer]

        def put(stage, k, m):
            tile = tiles[layer * TILES + STAGES[stage][0] + k]
            m = m.transpose(1, 0, 2).reshape(P, -1)
            tile[:, :m.shape[1]] = m

        def cols(matrix, at, n=P):
            return matrix[:, at:at + n].reshape(-1, P, n)
        for k in range(48):
            put("ada", k, cols(w["w_ada"][layer], k * P))
        for k in range(XBC_B):
            put("proj", k, cols(w_in, o_xbc + k * P))
        pe = w_in[:, o_kv + KVL:o_kv + KVL + ROPE]
        put("proj", XBC_B, np.concatenate([w_in[:, o_dt:o_dt + 32], pe[:, swap], pe, pe], 1).reshape(-1, P, P))
        for k in range(KVB):
            put("proj", XBC_B + 1 + k, cols(w_in, o_kv + k * P))
        for k in range(QB):
            put("proj", XBC_B + 1 + KVB + k, cols(w_in, o_q + k * P))
        for k in range(DB):
            put("z", k, cols(w_in, k * P))
            put("f", k, cols(w_in, o_f + k * P))
            put("w_o", k, cols(w["w_o"][layer], k * P))
            for b, name in enumerate(("ssd", "mla", "fft")):
                put(f"out_{name}", 2 * k, cols(w_gate, b * D + k * P))
                put(f"out_{name}", 2 * k + 1, cols(w[f"w_{name}_out"][layer], k * P))
        q_up = w["w_q_up"][layer].reshape(QB, P, HEADS, HD + ROPE)
        q_up = np.concatenate([q_up, q_up[..., HD:][..., swap]], 3)
        kv_up = w["w_kv_up"][layer].reshape(KVB, P, HEADS, 2 * HD)
        for half in range(2):
            for i in range(4):
                h = half * HALF + 2 * i
                put(f"heads{half}", i, q_up[:, :, h:h + 2].transpose(2, 0, 1, 3).reshape(2 * QB, P, P))
            for i in range(2):
                h = half * HALF + 4 * i
                k_part = kv_up[:, :, h:h + 4, :HD].reshape(KVB, P, 2, 2 * HD).transpose(2, 0, 1, 3)
                put(f"heads{half}", 4 + i, k_part.reshape(2 * KVB, P, P))
                put(f"heads{half}", 6 + i, kv_up[:, :, h:h + 4, HD:].reshape(KVB, P, 4 * HD))
            for i in range(FF_H):
                b = half * FF_H + i
                put(f"up{half}", 2 * i, cols(w_up, b * P))
                put(f"up{half}", 2 * i + 1, cols(w_up, (FF_B + b) * P))
                put(f"down{half}", i, w["w_down"][layer][b * P:(b + 1) * P].reshape(1, P, D))
    return tiles


def pack_params(w):
    out = np.zeros((LAYERS, P, N_PARAMS), np.float32)

    def put(name, value):
        at, n = PARAMS[name]
        out[:, :, at:at + n] = value.transpose(1, 0, 2)

    def columns(v):
        return v.reshape(LAYERS, -1, P).transpose(2, 0, 1)
    for name in ("b_ada", "g_pre_mix", "g_post_mix", "g_pre_ffn", "g_post_ffn", "b_gate"):
        put(name, columns(w[name]))
    put("g_ssd", columns(w["g_ssd_norm"]))
    put("g_q", columns(w["g_q_norm"]))
    put("g_kv", columns(w["g_kv_norm"]))
    put("conv_b", columns(w["conv_ssd_b"]))
    put("conv_w", w["conv_ssd_w"].reshape(LAYERS, 3, XBC_B, P).transpose(3, 0, 2, 1).reshape(P, LAYERS, -1))
    put("ffn_b", w["conv_ffn_b"].reshape(LAYERS, 2, FF_B, P).transpose(3, 0, 2, 1).reshape(P, LAYERS, -1))
    put("ffn_w", w["conv_ffn_w"].reshape(LAYERS, 3, 2, FF_B, P).transpose(4, 0, 3, 2, 1).reshape(P, LAYERS, -1))
    put("d_skip", columns(np.repeat(w["d_skip"], HD, axis=1)))
    put("dt_bias", np.broadcast_to(w["dt_bias"].reshape(1, LAYERS, 32), (P, LAYERS, 32)))
    put("a_log", np.broadcast_to(w["a_log"].reshape(1, LAYERS, 32), (P, LAYERS, 32)))
    return out


def feature_major(v):
    return v.reshape(v.shape[0], -1, P).transpose(2, 1, 0)


def kernel(**inputs):
    import concourse.bacc as bacc
    from concourse.bass_utils import run_bass_kernel_spmd

    w = {k: np.ascontiguousarray(v) for k, v in inputs.items()}
    arrays = {
        "in_x": feature_major(np.concatenate([w["x_prompt"][0], w["x_sample"][0]], 0)),
        "in_cond": feature_major(np.stack([w["c_ctx"], w["c"][0]])),
        "in_state": w["state_ssm"][0].transpose(0, 4, 1, 2, 3).reshape(LAYERS, STATE, 2, D),
        "in_ckv": w["cache_ckv"][0].reshape(LAYERS, PAST, KVB, P).transpose(0, 3, 2, 1),
        "in_kpe": w["cache_kpe"][0].transpose(0, 2, 1),
        "in_params": pack_params(w),
        "in_consts": constant_tables(),
        "in_weights": pack_weights(w),
    }
    arrays = {k: np.ascontiguousarray(v) for k, v in arrays.items()}
    outs = {
        "out_x": (P, DB, T),
        "out_ckv": (LAYERS, P, KVB, CTX),
        "out_kpe": (LAYERS, ROPE, CTX),
        "out_state": (LAYERS, 2, STATE, D),
    }
    nc = bacc.Bacc("TRN2", target_bir_lowering=False, num_devices=1)
    args = [nc.dram_tensor(k, v.shape, F32, kind="ExternalInput").ap() for k, v in arrays.items()]
    args += [nc.dram_tensor(k, s, F32, kind="ExternalOutput").ap() for k, s in outs.items()]
    build_program(nc, *args)
    r = run_bass_kernel_spmd(nc, [arrays], core_ids=[0]).results[0]
    y = r["out_x"].transpose(2, 1, 0).reshape(T, D)
    return (
        y[None, :CTX], y[None, CTX:],
        r["out_ckv"].transpose(0, 3, 2, 1).reshape(1, LAYERS, CTX, KVL),
        r["out_kpe"].transpose(0, 2, 1)[None],
        r["out_state"].reshape(LAYERS, 2, STATE, HEADS, HD).transpose(0, 1, 3, 4, 2)[None],
    )
```

```python
from contextlib import ExitStack

import numpy as np

import concourse.bass as bass
from concourse import mybir

F32 = mybir.dt.float32
F32R = mybir.dt.float32r
BF16 = mybir.dt.bfloat16
ALU = mybir.AluOpType
ACT = mybir.ActivationFunctionType
AX = mybir.AxisListType

P = 128
LAYERS = 2
CTX, LAT, PAST = 128, 256, 128
T = CTX + LAT
KEYS = T + PAST
D = 1024
DB = D // P
HEADS = 16
HALF = HEADS // 2
HD = 64
STATE = 128
ROPE = 32
QL, KVL = 384, 256
QB, KVB = QL // P, KVL // P
XBC_B = 12
FF_B = 22
FF_H = FF_B // 2
GROUP_W = 256
GROUPS = 4
EPS = 1e-6
ATTN_SCALE = float((HD + ROPE) ** -0.5)
SEGS = ((0, CTX), (CTX, T))
CHUNKS = T // P
PROB = 3 * LAT + CTX

RING = 4
AHEAD = 2
STAGES = {}
TILES = 0
for _name, _count in (("proj", 18), ("z", 8), ("out_ssd", 16), ("heads0", 8), ("heads1", 8),
                      ("out_mla", 16), ("f", 8), ("out_fft", 16), ("w_o", 8),
                      ("up0", 22), ("down0", 11), ("up1", 22), ("down1", 11)):
    STAGES[_name] = (TILES, _count)
    TILES += _count
TURNS = TILES // RING
assert TILES % RING == 0

SIDE = 12
SIDE_TILES = 4
SIDE_ARRIVED = [16, 16, 32, 32, 64, 64, 80, 80, 96, 96, 112, 112]

PARAMS = {}
N_PARAMS = 0
for _name, _count in (("b_ada", 48), ("g_pre_mix", 8), ("g_post_mix", 8), ("g_pre_ffn", 8), ("g_post_ffn", 8),
                      ("b_gate", 24), ("conv_w", 36), ("conv_b", 12), ("ffn_w", 132), ("ffn_b", 44),
                      ("d_skip", 8), ("g_ssd", 8), ("g_q", 3), ("g_kv", 2), ("dt_bias", 32), ("a_log", 32)):
    PARAMS[_name] = (N_PARAMS, _count)
    N_PARAMS += _count

CONSTS = {}
N_CONSTS = 0
for _name, _count in (("ident", 128), ("tri", 256), ("ones", 128), ("rope", T), ("dft_ch", 2 * 512),
                      ("dft_lat", 2 * 2 * 256), ("dft_ctx", 2 * 128)):
    CONSTS[_name] = (N_CONSTS, _count)
    N_CONSTS += _count
N_KEPT = CONSTS["dft_ch"][0]
N_DFT = N_CONSTS - N_KEPT


class Signal:

    def __init__(self, sem, per_layer):
        self.sem, self.per_layer = sem, per_layer

    def at(self, layer, n):
        return layer * self.per_layer + n


DVE_LINKS = 61
ACT_LINKS = 0


def build_program(nc, a_x, a_cond, a_state, a_ckv, a_kpe, a_params, a_consts, a_weights, a_ada,
                  o_x, o_ckv, o_kpe, o_state):
    ctx = ExitStack()
    with ctx:
        def sb(name, shape, dt=F32):
            return ctx.enter_context(nc.sbuf_tensor(name, shape, dt))

        def sem(name):
            return ctx.enter_context(nc.semaphore(name))

        def signal(name, per_layer):
            return Signal(sem(name), per_layer)

        consts = sb("consts", [P, N_KEPT])
        params = sb("params", [P, N_PARAMS])
        raw = sb("raw", [P, RING, 1024])
        w_hi = sb("w_hi", [P, AHEAD, 1024], F32R)
        w_lo = sb("w_lo", [P, AHEAD, 1024], F32R)
        x = sb("x", [P, DB, T])
        cond = sb("cond", [P, DB, 2])
        cond_pad = sb("cond_pad", [P, DB, 14])
        mod = sb("mod", [P, DB, 2])
        coef = sb("coef", [P, 6, DB, 2])
        h_hi = sb("h_hi", [P, DB, T], F32R)
        h_lo = sb("h_lo", [P, DB, T], F32R)
        in_hi = sb("in_hi", [P, DB * T + KVB * KEYS + QB * T], F32R)
        in_lo = sb("in_lo", [P, DB * T + KVB * KEYS + QB * T], F32R)
        y_hi, y_lo = (v[:, 0:FF_H * T].rearrange("p (k n) -> p k n", k=FF_H) for v in (in_hi, in_lo))
        kvq_hi, kvq_lo = (v[:, DB * T:] for v in (in_hi, in_lo))
        wide = sb("wide", [P, DB, T])
        mix = sb("mix", [P, DB, T])
        root = sb("root", [P, T])
        rstd = sb("rstd", [P, T])
        conv = sb("conv", [P, AHEAD, T])
        gate = sb("gate", [P, T])
        gated = sb("gated", [P, T])
        kpe = sb("kpe", [96, KEYS])
        low = mix[:, 0:KVB + QB, :]
        ckv = sb("ckv", [P, KVB, KEYS])
        stat = sb("stat", [P, 64])
        region = sb("region", [P, 12 * 1024])

        def view(at, shape):
            n = int(np.prod(shape))
            v = region[:, at:at + n]
            names = [chr(97 + i) for i in range(len(shape))]
            if len(shape) == 1:
                return v
            return v.rearrange(f"p ({' '.join(names)}) -> p {' '.join(names)}",
                               **dict(zip(names[1:], shape[1:])))

        K1 = HEADS * HD
        tok_major = "p k n -> p (k n)"
        side_slot = [view(0, [SIDE_TILES, 1024]), view(4096, [SIDE_TILES, 1024])]
        mod_rows = region[0:8, 12032:12032 + 2 * P].rearrange("p (i n) -> p i n", i=2)
        side_three = {4: wide[:, :, :].rearrange(tok_major), 5: view(0, [3 * 1024])}
        side_last = view(11008, [1024])
        xbc = view(0, [XBC_B, T])
        b_tok = view(4608, [CHUNKS, 256])
        cb = view(5376, [CHUNKS * 2, P])
        kpe_raw = region[:, 6144:6144 + CTX]
        xdt = view(6912, [2, K1])
        decay = view(8960, [2 * HALF, P])
        h_state = view(8960, [2, K1])
        x_end = view(6912, [2, K1])
        off_tok = view(6912, [2, K1])
        xs_tok = mix[:, :, :].rearrange(tok_major).rearrange("p (c n) -> p c n", c=CHUNKS)
        wide_tok = wide[:, :, :].rearrange(tok_major).rearrange("p (c n) -> p c n", c=CHUNKS)
        ctx_states = wide_tok
        scaled = wide_tok[:, 2, :]
        q_t = view(0, [HALF, T])
        k_t = view(3072, [HALF, KEYS])
        v_tok = view(7168, [4, HALF // 2, 3, HD])
        prob_t = view(10240, [2, PROB])
        rot = conv
        f_ch = view(0, [CHUNKS, GROUPS, 512])
        dft = view(12288 - N_DFT, [N_DFT])

        dts = sb("dts", [P, 9, CHUNKS * 32])
        dta_parts = sb("dta_parts", [P, 3, CHUNKS * 32], BF16)
        tri_bf = sb("tri_bf", [P, 2, P], BF16)
        far_bf = sb("far_bf", [P, 2, P], BF16)
        ident_bf = sb("ident_bf", [P, P], BF16)
        dt_t = gated[0:32, :]

        ps = ctx.enter_context(nc.psum_tensor("ps", [P, 8, 512], F32))
        flat = ps[:, :, :].rearrange("p b n -> p (b n)")

        def const(name):
            at, n = CONSTS[name]
            return consts[:, at:at + n] if at < N_KEPT else dft[:, at - N_KEPT:at - N_KEPT + n]

        def param(name, i=0, n=1):
            at = PARAMS[name][0]
            return params[:, at + i:at + i + n]

        ident = const("ident")
        ones = const("ones")
        tri = [const("tri")[:, 0:P], const("tri")[:, P:2 * P]]
        dft_ch = const("dft_ch").rearrange("p (k n) -> p k n", k=2)
        dft_lat = const("dft_lat").rearrange("p (k s n) -> p k s n", k=2, s=2)
        dft_ctx = const("dft_ctx").rearrange("p (s n) -> p s n", s=2)
        rope = const("rope")
        ckv_hi = kvq_hi[:, 0:KVB * KEYS].rearrange("p (k n) -> p k n", k=KVB)
        ckv_lo = kvq_lo[:, 0:KVB * KEYS].rearrange("p (k n) -> p k n", k=KVB)
        q_hi = kvq_hi[:, KVB * KEYS:].rearrange("p (k n) -> p k n", k=QB)
        q_lo = kvq_lo[:, KVB * KEYS:].rearrange("p (k n) -> p k n", k=QB)

        loaded = sem("loaded")
        stored = sem("stored")
        arrived = [Signal(sem(f"arrived{j}"), 16 * TURNS) for j in range(RING)]
        hi_made = signal("hi_made", TILES)
        lo_made = signal("lo_made", TILES)
        used = signal("used", TILES)
        taken = signal("taken", TILES)
        ready = sem("ready")
        cond_ready = sem("cond_ready")
        pool_marks, pe_marks, dve_marks = sem("pool_marks"), sem("pe_marks"), sem("dve_marks")
        squares = signal("squares", 7)
        sums = signal("sums", 7)
        roots = signal("roots", 7)
        side_in = [Signal(sem(f"side_in{i}"), 112) for i in range(2)]
        side_used = signal("side_used", SIDE)
        rows_out = signal("rows_out", SIDE)
        cols_made = signal("cols_made", SIDE // 2)
        cols_taken = signal("cols_taken", SIDE // 2)
        h_value = signal("h_value", 2 * DB)
        h_hi_made = signal("h_hi_made", 2 * DB)
        h_lo_made = signal("h_lo_made", 2 * DB)
        kvq_value = signal("kvq_value", 5)
        kvq_hi_made = signal("kvq_hi_made", 5)
        kvq_lo_made = signal("kvq_lo_made", 5)
        y_value = signal("y_value", 2 * DB)
        y_hi_made = signal("y_hi_made", 4 * DB + FF_B)
        y_lo_made = signal("y_lo_made", 4 * DB + FF_B)
        conv_mid = signal("conv_mid", XBC_B + 2 * FF_B)
        conv_left = signal("conv_left", XBC_B + 2 * FF_B)
        conv_done = signal("conv_done", XBC_B + 2 * FF_B)
        silu_done = signal("silu_done", XBC_B + FF_B + DB)
        ag_value = signal("ag_value", FF_B)
        misc_copied = signal("misc_copied", 1)
        cache_in = signal("cache_in", 32)
        params_in = signal("params_in", 16)
        caches_free = signal("caches_free", 1)
        kpe_ready = signal("kpe_ready", 3)
        kpe_spread = signal("kpe_spread", 3)
        ckv_ready = signal("ckv_ready", 1)
        transposed = signal("transposed", CHUNKS)
        tok_ready = signal("tok_ready", CHUNKS)
        dt_ready = signal("dt_ready", 1)
        acum_sums = signal("acum_sums", 1)
        cb_made = signal("cb_made", 1)
        xdt_ready = signal("xdt_ready", CHUNKS)
        rows_made = signal("rows_made", 4 * CHUNKS)
        decay_ready = signal("decay_ready", 4 * CHUNKS)
        weighted = signal("weighted", 4 * CHUNKS)
        y_diag = signal("y_diag", 4 * CHUNKS)
        y_added = signal("y_added", 2 * CHUNKS)
        state_in = signal("state_in", 16)
        ends_ready = signal("ends_ready", 4)
        states_made = signal("states_made", 4)
        new_state = signal("new_state", 2)
        state_out = signal("state_out", 32)
        state_next = signal("state_next", 2)
        off_made = signal("off_made", 4)
        off_ready = signal("off_ready", 4)
        off_turned = signal("off_turned", 2)
        off_back = signal("off_back", 2)
        gate_made = signal("gate_made", 3 * DB)
        q_plain = signal("q_plain", HALF)
        q_rot = signal("q_rot", 3 * HALF)
        k_even = signal("k_even", 4)
        k_odd = signal("k_odd", 4)
        v_ready = signal("v_ready", 4)
        scored = signal("scored", HEADS)
        maxed = signal("maxed", HEADS)
        max_turned = signal("max_turned", HEADS)
        max_in = signal("max_in", HEADS)
        scored_t = signal("scored_t", HEADS)
        exped = signal("exped", HEADS)
        o_made = signal("o_made", HEADS)
        o_ready = signal("o_ready", HEADS)
        dft_in = signal("dft_in", 16)
        f_ready = signal("f_ready", DB)
        ch_made = signal("ch_made", CHUNKS * GROUPS)
        ch_taken = signal("ch_taken", CHUNKS * GROUPS)
        pos_made = signal("pos_made", DB)
        wo_ready = signal("wo_ready", DB)
        down_made = signal("down_made", 2)
        down_taken = signal("down_taken", 2)
        x_ready = signal("x_ready", 1)
        x_mid = signal("x_mid", 1)
        dt_abs = signal("dt_abs", 1)
        dt_exp = signal("dt_exp", 2)
        to_end = signal("to_end", 1)
        mixed = signal("mixed", 1 + 2 * DB)
        dve_chain = signal("dve_chain", DVE_LINKS)
        act_chain = signal("act_chain", ACT_LINKS)

        def through(eng, stage, body):
            t, count = STAGES[stage]
            first, end = t, t + count
            while t % RING and t < end:
                body(t, t // RING, t % RING, t - first)
                t += 1
            turns = (end - t) // RING
            if turns > 1:
                with eng.Fori(0, turns) as r:
                    for j in range(RING):
                        body(r * RING + (t + j), r + t // RING, j, r * RING + (t + j - first))
                t += turns * RING
            while t < end:
                body(t, t // RING, t % RING, t - first)
                t += 1

        def at_tile(slot, name="raw"):
            return raw[:, slot % RING, :]

        def settle(eng, mark):
            eng.sem_inc(mark, 1)

        def after(dve):
            settle(dve, dve_marks)
            return dve.engine_nop()

        def spread(ap, n):
            return ap.unsqueeze(2).broadcast_to([ap.shape[0], ap.shape[1], n])

        def repeat(ap, n):
            return ap.unsqueeze(1).broadcast_to([ap.shape[0], n, ap.shape[1]])

        def ssd(pe, L):
            for c in range(CHUNKS):
                at = (0, 3, 0)[c] * 512
                if c == 2:
                    pe.wait_ge(tok_ready.sem, tok_ready.at(L, 1))
                if c == 1:
                    pe.wait_ge(rows_out.sem, rows_out.at(L, 5))
                cols = slice(c * P, (c + 1) * P)
                for b in range(10):
                    pe.transpose(flat[:, at + b * P:at + (b + 1) * P], xbc[:, b, cols], ident)
                m = pe.transpose(flat[:, at + 10 * P:at + 10 * P + 32], dt_t[:, cols], ident[0:32, 0:32])
                m.then_inc(transposed.sem, 1)
            for c in range(CHUNKS):
                cols = slice(c * P, (c + 1) * P)
                for g in range(2):
                    m = pe.matmul(flat[:, 6 * 512 + (2 * c + g) * P:6 * 512 + (2 * c + g + 1) * P],
                                  xbc[:, 8 + g, cols], xbc[:, 10 + g, cols], start=True, stop=True)
            m.then_inc(cb_made.sem, 1)
            pe.wait_ge(dt_ready.sem, dt_ready.at(L, 1))
            pe.wait_ge(tok_ready.sem, tok_ready.at(L, CHUNKS))
            dta = dts[:, 1, :].rearrange("p (c d h) -> p c d h", c=CHUNKS, d=2)
            for d in range(2):
                pe.matmul(ps[:, 3, d * 48:(d + 1) * 48], tri[d], dta[:, :, d, :], start=True, stop=True)
            pe.matmul(ps[:, 3, 96:192], ones, dts[:, 1, :], start=True, stop=True).then_inc(acum_sums.sem, 1)

            def state(n):
                d, c = STATES[n]
                pe.wait_ge(ends_ready.sem, ends_ready.at(L, n + 1))
                if n >= 2:
                    pe.wait_ge(new_state.sem, new_state.at(L, n - 1))
                for g in range(2):
                    m = pe.matmul(ps[:, 2 * (n % 2) + g, :], b_tok[:, c, g * P:(g + 1) * P],
                                  x_end[:, n % 2, g * 512:(g + 1) * 512], start=True, stop=True)
                m.then_inc(states_made.sem, 1)

            def entering(n):
                d, c = ENTERING[n]
                if n < 2:
                    pe.wait_ge(state_in.sem, state_in.at(L, 16))
                else:
                    pe.wait_ge(state_next.sem, state_next.at(L, n - 1))
                    pe.wait_ge(off_ready.sem, off_ready.at(L, n - 1))
                for g in range(2):
                    m = pe.matmul(ps[:, 4 + 2 * (n % 2) + g, :], xbc[:, 10 + g, c * P:(c + 1) * P],
                                  h_state[:, d, g * 512:(g + 1) * 512], start=True, stop=True)
                m.then_inc(off_made.sem, 1)
            for n in range(4):
                state(n)
            for n in range(4):
                entering(n)
            pe.wait_ge(off_ready.sem, off_ready.at(L, 4))
            for c in range(2):
                for b in range(DB):
                    m = pe.transpose(ps[:, 2 * c + b // 4, b % 4 * P:(b % 4 + 1) * P], off_tok[:, c, b * P:(b + 1) * P],
                                     ident)
                m.then_inc(off_turned.sem, 1)

            def rows(u):
                c, g, d = UNITS[u]
                if u >= 2:
                    pe.wait_ge(decay_ready.sem, decay_ready.at(L, u - 1))
                for h in range(HALF):
                    bank = ps[:, 4 + 2 * (u % 2) + h // 4, :]
                    if h % 4 == 0:
                        pe.matmul(bank, ident_bf[:, :], repeat(far_bf[:, d, :], 4), start=True, stop=False)
                    at = c * 32 + d * 16 + g * HALF + h
                    for i in range(3):
                        m = pe.matmul(bank[:, h % 4 * P:(h % 4 + 1) * P],
                                      dta_parts[:, i, at:at + 1].broadcast_to([P, P]), tri_bf[:, d, :],
                                      start=False, stop=(h % 4 == 3 and i == 2))
                m.then_inc(rows_made.sem, 1)

            rows(0)
            for u, (c, g, d) in enumerate(UNITS):
                if u + 1 < len(UNITS):
                    rows(u + 1)
                if u == 0:
                    pe.wait_ge(off_back.sem, off_back.at(L, 2))
                if d == 0 and u >= 8:
                    pe.wait_ge(y_added.sem, y_added.at(L, u // 2 - 3))
                pe.wait_ge(xdt_ready.sem, xdt_ready.at(L, c + 1))
                pe.wait_ge(weighted.sem, weighted.at(L, u + 1))
                for h in range(HALF):
                    half = h % 2 * HD
                    m = pe.matmul(ps[half:half + HD, (u // 2) % 4, h // 2 * P:(h // 2 + 1) * P],
                                  xdt[:, d, (g * HALF + h) * HD:(g * HALF + h + 1) * HD], decay[:, u % 2 * HALF + h, :],
                                  start=(d == 0 and h < 2), stop=(d == 1), skip_group_check=True)
                m.then_inc(y_diag.sem, 1)

        def attention(pe, L, half, product, weights, tile_in):
            t0 = STAGES[f"heads{half}"][0]
            for i in range(4):
                t = t0 + i
                tile_in(L, t)
                if half == 0 and i == 0:
                    pe.wait_ge(kvq_lo_made.sem, kvq_lo_made.at(L, 5))
                for hh in range(2):
                    m = product(ps[:, 2 * (t % AHEAD) + hh, 0:T],
                                [(*weights(t, hh * QB + kk), q_hi[:, kk, :], q_lo[:, kk, :]) for kk in range(QB)])
                m.then_inc(used.sem, 1)
            for i in range(2):
                t = t0 + 4 + i
                tile_in(L, t)
                for b in range(2):
                    m = product(ps[:, 2 * (t % AHEAD) + b, :],
                                [(*weights(t, b * KVB + kk), ckv_hi[:, kk, :], ckv_lo[:, kk, :]) for kk in range(KVB)])
                m.then_inc(used.sem, 1)
            for i in range(2):
                t = t0 + 6 + i
                tile_in(L, t)
                for s in range(KEYS // P):
                    cols = slice(s * P, (s + 1) * P)
                    parts = []
                    for kk in range(KVB):
                        wh, wl = weights(t, 0, n=256, at=kk * 256)
                        parts.append((ckv_hi[:, kk, cols], ckv_lo[:, kk, cols], wh, wl))
                    m = product(ps[:, 2 * (t % AHEAD) + s // 2, (s % 2) * 256:(s % 2 + 1) * 256], parts)
                m.then_inc(used.sem, 1)
            pe.wait_ge(taken.sem, taken.at(L, t0 + 8 + AHEAD))
            pe.wait_ge(v_ready.sem, v_ready.at(L, 2 * half + 2))
            pe.wait_ge(kpe_spread.sem, kpe_spread.at(L, 3))

            base = half * HALF

            def scores(h):
                if h:
                    pe.wait_ge(maxed.sem, maxed.at(L, base + h))
                for qt in range(CHUNKS):
                    keys, at = (slice(0, CTX), 0) if qt == 0 else (slice(CTX, KEYS), CTX + (qt - 1) * T)
                    m = pe.matmul(flat[:, at:at + keys.stop - keys.start], q_t[0:96, h, qt * P:(qt + 1) * P],
                                  k_t[0:96, h, keys], start=True, stop=True)
                m.then_inc(scored.sem, 1)

            def maxima(h):
                pe.wait_ge(maxed.sem, maxed.at(L, base + h + 1))
                for qt in range(CHUNKS):
                    m = pe.matmul(ps[96:97, 6, qt * P:(qt + 1) * P], stat[:, 3 * (h % 2) + qt:3 * (h % 2) + qt + 1], ident,
                                  start=True, stop=True)
                m.then_inc(max_turned.sem, 1)

            def scores_t(h):
                pe.wait_ge(max_in.sem, max_in.at(L, base + h + 1))
                if h:
                    pe.wait_ge(exped.sem, exped.at(L, base + h))
                for i in range(4):
                    keys, queries = (i + 1, slice(CTX, T)) if i < 3 else (0, slice(0, CTX))
                    at = 1024 + i * LAT
                    m = pe.matmul(flat[:, at:at + queries.stop - queries.start], k_t[0:97, h, keys * P:(keys + 1) * P],
                                  q_t[0:97, h, queries], start=True, stop=True)
                m.then_inc(scored_t.sem, 1)

            def output(h):
                pe.wait_ge(exped.sem, exped.at(L, base + h + 1))
                if base + h >= 2:
                    pe.wait_ge(o_ready.sem, o_ready.at(L, base + h - 1))

                def v_ones(tile):
                    return v_tok[:, tile, h // 2, h % 2:h % 2 + 2, :]
                p = prob_t[:, h % 2, :]
                pe.matmul(ps[:, 4 + h % 2, 0:CTX], v_ones(0), p[:, 3 * LAT:PROB], start=True, stop=True)
                for i in range(3):
                    m = pe.matmul(ps[:, 4 + h % 2, CTX:T], v_ones(1 + i), p[:, i * LAT:(i + 1) * LAT],
                                  start=(i == 0), stop=(i == 2))
                m.then_inc(o_made.sem, 1)

            scores(0)
            maxima(0)
            for h in range(HALF):
                if h + 1 < HALF:
                    scores(h + 1)
                scores_t(h)
                if h + 1 < HALF:
                    maxima(h + 1)
                if h:
                    output(h - 1)
            output(HALF - 1)

        def fourier(pe, L):
            pe.wait_ge(f_ready.sem, f_ready.at(L, DB))
            pe.wait_ge(dft_in.sem, dft_in.at(L, 16))
            for i in range(CHUNKS * GROUPS):
                c, g = i // GROUPS, i % GROUPS
                if i >= 4:
                    pe.wait_ge(ch_taken.sem, ch_taken.at(L, i - 3))
                for kk in range(2):
                    m = pe.matmul(ps[:, 4 + i % 4, :], wide[:, 2 * g + kk, c * P:(c + 1) * P], dft_ch[:, kk, :],
                                  start=(kk == 0), stop=(kk == 1))
                m.then_inc(ch_made.sem, 1)
            pe.wait_ge(ch_taken.sem, ch_taken.at(L, CHUNKS * GROUPS))
            for b in range(DB):
                g, w = b // 2, (b % 2) * P
                if b >= 4:
                    pe.wait_ge(y_lo_made.sem, y_lo_made.at(L, 2 * DB + b - 3))
                for s in range(2):
                    pe.matmul(ps[:, 4 + b % 4, 0:CTX], f_ch[:, 0, g, s * 256 + w:s * 256 + w + P], dft_ctx[:, s, :],
                              start=(s == 0), stop=(s == 1))
                for i in range(4):
                    c, s = i // 2, i % 2
                    m = pe.matmul(ps[:, 4 + b % 4, CTX:T], f_ch[:, 1 + c, g, s * 256 + w:s * 256 + w + P],
                                  dft_lat[:, c, s, :], start=(i == 0), stop=(i == 3))
                m.then_inc(pos_made.sem, 1)

        STATES = [(0, 0), (1, 0), (0, 1), (1, 2)]
        ENTERING = [(0, 1), (1, 2), (0, 2), (1, 1)]
        UNITS = [(c, g, d) for c in range(CHUNKS) for g in range(2) for d in range(2)]

        def up_stage(eng, half, body):
            t, count = STAGES[f"up{half}"]
            first, end = t, t + count
            def one(t, turn, j, k, par, i):
                body(t, turn, j, k, par == 0, i)
            while t % RING and t < end:
                one(t, t // RING, t % RING, t - first, (t - first) % 2, (t - first) // 2)
                t += 1
            turns = (end - t) // RING
            with eng.Fori(0, turns) as r:
                for j in range(RING):
                    k0 = t + j - first
                    one(r * RING + (t + j), r + t // RING, j, r * RING + k0, k0 % 2, r * (RING // 2) + k0 // 2)
            t += turns * RING
            while t < end:
                one(t, t // RING, t % RING, t - first, (t - first) % 2, (t - first) // 2)
                t += 1

        def sub_stage(eng, first, count, body):
            t, end = first, first + count
            while t % RING and t < end:
                body(t, t // RING, t % RING, t - first)
                t += 1
            turns = (end - t) // RING
            if turns:
                with eng.Fori(0, turns) as r:
                    for j in range(RING):
                        body(r * RING + (t + j), r + t // RING, j, r * RING + (t + j - first))
                t += turns * RING
            while t < end:
                body(t, t // RING, t % RING, t - first)
                t += 1

        def lagged(eng, first, count, body):
            for t in range(first, first + RING):
                body(t, t // RING, t % RING, t - first)
            sub_stage(eng, first + RING, count - RING, lambda t, turn, j, k: body(t, turn, j, k + RING))

        def param_at(name, k, step, i):
            at = PARAMS[name][0]
            start = k * step + (at + i)
            return params[:, bass.ds(start, 1)]

        def gates(L, act, refill, stage, branch):
            def body(t, turn, j, k, i, is_gate):
                refill(L, t, turn, j)
                if is_gate:
                    act.wait_ge(taken.sem, taken.at(L, t + AHEAD))
                    act.activation(gate[:, :], ps[:, 2 * (j % 2), 0:T], ACT.Sigmoid,
                                   bias=param_at("b_gate", i + branch * DB, 1, 0)).then_inc(gate_made.sem, 1)
            pairs(act, stage, body)

        def pairs(eng, stage, body):
            t, count = STAGES[stage]
            first, end = t, t + count
            while t % RING and t < end:
                body(t, t // RING, t % RING, t - first, (t - first) // 2, (t - first) % 2 == 0)
                t += 1
            turns = (end - t) // RING
            with eng.Fori(0, turns) as r:
                for j in range(RING):
                    k0 = t + j - first
                    body(r * RING + (t + j), r + t // RING, j, r * RING + k0, r * (RING // 2) + k0 // 2, k0 % 2 == 0)
            t += turns * RING
            while t < end:
                body(t, t // RING, t % RING, t - first, (t - first) // 2, (t - first) % 2 == 0)
                t += 1

        def ssd_act(L, act, link):
            act.wait_ge(kvq_lo_made.sem, kvq_lo_made.at(L, 5))
            for c in range(CHUNKS):
                at = (0, 3, 0)[c] * 512
                act.wait_ge(transposed.sem, transposed.at(L, c + 1))
                act.activation(xs_tok[:, c, :], flat[:, at:at + 1024], ACT.Copy)
                act.activation(b_tok[:, c, :], flat[:, at + 1024:at + 1280], ACT.Copy)
                act.activation(dts[:, 0, c * 32:(c + 1) * 32], flat[:, at + 1280:at + 1312], ACT.Copy)\
                   .then_inc(tok_ready.sem, 1)
            act.wait_ge(dt_abs.sem, dt_abs.at(L, 1))
            act.activation(dts[:, 3, :], dts[:, 2, :], ACT.Exp, scale=-1.0)
            act.activation(dts[:, 4, 0:32], param("a_log", 0, 32), ACT.Exp).then_inc(dt_exp.sem, 1)
            act.wait_ge(to_end.sem, to_end.at(L, 1))
            act.activation(dts[:, 6, :], dts[:, 5, :], ACT.Exp)
            act.activation(dts[:, 4, :], dts[:, 2, :], ACT.Exp)
            act.activation(dts[:, 7, :], ps[:, 3, 96:192], ACT.Exp).then_inc(dt_exp.sem, 1)
            for u, (c, g, d) in enumerate(UNITS):
                act.wait_ge(rows_made.sem, rows_made.at(L, u + 1))
                if u == 0:
                    act.wait_ge(off_made.sem, off_made.at(L, 4))
                if u >= 2:
                    act.wait_ge(y_diag.sem, y_diag.at(L, u - 1))
                for h in range(HALF):
                    at = c * 32 + d * 16 + g * HALF + h
                    m = act.activation(decay[:, u % 2 * HALF + h, :],
                                       ps[:, 4 + 2 * (u % 2) + h // 4, h % 4 * P:(h % 4 + 1) * P], ACT.Exp,
                                       bias=dts[:, 3, at:at + 1])
                m.then_inc(decay_ready.sem, 1)

        def attention_act(L, act, refill, half):
            t0 = STAGES[f"heads{half}"][0]
            for i in range(4):
                t = t0 + i
                refill(L, t, t // RING, t % RING)
                act.activation(q_t[0:64, 2 * i:2 * i + 2, :], ps[0:64, 2 * (t % 2):2 * (t % 2) + 2, 0:T], ACT.Copy)\
                   .then_inc(q_plain.sem, 1)
            for i in range(2):
                t = t0 + 4 + i
                refill(L, t, t // RING, t % RING)
                act.activation(k_t[0:64, 4 * i:4 * i + 4:2, :], ps[0:64, 2 * (t % 2):2 * (t % 2) + 2, :], ACT.Copy)\
                   .then_inc(k_even.sem, 1)
            for i in range(2):
                t = t0 + 6 + i
                refill(L, t, t // RING, t % RING)
                b = 2 * (t % 2)
                for s in range(4):
                    m = act.activation(v_tok[:, s, 2 * i:2 * i + 2, 0:3:2, :],
                                       flat[:, b * 512 + s * 256:b * 512 + (s + 1) * 256]
                                       .rearrange("p (h e n) -> p h e n", h=2, e=2), ACT.Copy)
                m.then_inc(v_ready.sem, 1)
            if half:
                for b in (2, 3):
                    o_hi(L, b)
            base = half * HALF

            def max_row(h):
                act.wait_ge(max_turned.sem, max_turned.at(L, base + h + 1))
                act.activation(q_t[96:97, h, :], ps[96:97, 6, 0:T], ACT.Copy, scale=-1.0).then_inc(max_in.sem, 1)

            max_row(0)
            for h in range(HALF):
                act.wait_ge(scored_t.sem, scored_t.at(L, base + h + 1))
                if base + h >= 2:
                    act.wait_ge(o_made.sem, o_made.at(L, base + h - 1))
                act.activation(prob_t[:, h % 2, :], flat[:, 1024:1024 + PROB], ACT.Exp, scale=ATTN_SCALE)\
                   .then_inc(exped.sem, 1)
                if h + 1 < HALF:
                    max_row(h + 1)
                if h in (4, 6):
                    o_hi(L, 4 * half + h // 2 - 2)
            if half:
                for b in (6, 7):
                    o_hi(L, b)

        def o_hi(L, b):
            nc.scalar.wait_ge(o_ready.sem, o_ready.at(L, 2 * b + 2))
            nc.scalar.activation(y_hi[:, b, :], wide[:, b, :], ACT.Copy).then_inc(y_hi_made.sem, 1)

        def y_los(L, n, value):
            dve = nc.vector
            for k in range(DB):
                dve.wait_ge(y_hi_made.sem, y_hi_made.at(L, n * DB + k + 1))
                dve.tensor_tensor(y_lo[:, k, :], value(k), y_hi[:, k, :].bitcast(F32), ALU.subtract)\
                   .then_inc(y_lo_made.sem, 1)

        def merge(L, stage, branch):
            dve = nc.vector

            def body(t, turn, j, k, i, is_gate):
                dve.wait_ge(hi_made.sem, hi_made.at(L, t + AHEAD + 1))
                dve.tensor_tensor(w_lo[:, j % AHEAD, :], raw[:, (j + AHEAD) % RING, :],
                                  w_hi[:, j % AHEAD, :].bitcast(F32), ALU.subtract).then_inc(lo_made.sem, 1)
                if is_gate:
                    dve.wait_ge(gate_made.sem, gate_made.at(L, i + branch * DB + 1))
                    after(dve).then_inc(taken.sem, 1)
                    return
                dve.wait_ge(used.sem, used.at(L, t + 1))
                bank = ps[:, 2 * (j % 2), 0:T]
                if branch == 0:
                    dve.tensor_tensor(mix[:, i, :], gate[:, :], bank, ALU.mult).then_inc(taken.sem, 1)
                else:
                    dve.wait_ge(mixed.sem, mixed.at(L, i + (1 + (branch - 1) * DB)))
                    dve.tensor_tensor(gated[:, :], gate[:, :], bank, ALU.mult).then_inc(taken.sem, 1)
                    dve.wait_ge(taken.sem, taken.at(L, t + 1 + AHEAD))
                    dve.tensor_tensor(mix[:, i, :], mix[:, i, :], gated[:, :], ALU.add).then_inc(mixed.sem, 1)
            pairs(dve, stage, body)
            if branch == 0:
                after(dve).then_inc(mixed.sem, 1)

        def ssd_dve(L, dve, link):
            dt, dta, mag, e, ea_log, s2 = (dts[:, i, :] for i in range(6))
            acum, minus_acum, exp_a, end = (dts[:, i, :] for i in (2, 3, 4, 5))
            exp_end, exp_all, poly = (dts[:, i, :] for i in (6, 7, 8))

            def per_head(ap):
                return ap.rearrange("p (c n) -> p c n", c=CHUNKS)
            dve.wait_ge(tok_ready.sem, tok_ready.at(L, CHUNKS))
            link(L, dve.tensor_tensor(per_head(dt), per_head(dt), repeat(param("dt_bias", 0, 32), CHUNKS), ALU.add))
            link(L, dve.tensor_scalar(mag, dt, -1.0, None, ALU.mult))
            dve.tensor_tensor(mag, mag, dt, ALU.max).then_inc(dt_abs.sem, 1)
            dve.wait_ge(dt_exp.sem, dt_exp.at(L, 1))
            link(L, dve.tensor_scalar(s2, e, 2.0, None, ALU.add))
            link(L, dve.reciprocal(s2, s2))
            link(L, dve.tensor_tensor(e, e, s2, ALU.mult))
            link(L, dve.tensor_tensor(s2, e, e, ALU.mult))
            link(L, dve.tensor_scalar(poly, s2, 1.0 / 17, None, ALU.mult))
            for q in (15, 13, 11, 9, 7, 5, 3):
                link(L, dve.scalar_tensor_tensor(out=poly, in0=poly, scalar=1.0 / q, in1=s2, op0=ALU.add, op1=ALU.mult))
            link(L, dve.scalar_tensor_tensor(out=poly, in0=poly, scalar=1.0, in1=e, op0=ALU.add, op1=ALU.mult))
            link(L, dve.tensor_scalar(dt, dt, 0.0, None, ALU.max))
            link(L, dve.scalar_tensor_tensor(out=dt, in0=poly, scalar=2.0, in1=dt, op0=ALU.mult, op1=ALU.add))
            dve.scalar_tensor_tensor(out=per_head(dta), in0=per_head(dt), scalar=-1.0,
                                     in1=repeat(ea_log[:, 0:32], CHUNKS), op0=ALU.mult, op1=ALU.mult)\
               .then_inc(dt_ready.sem, 1)
            dve.wait_ge(dt_ready.sem, dt_ready.at(L, 1))
            link(L, dve.tensor_copy(dta_parts[:, 0, :], dta))
            link(L, dve.tensor_tensor(s2, dta, dta_parts[:, 0, :], ALU.subtract))
            link(L, dve.tensor_copy(dta_parts[:, 1, :], s2))
            link(L, dve.tensor_tensor(dta_parts[:, 2, :], s2, dta_parts[:, 1, :], ALU.subtract))
            dve.wait_ge(cb_made.sem, cb_made.at(L, 1))
            link(L, dve.tensor_copy(cb[:, :, :], flat[:, 6 * 512:6 * 512 + 768].rearrange("p (i n) -> p i n", n=P)))
            dve.wait_ge(acum_sums.sem, acum_sums.at(L, 1))
            for d in range(2):
                m = dve.tensor_copy(acum.rearrange("p (c d h) -> p c d h", c=CHUNKS, d=2)[:, :, d, :],
                                    ps[:, 3, d * 48:(d + 1) * 48].rearrange("p (c h) -> p c h", c=CHUNKS))
            link(L, m)
            dve.tensor_scalar(minus_acum, acum, -1.0, None, ALU.mult)
            dve.tensor_tensor(end, ps[:, 3, 96:192], acum, ALU.subtract).then_inc(to_end.sem, 1)
            dve.wait_ge(dt_exp.sem, dt_exp.at(L, 2))

            def heads(v):
                return v.rearrange("p (h n) -> p h n", n=HD)

            def at_heads(table, d, c):
                return spread(table[:, c * 32 + d * 16:c * 32 + d * 16 + 16], HD)

            link(L, dve.tensor_tensor(poly, dt, exp_end, ALU.mult))
            for n, (d, c) in enumerate(STATES):
                if n >= 2:
                    dve.wait_ge(states_made.sem, states_made.at(L, n - 1))
                dve.tensor_tensor(heads(x_end[:, n % 2, :]), heads(xs_tok[:, c, :]), at_heads(poly, d, c), ALU.mult)\
                   .then_inc(ends_ready.sem, 1)
                if n in (1, 2):
                    dve.wait_ge(states_made.sem, states_made.at(L, n))
                    dve.tensor_copy(ctx_states[:, n - 1, :], flat[:, (n - 1) * 1024:n * 1024]).then_inc(new_state.sem, 1)
            dve.wait_ge(states_made.sem, states_made.at(L, 4))
            for n, (d, c) in enumerate(ENTERING):
                off = flat[:, 2048 + 1024 * (n % 2):3072 + 1024 * (n % 2)]
                dve.wait_ge(off_made.sem, off_made.at(L, n + 1))
                if n < 2:
                    dve.tensor_tensor(heads(off_tok[:, c - 1, :]), heads(off), at_heads(exp_a, d, c), ALU.mult)\
                       .then_inc(off_ready.sem, 1)
                    link(L, dve.tensor_tensor(heads(h_state[:, d, :]), heads(h_state[:, d, :]), at_heads(exp_all, d, c),
                                              ALU.mult))
                    dve.tensor_tensor(h_state[:, d, :], h_state[:, d, :], flat[:, 1024 * n:1024 * (n + 1)], ALU.add)\
                       .then_inc(state_next.sem, 1)
                else:
                    link(L, dve.tensor_tensor(heads(scaled), heads(off), at_heads(exp_a, d, c), ALU.mult))
                    dve.tensor_tensor(off_tok[:, c - 1, :], off_tok[:, c - 1, :], scaled, ALU.add)\
                       .then_inc(off_ready.sem, 1)
                    dve.wait_ge(off_ready.sem, off_ready.at(L, n + 1))
            dve.wait_ge(state_out.sem, state_out.at(L, 32))
            for c in range(2):
                dve.wait_ge(off_turned.sem, off_turned.at(L, c + 1))
                cols = slice((1 + c) * P, (2 + c) * P)
                for b in range(DB):
                    m = dve.scalar_tensor_tensor(out=wide[:, b, cols], in0=xbc[:, b, cols], scalar=param("d_skip", b),
                                                 in1=ps[:, 2 * c + b // 4, b % 4 * P:(b % 4 + 1) * P],
                                                 op0=ALU.mult, op1=ALU.add)
                m.then_inc(off_back.sem, 1)

            def x_dt(c):
                for d in range(2):
                    m = dve.tensor_tensor(heads(xdt[:, d, :]), heads(xs_tok[:, c, :]), at_heads(dt, d, c), ALU.mult)
                m.then_inc(xdt_ready.sem, 1)

            def add_y(n):
                c, g = n // 2, n % 2
                cols = slice(c * P, (c + 1) * P)
                dve.wait_ge(y_diag.sem, y_diag.at(L, 2 * n + 2))
                sums_ = ps[:, n % 4, :].rearrange("p (b n) -> p b n", b=4)
                if c == 0:
                    for b in range(4):
                        m = dve.scalar_tensor_tensor(out=wide[:, 4 * g + b, cols], in0=xbc[:, 4 * g + b, cols],
                                                     scalar=param("d_skip", 4 * g + b), in1=sums_[:, b, :],
                                                     op0=ALU.mult, op1=ALU.add)
                else:
                    m = dve.tensor_tensor(wide[:, 4 * g:4 * g + 4, cols], wide[:, 4 * g:4 * g + 4, cols], sums_, ALU.add)
                m.then_inc(y_added.sem, 1)

            x_dt(0)
            for u, (c, g, d) in enumerate(UNITS):
                dve.wait_ge(decay_ready.sem, decay_ready.at(L, u + 1))
                buf = decay[:, u % 2 * HALF:(u % 2 + 1) * HALF, :]
                dve.tensor_tensor(buf, buf, repeat(cb[:, 2 * c + g, :], HALF), ALU.mult).then_inc(weighted.sem, 1)
                if d == 1 and g == 1:
                    if u + 1 < len(UNITS):
                        dve.wait_ge(y_diag.sem, y_diag.at(L, u + 1))
                        x_dt(c + 1)
                    add_y(u // 2 - 1)
                    add_y(u // 2)
            dve.wait_ge(y_added.sem, y_added.at(L, 2 * CHUNKS))

        def attention_dve(L, dve, link, split, tick_taken, half):
            t0 = STAGES[f"heads{half}"][0]
            for i in range(4):
                t = t0 + i
                split(L, t, t // RING, t % RING)
                dve.wait_ge(q_plain.sem, q_plain.at(L, 4 * half + i + 1))
                b = 2 * (t % 2)
                n = 3 * (4 * half + i)
                if n:
                    dve.wait_ge(q_rot.sem, q_rot.at(L, n))
                dve.tensor_tensor(rot[64:96, :, :], ps[96:128, b:b + 2, 0:T], repeat(rope[96:128, :], 2), ALU.mult)\
                   .then_inc(q_rot.sem, 1)
                dve.tensor_tensor(q_t[64:96, 2 * i:2 * i + 2, :], ps[64:96, b:b + 2, 0:T], repeat(rope[64:96, :], 2),
                                  ALU.mult).then_inc(q_rot.sem, 1)
                dve.wait_ge(q_rot.sem, q_rot.at(L, n + 2))
                tick_taken()
                dve.tensor_tensor(q_t[64:96, 2 * i:2 * i + 2, :], q_t[64:96, 2 * i:2 * i + 2, :], rot[64:96, :, :],
                                  ALU.add).then_inc(q_rot.sem, 1)
            for i in range(2):
                t = t0 + 4 + i
                split(L, t, t // RING, t % RING)
                dve.wait_ge(k_even.sem, k_even.at(L, 2 * half + i + 1))
                b = 2 * (t % 2)
                dve.tensor_copy(k_t[0:64, 4 * i + 1:4 * i + 4:2, :], ps[64:128, b:b + 2, :]).then_inc(taken.sem, 1)
            for i in range(2):
                t = t0 + 6 + i
                split(L, t, t // RING, t % RING)
                dve.wait_ge(v_ready.sem, v_ready.at(L, 2 * half + i + 1))
                tick_taken()
            base = half * HALF

            def o_lo(b):
                dve.wait_ge(y_hi_made.sem, y_hi_made.at(L, DB + b + 1))
                dve.tensor_tensor(y_lo[:, b, :], wide[:, b, :], y_hi[:, b, :].bitcast(F32), ALU.subtract)\
                   .then_inc(y_lo_made.sem, 1)

            def maxima(h):
                dve.wait_ge(scored.sem, scored.at(L, base + h + 1))
                at = 3 * (h % 2)
                dve.tensor_reduce(stat[:, at:at + 1], ps[:, 0, 0:CTX], AX.X, ALU.max)
                dve.tensor_reduce(stat[:, at + 1:at + 3], flat[:, CTX:CTX + 2 * T].rearrange("p (i n) -> p i n", i=2),
                                  AX.X, ALU.max).then_inc(maxed.sem, 1)

            def normalise(h):
                dve.wait_ge(o_made.sem, o_made.at(L, base + h + 1))
                bank = ps[:, 4 + h % 2, 0:T]
                at = h % 2 * HD
                own, other = slice(at, at + HD), slice(HD - at, P - at)
                link(L, dve.reciprocal(gated[own, :], bank[other, :]))
                dve.tensor_tensor(wide[own, (base + h) // 2, :], bank[own, :], gated[own, :], ALU.mult)\
                   .then_inc(o_ready.sem, 1)

            if half:
                for b in (2, 3):
                    o_lo(b)
            maxima(0)
            for h in range(HALF):
                if h + 1 < HALF:
                    maxima(h + 1)
                if h:
                    normalise(h - 1)
                if h in (6, 7):
                    o_lo(4 * half + h - 6)
            normalise(HALF - 1)
            if half:
                for b in (6, 7):
                    o_lo(b)

        block = ctx.enter_context(nc.Block())


        @block.sync
        def _(sp):
            total = LAYERS * TILES
            for t in range(RING):
                sp.dma_start(raw[:, t, :], a_weights[t]).then_inc(arrived[t].sem, 16)
            with sp.Fori(0, total // RING - 1) as r:
                for j in range(RING):
                    sp.wait_ge(lo_made.sem, r * RING + (j + 1))
                    sp.dma_start(raw[:, j, :], a_weights[r * RING + (RING + j)]).then_inc(arrived[j].sem, 16)
            for j in range(AHEAD):
                sp.wait_ge(lo_made.sem, total - RING + j + 1)
                sp.dma_start(raw[:, j, :], a_weights[j]).then_inc(arrived[j].sem, 16)

        @block.gpsimd
        def _(pool):
            pool.dma_start(consts[:, :], a_consts[:, 0:N_KEPT]).then_inc(loaded, 16)
            pool.dma_start(x[:, :, :], a_x).then_inc(loaded, 16)
            pool.dma_start(cond[:, :, :], a_cond).then_inc(loaded, 16)
            def side_load(L, g):
                if g == 4:
                    pool.wait_ge(h_lo_made.sem, h_lo_made.at(L, DB))
                elif g == 5:
                    pool.wait_ge(y_added.sem, y_added.at(L, 2 * CHUNKS))
                elif g == 6:
                    pool.wait_ge(pos_made.sem, pos_made.at(L, DB))
                else:
                    pool.wait_ge(side_used.sem, side_used.at(L, g + 1))
                settle(pool, pool_marks)
                into = side_in[g % 2].sem
                if g in (4, 5):
                    pool.dma_start(side_three[g], a_ada[L, g, :, 0:3072]).then_inc(into, 16)
                    pool.dma_start(side_last, a_ada[L, g, :, 3072:4096]).then_inc(into, 16)
                else:
                    pool.dma_start(side_slot[g % 2], a_ada[L, g].rearrange("p (i n) -> p i n", i=SIDE_TILES))\
                        .then_inc(into, 16)

            with pool.Fori(0, LAYERS) as L:
                side_load(L, 0)
                side_load(L, 1)
                pool.wait_ge(caches_free.sem, caches_free.at(L, 1))
                settle(pool, pool_marks)
                pool.dma_start(params[:, :], a_params[L]).then_inc(params_in.sem, 16)
                pool.dma_start(h_state[:, :, :], a_state[L]).then_inc(state_in.sem, 16)
                pool.dma_start(ckv[:, :, T:KEYS], a_ckv[L]).then_inc(cache_in.sem, 16)
                pool.dma_start(kpe[64:96, T:KEYS], a_kpe[L]).then_inc(cache_in.sem, 16)
                side_load(L, 2)
                side_load(L, 3)
                side_load(L, 4)
                pool.wait_ge(misc_copied.sem, misc_copied.at(L, 1))
                settle(pool, pool_marks)
                pool.dma_start(o_kpe[L], kpe_raw[64:96, :]).then_inc(stored, 16)
                pool.wait_ge(ckv_ready.sem, ckv_ready.at(L, 1))
                settle(pool, pool_marks)
                pool.dma_start(o_ckv[L], ckv[:, :, 0:CTX]).then_inc(stored, 16)
                for d in range(2):
                    pool.wait_ge(new_state.sem, new_state.at(L, d + 1))
                    settle(pool, pool_marks)
                    pool.dma_start(o_state[L, d], ctx_states[:, d, :]).then_inc(state_out.sem, 16)
                side_load(L, 5)
                pool.wait_ge(y_added.sem, y_added.at(L, 2 * CHUNKS))
                pool.wait_ge(kpe_ready.sem, kpe_ready.at(L, 3))
                pool.wait_ge(cache_in.sem, cache_in.at(L, 32))
                pool.wait_ge(stored, (L + 1) * 32)
                settle(pool, pool_marks)
                pool.memset(k_t[96:97, :, :], 1.0).then_inc(kpe_spread.sem, 1)
                pool.wait_ge(kpe_spread.sem, kpe_spread.at(L, 1))
                settle(pool, pool_marks)
                pool.memset(v_tok[:, :, :, 1, :], 1.0).then_inc(kpe_spread.sem, 1)
                pool.wait_ge(kpe_spread.sem, kpe_spread.at(L, 2))
                settle(pool, pool_marks)
                pool.tensor_copy(k_t[64:96, :, :], repeat(kpe[64:96, :], HALF)).then_inc(kpe_spread.sem, 1)
                pool.wait_ge(o_made.sem, o_made.at(L, HEADS))
                settle(pool, pool_marks)
                pool.dma_start(dft, a_consts[:, N_KEPT:]).then_inc(dft_in.sem, 16)
                for g in range(6, SIDE):
                    side_load(L, g)
            pool.wait_ge(x_ready.sem, LAYERS * x_ready.per_layer)
            pool.dma_start(o_x, x[:, :, :]).then_inc(stored, 16)
            pool.wait_ge(stored, 16 * (2 * LAYERS + 1))
            pool.wait_ge(state_out.sem, LAYERS * 32)
            for j in range(AHEAD):
                pool.wait_ge(arrived[j].sem, 16 * (LAYERS * TURNS + 1))

        @block.tensor
        def _(pe):
            def product(out, blocks, first=True, last=True):
                for i, (ah, al, bh, bl) in enumerate(blocks):
                    start, stop = first and i == 0, last and i == len(blocks) - 1
                    pe.matmul(out, ah, bh, start=start, stop=False)
                    pe.matmul(out, ah, bl, start=False, stop=False)
                    m = pe.matmul(out, al, bh, start=False, stop=stop)
                return m

            def weights(j, k, n=P, at=None):
                lo = k * P if at is None else at
                return w_hi[:, j % AHEAD, lo:lo + n], w_lo[:, j % AHEAD, lo:lo + n]

            def tile_in(L, t):
                pe.wait_ge(lo_made.sem, lo_made.at(L, t + 1))
                pe.wait_ge(taken.sem, taken.at(L, t + 1))

            def bank(j):
                return 2 * (j % AHEAD)

            def project(L, stage, hi, lo, n=T):
                def body(t, turn, j, k):
                    tile_in(L, t)
                    product(ps[:, bank(j), 0:n], [(*weights(j, kk), hi[:, kk, 0:n], lo[:, kk, 0:n])
                                                  for kk in range(DB)]).then_inc(used.sem, 1)
                through(pe, stage, body)

            def norm_sum(L, n, blocks, sq):
                pe.wait_ge(squares.sem, squares.at(L, n))
                for kk in range(blocks):
                    m = pe.matmul(ps[:, 7, 0:T], ones, sq[:, kk, :], start=(kk == 0), stop=(kk == blocks - 1))
                m.then_inc(sums.sem, 1)

            def out_project(L, stage):
                def body(t, turn, j, k):
                    tile_in(L, t)
                    hi, lo = (h_hi, h_lo) if j % 2 == 0 else (y_hi, y_lo)
                    product(ps[:, bank(j), 0:T], [(*weights(j, kk), hi[:, kk, :], lo[:, kk, :])
                                                  for kk in range(DB)]).then_inc(used.sem, 1)
                assert STAGES[stage][0] % 2 == 0
                through(pe, stage, body)

            def side(L, g):
                pe.wait_ge(side_in[g % 2].sem, side_in[g % 2].at(L, SIDE_ARRIVED[g]))
                for i in range(SIDE_TILES):
                    if g in (4, 5):
                        tile = side_three[g][:, i * 1024:(i + 1) * 1024] if i < 3 else side_last
                    else:
                        tile = side_slot[g % 2][:, i, :]
                    for kk in range(DB):
                        m = pe.matmul(ps[0:8, 5 + g % 2, 0:P], cond_pad[:, kk, 6 - 2 * i:14 - 2 * i],
                                      tile[:, kk * P:(kk + 1) * P], start=(i == 0 and kk == 0),
                                      stop=(i == SIDE_TILES - 1 and kk == DB - 1))
                m.then_inc(side_used.sem, 1)

            def columns(L, v):
                pe.wait_ge(rows_out.sem, rows_out.at(L, 2 * v + 2))
                if v:
                    pe.wait_ge(cols_taken.sem, cols_taken.at(L, v))
                for p in range(2):
                    m = pe.matmul(ps[:, 4, 8 * p:8 * p + 8], mod_rows[:, p, :], ident[0:8, 0:8], start=True, stop=True)
                m.then_inc(cols_made.sem, 1)

            pe.wait_ge(loaded, 48)
            pe.wait_ge(cond_ready, 2)
            pe.wait_ge(side_used.sem, 2)
            with pe.Fori(0, LAYERS) as L:
                side(L, 0)
                side(L, 1)
                norm_sum(L, 1, DB, wide)
                columns(L, 0)
                side(L, 2)
                side(L, 3)
                columns(L, 1)
                pe.wait_ge(h_lo_made.sem, h_lo_made.at(L, DB))
                settle(pe, pe_marks)
                project(L, "proj", h_hi, h_lo)
                norm_sum(L, 2, KVB, mix[:, KVB + QB:, :])
                side(L, 4)
                norm_sum(L, 3, QB, mix[:, KVB + QB:, :])
                ssd(pe, L)
                pe.wait_ge(y_added.sem, y_added.at(L, 2 * CHUNKS - 1))
                project(L, "z", h_hi, h_lo)
                norm_sum(L, 4, DB, mix)
                side(L, 5)
                pe.wait_ge(y_lo_made.sem, y_lo_made.at(L, DB))
                out_project(L, "out_ssd")
                columns(L, 2)
                pe.wait_ge(cols_taken.sem, cols_taken.at(L, 3))
                attention(pe, L, 0, product, weights, tile_in)
                attention(pe, L, 1, product, weights, tile_in)
                pe.wait_ge(y_lo_made.sem, y_lo_made.at(L, 2 * DB))
                out_project(L, "out_mla")
                project(L, "f", h_hi, h_lo)
                fourier(pe, L)
                pe.wait_ge(y_lo_made.sem, y_lo_made.at(L, 3 * DB))
                out_project(L, "out_fft")
                side(L, 6)
                pe.wait_ge(y_lo_made.sem, y_lo_made.at(L, 4 * DB))
                project(L, "w_o", y_hi, y_lo)
                norm_sum(L, 5, DB, mix)
                side(L, 7)
                columns(L, 3)
                side(L, 8)
                norm_sum(L, 6, DB, mix)
                side(L, 9)
                columns(L, 4)
                pe.wait_ge(h_lo_made.sem, h_lo_made.at(L, 2 * DB))
                for half in range(2):
                    if half:
                        pe.wait_ge(down_taken.sem, down_taken.at(L, 1))
                        side(L, 11)
                    project(L, f"up{half}", h_hi, h_lo)
                    if half == 0:
                        side(L, 10)
                        pe.wait_ge(cols_taken.sem, cols_taken.at(L, 5))
                        pe.wait_ge(rows_out.sem, rows_out.at(L, 11))
                    else:
                        columns(L, 5)
                        pe.wait_ge(cols_taken.sem, cols_taken.at(L, 6))
                    pe.wait_ge(taken.sem, taken.at(L, STAGES[f"down{half}"][0] + AHEAD))

                    def down(t, turn, j, k, half=half):
                        pe.wait_ge(lo_made.sem, lo_made.at(L, t + 1))
                        pe.wait_ge(y_lo_made.sem, y_lo_made.at(L, 4 * DB + half * FF_H + 1 + k))
                        for b in range(DB):
                            wh, wl = weights(j, b)
                            m = product(ps[:, b, 0:T], [(wh, wl, y_hi[:, k, :], y_lo[:, k, :])],
                                        first=(k == 0), last=(k == FF_H - 1))
                        m.then_inc(used.sem, 1)
                    t0 = STAGES[f"down{half}"][0]
                    for k in range(FF_H):
                        down(t0 + k, (t0 + k) // RING, (t0 + k) % RING, k)
                    m = pe.matmul(ps[0:1, 7, 510:511], ones[:, 0:1], ones[:, 0:1], start=True, stop=True)
                    m.then_inc(down_made.sem, 1)
                pe.wait_ge(down_taken.sem, down_taken.at(L, 2))
                norm_sum(L, 7, DB, mix)

        @block.scalar
        def _(act):
            steps = [0]

            def link(L, ins):
                steps[0] += 1
                ins.then_inc(act_chain.sem, 1)
                act.wait_ge(act_chain.sem, act_chain.at(L, steps[0]))

            def refill(L, t, turn, j):
                act.wait_ge(used.sem, used.at(L, t + 1))
                nxt = (j + AHEAD) % RING
                act.wait_ge(arrived[nxt].sem, arrived[nxt].at(L, 16 * (turn + (j + AHEAD) // RING + 1)))
                act.activation(w_hi[:, j % AHEAD, :], raw[:, nxt, :], ACT.Copy).then_inc(hi_made.sem, 1)

            def idle(L, stage):
                through(act, stage, lambda t, turn, j, k: refill(L, t, turn, j))

            def rows(L, g):
                act.wait_ge(side_used.sem, side_used.at(L, g + 3))
                if g >= 2:
                    act.wait_ge(cols_made.sem, cols_made.at(L, g // 2))
                act.activation(mod_rows[:, g % 2, :], ps[0:8, 5 + g % 2, 0:P], ACT.Copy).then_inc(rows_out.sem, 1)

            def norm(L, n, src, width, sq, groups=()):
                act.activation(sq, src, ACT.Square).then_inc(squares.sem, 1)
                for g in groups:
                    rows(L, g)
                act.wait_ge(sums.sem, sums.at(L, n))
                act.activation(root[:, :], ps[:, 7, 0:T], ACT.Sqrt, scale=1.0 / width, bias=eps[:, 0:1]).then_inc(roots.sem, 1)

            eps = stat[:, 63:64]
            act.wait_ge(loaded, 48)
            act.wait_ge(ready, 1)
            act.activation(cond_pad[:, :, 6:8], cond[:, :, :], ACT.Silu).then_inc(cond_ready, 1)
            for t in range(AHEAD):
                act.wait_ge(arrived[t].sem, 16)
                act.activation(w_hi[:, t, :], raw[:, t, :], ACT.Copy).then_inc(hi_made.sem, 1)
            with act.Fori(0, LAYERS) as L:
                act.wait_ge(params_in.sem, params_in.at(L, 16))
                norm(L, 1, x[:, :, :], D, wide[:, :, :], (0, 1))
                rows(L, 2)
                rows(L, 3)
                for k in range(DB):
                    act.wait_ge(h_value.sem, h_value.at(L, k + 1))
                    act.activation(h_hi[:, k, :], wide[:, k, :], ACT.Copy).then_inc(h_hi_made.sem, 1)

                def centre(L, j, w_name, b_name, k):
                    act.activation(conv[:, j % 2, :], ps[:, 2 * (j % 2), 0:T], ACT.Identity,
                                   scale=param_at(w_name, k, 3, 1), bias=param_at(b_name, k, 1, 0))\
                       .then_inc(conv_mid.sem, 1)

                def xbc_silu(j, k):
                    act.wait_ge(conv_done.sem, conv_done.at(L, k + 1))
                    act.activation(xbc[:, k, :], conv[:, j % 2, :], ACT.Silu).then_inc(silu_done.sem, 1)

                def proj(t, turn, j, k):
                    refill(L, t, turn, j)
                    if not (isinstance(k, int) and k < 2):
                        act.wait_ge(silu_done.sem, silu_done.at(L, k - 1))
                    centre(L, j, "conv_w", "conv_b", k)
                    if not (isinstance(k, int) and k == 0):
                        xbc_silu(j + 1, k - 1)
                t0 = STAGES["proj"][0]
                lagged(act, t0, XBC_B, proj)
                for k in range(XBC_B, 18):
                    t = t0 + k
                    refill(L, t, t // RING, t % RING)
                    if k == XBC_B:
                        xbc_silu(k - 1, k - 1)
                        bank = ps[:, 2 * (t % 2), :]
                        act.activation(dt_t[:, :], bank[0:32, 0:T], ACT.Copy)
                        act.activation(kpe_raw[64:96, :], bank[64:96, 0:CTX], ACT.Copy).then_inc(misc_copied.sem, 1)
                act.wait_ge(taken.sem, taken.at(L, t0 + 18 + AHEAD))
                norm(L, 2, low[:, 0:KVB, :], KVL, mix[:, KVB + QB:KVB + QB + KVB, :])
                act.wait_ge(kvq_value.sem, kvq_value.at(L, 2))
                act.wait_ge(cache_in.sem, cache_in.at(L, 32))
                for k in range(KVB):
                    act.activation(ckv_hi[:, k, :], ckv[:, k, :], ACT.Copy).then_inc(kvq_hi_made.sem, 1)
                norm(L, 3, low[:, KVB:, :], QL, mix[:, KVB + QB:, :], (4,))
                act.wait_ge(kvq_value.sem, kvq_value.at(L, 5))
                for k in range(QB):
                    act.activation(q_hi[:, k, :], low[:, KVB + k, :], ACT.Copy).then_inc(kvq_hi_made.sem, 1)
                ssd_act(L, act, link)

                def z_tile(t, turn, j, k):
                    refill(L, t, turn, j)
                    act.activation(conv[:, j % 2, :], ps[:, 2 * (j % 2), 0:T], ACT.Silu).then_inc(silu_done.sem, 1)
                through(act, "z", z_tile)
                act.wait_ge(y_value.sem, y_value.at(L, DB))
                norm(L, 4, wide[:, :, :], D, mix[:, :, :])
                act.wait_ge(y_value.sem, y_value.at(L, 2 * DB))
                for k in range(DB):
                    act.activation(y_hi[:, k, :], wide[:, k, :], ACT.Copy).then_inc(y_hi_made.sem, 1)
                rows(L, 5)
                gates(L, act, refill, "out_ssd", 0)

                attention_act(L, act, refill, 0)
                attention_act(L, act, refill, 1)
                gates(L, act, refill, "out_mla", 1)

                def f_tile(t, turn, j, k):
                    refill(L, t, turn, j)
                    act.activation(wide[:, k, :], ps[:, 2 * (j % 2), 0:T], ACT.Copy).then_inc(f_ready.sem, 1)
                through(act, "f", f_tile)
                for i in range(CHUNKS * GROUPS):
                    act.wait_ge(ch_made.sem, ch_made.at(L, i + 1))
                    act.activation(f_ch[:, i // GROUPS, i % GROUPS, :], ps[:, 4 + i % 4, :], ACT.Copy)\
                       .then_inc(ch_taken.sem, 1)
                for b in range(DB):
                    act.wait_ge(pos_made.sem, pos_made.at(L, b + 1))
                    act.activation(y_hi[:, b, :], ps[:, 4 + b % 4, 0:T], ACT.Copy).then_inc(y_hi_made.sem, 1)
                gates(L, act, refill, "out_fft", 2)
                act.wait_ge(mixed.sem, mixed.at(L, 1 + 2 * DB))
                for k in range(DB):
                    act.activation(y_hi[:, k, :], mix[:, k, :], ACT.Copy).then_inc(y_hi_made.sem, 1)

                rows(L, 6)

                def wo_tile(t, turn, j, k):
                    refill(L, t, turn, j)
                    act.activation(wide[:, k, :], ps[:, 2 * (j % 2), 0:T], ACT.Copy).then_inc(wo_ready.sem, 1)
                through(act, "w_o", wo_tile)
                act.wait_ge(wo_ready.sem, wo_ready.at(L, DB))
                act.wait_ge(y_lo_made.sem, y_lo_made.at(L, 4 * DB))
                norm(L, 5, wide[:, :, :], D, mix[:, :, :])
                rows(L, 7)
                act.wait_ge(x_mid.sem, x_mid.at(L, 1))
                norm(L, 6, x[:, :, :], D, mix[:, :, :], (8,))
                rows(L, 9)
                for k in range(DB):
                    act.wait_ge(h_value.sem, h_value.at(L, DB + k + 1))
                    act.activation(h_hi[:, k, :], wide[:, k, :], ACT.Copy).then_inc(h_hi_made.sem, 1)
                for half in range(2):
                    base = half * FF_B

                    def finish(j, k, a, i, half=half, base=base):
                        if a:
                            act.wait_ge(conv_done.sem, conv_done.at(L, k + (XBC_B + base + 1)))
                            act.activation(gate[:, :], conv[:, j % 2, :], ACT.Silu).then_inc(silu_done.sem, 1)
                        else:
                            act.wait_ge(ag_value.sem, ag_value.at(L, i + (half * FF_H + 1)))
                            act.activation(y_hi[:, i, :], gated[:, :], ACT.Copy).then_inc(y_hi_made.sem, 1)

                    def up(t, turn, j, k, a, i, half=half, base=base):
                        refill(L, t, turn, j)
                        first = isinstance(k, int)
                        if a and not (first and k < 2):
                            act.wait_ge(silu_done.sem, silu_done.at(L, i + (XBC_B + DB + half * FF_H)))
                        if not a and not (first and k < 2):
                            act.wait_ge(ag_value.sem, ag_value.at(L, i + half * FF_H))
                        centre(L, j, "ffn_w", "ffn_b", k + base)
                        if not (first and k == 0):
                            finish(j + 1, k - 1, not a, i if not a else i - 1)
                    up_stage(act, half, up)
                    finish(STAGES[f"up{half}"][0] + FF_B - 1, FF_B - 1, False, FF_H - 1)
                    if half == 0:
                        rows(L, 10)
                    t0 = STAGES[f"down{half}"][0]
                    for k in range(FF_H):
                        refill(L, t0 + k, (t0 + k) // RING, (t0 + k) % RING)
                    if half == 0:
                        rows(L, 11)
                act.wait_ge(down_taken.sem, down_taken.at(L, 2))
                norm(L, 7, wide[:, :, :], D, mix[:, :, :])
                act.wait_ge(x_ready.sem, x_ready.at(L, 1))
            assert steps[0] == ACT_LINKS, steps

        @block.vector
        def _(dve):
            steps = [0]

            def link(L, ins):
                steps[0] += 1
                ins.then_inc(dve_chain.sem, 1)
                dve.wait_ge(dve_chain.sem, dve_chain.at(L, steps[0]))

            def split(L, t, turn, j):
                dve.wait_ge(hi_made.sem, hi_made.at(L, t + AHEAD + 1))
                dve.tensor_tensor(w_lo[:, j % AHEAD, :], raw[:, (j + AHEAD) % RING, :],
                                  w_hi[:, j % AHEAD, :].bitcast(F32), ALU.subtract).then_inc(lo_made.sem, 1)

            def lo_part(out, value, hi):
                return dve.tensor_tensor(out, value, hi.bitcast(F32), ALU.subtract)

            def tick_taken():
                after(dve).then_inc(taken.sem, 1)

            def norm(L, n):
                dve.wait_ge(roots.sem, roots.at(L, n))
                link(L, dve.reciprocal(rstd[:, :], root[:, :]))

            def modulate(L, which):
                for k in range(DB):
                    for s, (lo, hi) in enumerate(SEGS):
                        m = dve.tensor_scalar(wide[:, k, lo:hi], wide[:, k, lo:hi], coef[:, 3 * which, k, s:s + 1],
                                              coef[:, 3 * which + 1, k, s:s + 1], ALU.mult, ALU.add)
                    m.then_inc(h_value.sem, 1)
                for k in range(DB):
                    dve.wait_ge(h_hi_made.sem, h_hi_made.at(L, which * DB + k + 1))
                    lo_part(h_lo[:, k, :], wide[:, k, :], h_hi[:, k, :]).then_inc(h_lo_made.sem, 1)

            def vector(L, v):
                which, kind = v // 3, v % 3
                dve.wait_ge(cols_made.sem, cols_made.at(L, v + 1))
                out = coef[:, 3 * which + (1, 0, 2)[kind], :, :]
                m = dve.tensor_tensor(out if kind == 0 else mod[:, :, :],
                                      ps[:, 4, 0:16].rearrange("p (k s) -> p k s", s=2),
                                      spread(param("b_ada", v * DB, DB), 2), ALU.add)
                m.then_inc(cols_taken.sem, 1)
                dve.wait_ge(cols_taken.sem, cols_taken.at(L, v + 1))
                if kind == 1:
                    link(L, dve.scalar_tensor_tensor(
                        out=out, in0=mod[:, :, :], scalar=1.0,
                        in1=spread(param(("g_pre_mix", "g_pre_ffn")[which], 0, DB), 2), op0=ALU.add, op1=ALU.mult))
                elif kind == 2:
                    link(L, dve.tensor_tensor(out, mod[:, :, :],
                                              spread(param(("g_post_mix", "g_post_ffn")[which], 0, DB), 2), ALU.mult))

            def residual(L, which, signal_):
                link(L, dve.tensor_tensor(wide[:, :, :], wide[:, :, :], repeat(rstd[:, :], DB), ALU.mult))
                for k in range(DB):
                    for s, (lo, hi) in enumerate(SEGS):
                        m = dve.scalar_tensor_tensor(out=x[:, k, lo:hi], in0=wide[:, k, lo:hi],
                                                     scalar=coef[:, 3 * which + 2, k, s:s + 1], in1=x[:, k, lo:hi],
                                                     op0=ALU.mult, op1=ALU.add)
                m.then_inc(signal_.sem, 1)

            def taps(L, n, j, w_name, k, last):
                dve.wait_ge(conv_mid.sem, conv_mid.at(L, n + 1))
                bank, buf = ps[:, 2 * (j % 2), :], conv[:, j % 2, :]
                for lo, hi in SEGS:
                    m = dve.scalar_tensor_tensor(out=buf[:, lo + 1:hi], in0=bank[:, lo:hi - 1],
                                                 scalar=param_at(w_name, k, 3, 0), in1=buf[:, lo + 1:hi],
                                                 op0=ALU.mult, op1=ALU.add)
                m.then_inc(conv_left.sem, 1)
                dve.wait_ge(conv_left.sem, conv_left.at(L, n + 1))
                for lo, hi in SEGS:
                    m = dve.scalar_tensor_tensor(out=buf[:, lo:hi - 1], in0=bank[:, lo + 1:hi],
                                                 scalar=param_at(w_name, k, 3, 2), in1=buf[:, lo:hi - 1],
                                                 op0=ALU.mult, op1=ALU.add)
                m.then_inc(conv_done.sem, 1)
                dve.wait_ge(conv_done.sem, conv_done.at(L, n + 1))
                tick_taken()

            dve.wait_ge(loaded, 48)
            dve.memset(cond_pad[:, :, 0:6], 0.0)
            dve.memset(cond_pad[:, :, 8:14], 0.0).then_inc(cond_ready, 1)
            dve.memset(stat[:, 63:64], EPS).then_inc(ready, 1)
            for d in range(2):
                dve.tensor_copy(tri_bf[:, d, :], tri[d])
                dve.tensor_scalar(far_bf[:, d, :], tri[d], 1.0, 1e30, ALU.subtract, ALU.mult)
            dve.tensor_copy(ident_bf[:, :], ident)
            for t in range(AHEAD):
                dve.wait_ge(hi_made.sem, t + 1)
                dve.tensor_tensor(w_lo[:, t, :], raw[:, t, :], w_hi[:, t, :].bitcast(F32), ALU.subtract)\
                   .then_inc(lo_made.sem, 1)
            for _ in range(AHEAD):
                tick_taken()
                after(dve).then_inc(side_used.sem, 1)
            after(dve).then_inc(caches_free.sem, 1)

            with dve.Fori(0, LAYERS) as L:
                dve.wait_ge(params_in.sem, params_in.at(L, 16))
                settle(dve, dve_marks)

                norm(L, 1)
                link(L, dve.tensor_tensor(wide[:, :, :], x[:, :, :], repeat(rstd[:, :], DB), ALU.mult))
                vector(L, 0)
                vector(L, 1)
                modulate(L, 0)

                def conv_tile(t, turn, j, k):
                    split(L, t, turn, j)
                    taps(L, k, j, "conv_w", k, None)
                t0 = STAGES["proj"][0]
                sub_stage(dve, t0, XBC_B, conv_tile)
                t = t0 + XBC_B
                j = t % RING
                split(L, t, t // RING, j)
                dve.wait_ge(misc_copied.sem, misc_copied.at(L, 1))
                bank = ps[:, 2 * (j % 2), :]
                dve.tensor_tensor(gated[64:96, :], bank[32:64, 0:T], rope[32:64, :], ALU.mult).then_inc(kpe_ready.sem, 1)
                dve.tensor_tensor(kpe[64:96, 0:T], bank[64:96, 0:T], rope[64:96, :], ALU.mult).then_inc(kpe_ready.sem, 1)
                dve.wait_ge(kpe_ready.sem, kpe_ready.at(L, 2))
                tick_taken()
                dve.tensor_tensor(kpe[64:96, 0:T], kpe[64:96, 0:T], gated[64:96, :], ALU.add).then_inc(kpe_ready.sem, 1)
                for k in range(KVB + QB):
                    t = t0 + XBC_B + 1 + k
                    j = t % RING
                    split(L, t, t // RING, j)
                    dve.wait_ge(used.sem, used.at(L, t + 1))
                    dve.tensor_copy(low[:, k, :], ps[:, 2 * (j % 2), 0:T]).then_inc(taken.sem, 1)
                norm(L, 2)
                for k in range(KVB):
                    link(L, dve.scalar_tensor_tensor(out=ckv[:, k, 0:T], in0=low[:, k, :], scalar=param("g_kv", k),
                                             in1=rstd[:, :], op0=ALU.mult, op1=ALU.mult))
                after(dve).then_inc(ckv_ready.sem, 1)
                for k in range(KVB):
                    after(dve).then_inc(kvq_value.sem, 1)
                for k in range(KVB):
                    dve.wait_ge(kvq_hi_made.sem, kvq_hi_made.at(L, k + 1))
                    lo_part(ckv_lo[:, k, :], ckv[:, k, :], ckv_hi[:, k, :]).then_inc(kvq_lo_made.sem, 1)
                norm(L, 3)
                for k in range(QB):
                    dve.scalar_tensor_tensor(out=low[:, KVB + k, :], in0=low[:, KVB + k, :], scalar=param("g_q", k),
                                             in1=rstd[:, :], op0=ALU.mult, op1=ALU.mult).then_inc(kvq_value.sem, 1)
                for k in range(QB):
                    dve.wait_ge(kvq_hi_made.sem, kvq_hi_made.at(L, KVB + k + 1))
                    lo_part(q_lo[:, k, :], low[:, KVB + k, :], q_hi[:, k, :]).then_inc(kvq_lo_made.sem, 1)
                ssd_dve(L, dve, link)

                def z_tile(t, turn, j, k):
                    split(L, t, turn, j)
                    dve.wait_ge(silu_done.sem, silu_done.at(L, XBC_B + k + 1))
                    dve.tensor_tensor(wide[:, k, :], wide[:, k, :], conv[:, j % 2, :], ALU.mult).then_inc(y_value.sem, 1)
                    tick_taken()
                through(dve, "z", z_tile)
                norm(L, 4)
                for k in range(DB):
                    dve.scalar_tensor_tensor(out=wide[:, k, :], in0=wide[:, k, :], scalar=param("g_ssd", k),
                                             in1=rstd[:, :], op0=ALU.mult, op1=ALU.mult).then_inc(y_value.sem, 1)
                y_los(L, 0, lambda k: wide[:, k, :])
                merge(L, "out_ssd", 0)
                vector(L, 2)

                attention_dve(L, dve, link, split, tick_taken, 0)
                attention_dve(L, dve, link, split, tick_taken, 1)
                merge(L, "out_mla", 1)
                through(dve, "f", lambda t, turn, j, k: (split(L, t, turn, j),
                                                        dve.wait_ge(f_ready.sem, f_ready.at(L, k + 1)),
                                                        tick_taken()))
                y_los(L, 2, lambda k: ps[:, 4 + k % 4, 0:T])
                merge(L, "out_fft", 2)
                y_los(L, 3, lambda k: mix[:, k, :])
                through(dve, "w_o", lambda t, turn, j, k: (split(L, t, turn, j),
                                                          dve.wait_ge(wo_ready.sem, wo_ready.at(L, k + 1)),
                                                          tick_taken()))
                norm(L, 5)
                residual(L, 0, x_mid)
                dve.wait_ge(x_mid.sem, x_mid.at(L, 1))
                vector(L, 3)
                norm(L, 6)
                link(L, dve.tensor_tensor(wide[:, :, :], x[:, :, :], repeat(rstd[:, :], DB), ALU.mult))
                vector(L, 4)
                modulate(L, 1)

                for half in range(2):
                    def ag_lo(i, half=half):
                        dve.wait_ge(y_hi_made.sem, y_hi_made.at(L, i + (4 * DB + half * FF_H + 1)))
                        lo_part(y_lo[:, i, :], gated[:, :], y_hi[:, i, :]).then_inc(y_lo_made.sem, 1)

                    def up(t, turn, j, k, a, i, half=half):
                        split(L, t, turn, j)
                        taps(L, k + (XBC_B + half * FF_B), j, "ffn_w", k + half * FF_B, None)
                        if a:
                            if not (isinstance(i, int) and i == 0):
                                ag_lo(i - 1)
                        else:
                            if not (isinstance(i, int) and i == 0):
                                dve.wait_ge(y_lo_made.sem, y_lo_made.at(L, i + (4 * DB + half * FF_H)))
                            dve.wait_ge(silu_done.sem, silu_done.at(L, i + (XBC_B + DB + half * FF_H + 1)))
                            dve.tensor_tensor(gated[:, :], gate[:, :], conv[:, j % 2, :], ALU.mult)\
                               .then_inc(ag_value.sem, 1)
                    up_stage(dve, half, up)
                    ag_lo(FF_H - 1)
                    if half:
                        vector(L, 5)
                    t0 = STAGES[f"down{half}"][0]
                    for k in range(FF_H):
                        split(L, t0 + k, (t0 + k) // RING, (t0 + k) % RING)
                        tick_taken()
                    dve.wait_ge(down_made.sem, down_made.at(L, half + 1))
                    if half == 0:
                        dve.tensor_copy(wide[:, :, :], ps[:, :, 0:T]).then_inc(down_taken.sem, 1)
                        dve.wait_ge(down_taken.sem, down_taken.at(L, 1))
                    else:
                        dve.tensor_tensor(wide[:, :, :], wide[:, :, :], ps[:, :, 0:T], ALU.add)\
                           .then_inc(down_taken.sem, 1)
                norm(L, 7)
                residual(L, 1, x_ready)
                dve.wait_ge(x_ready.sem, x_ready.at(L, 1))
                after(dve).then_inc(caches_free.sem, 1)
            assert steps[0] == DVE_LINKS, steps


def dft(n, scale):
    i = np.arange(n)
    angle = 2 * np.pi * ((i[:, None] * i[None, :]) % n) / n
    return np.cos(angle) * scale, np.sin(angle) * scale


def rope_swap():
    q = ROPE // 4
    i = np.arange(ROPE)
    second = (i // q) % 2 == 1
    return np.where(second, i - q, i + q), np.where(second, 1.0, -1.0)


def constant_tables():
    out = np.zeros((P, N_CONSTS), np.float32)

    def put(name, value):
        at, n = CONSTS[name]
        out[:, at:at + n] = np.asarray(value, np.float64).reshape(P, n)
    i = np.arange(P)
    put("ident", np.eye(P))
    put("tri", np.concatenate([i[:, None] <= i[None, :], i[:, None] >= i[None, :]], 1))
    put("ones", np.ones((P, P)))
    c, s = dft(GROUP_W, GROUP_W ** -0.5)
    put("dft_ch", np.concatenate([c, s], 1).reshape(2, P, 512).transpose(1, 0, 2))
    c, s = dft(LAT, LAT ** -0.5)
    put("dft_lat", np.stack([c, -s], 1).reshape(2, P, 2, LAT).transpose(1, 0, 2, 3))
    c, s = dft(CTX, CTX ** -0.5)
    put("dft_ctx", np.stack([c, -s], 1))
    quarter = ROPE // 4
    inv = (10000.0 ** (-np.arange(quarter, dtype=np.float32) / quarter)).astype(np.float32)
    t = np.arange(LAT)
    pos = np.stack([t // 64, t % 64]).astype(np.float32)
    f = np.arange(ROPE)
    angle = (pos[f // (2 * quarter)] * inv[f % quarter][:, None]).astype(np.float32).astype(np.float64)
    _, sign = rope_swap()
    table = np.zeros((P, T))
    cos = np.concatenate([np.ones((ROPE, CTX)), np.cos(angle)], 1)
    sin = np.concatenate([np.zeros((ROPE, CTX)), np.sin(angle) * sign[:, None]], 1)
    table[32:64], table[64:96], table[96:128] = sin, cos, sin
    put("rope", table)
    return out


def pack_weights(w):
    tiles = np.zeros((LAYERS * TILES, P, 1024), np.float32)
    swap, _ = rope_swap()
    o_xbc, o_dt, o_q, o_kv, o_f = 1024, 1024 + 1536, 1024 + 1536 + 32, 1024 + 1536 + 32 + QL, \
        1024 + 1536 + 32 + QL + KVL + ROPE
    for layer in range(LAYERS):
        w_in, w_gate, w_up = w["w_in"][layer], w["w_gate"][layer], w["w_up"][layer]

        def put(stage, k, m):
            tile = tiles[layer * TILES + STAGES[stage][0] + k]
            m = m.transpose(1, 0, 2).reshape(P, -1)
            tile[:, :m.shape[1]] = m

        def cols(matrix, at, n=P):
            return matrix[:, at:at + n].reshape(-1, P, n)
        for k in range(XBC_B):
            put("proj", k, cols(w_in, o_xbc + k * P))
        pe = w_in[:, o_kv + KVL:o_kv + KVL + ROPE]
        put("proj", XBC_B, np.concatenate([w_in[:, o_dt:o_dt + 32], pe[:, swap], pe, pe], 1).reshape(-1, P, P))
        for k in range(KVB):
            put("proj", XBC_B + 1 + k, cols(w_in, o_kv + k * P))
        for k in range(QB):
            put("proj", XBC_B + 1 + KVB + k, cols(w_in, o_q + k * P))
        for k in range(DB):
            put("z", k, cols(w_in, k * P))
            put("f", k, cols(w_in, o_f + k * P))
            put("w_o", k, cols(w["w_o"][layer], k * P))
            for b, name in enumerate(("ssd", "mla", "fft")):
                put(f"out_{name}", 2 * k, cols(w_gate, b * D + k * P))
                put(f"out_{name}", 2 * k + 1, cols(w[f"w_{name}_out"][layer], k * P))
        q_up = w["w_q_up"][layer].reshape(QB, P, HEADS, HD + ROPE)
        q_up = np.concatenate([q_up, q_up[..., HD:][..., swap]], 3)
        kv_up = w["w_kv_up"][layer].reshape(KVB, P, HEADS, 2 * HD)
        for half in range(2):
            for i in range(4):
                h = half * HALF + 2 * i
                put(f"heads{half}", i, q_up[:, :, h:h + 2].transpose(2, 0, 1, 3).reshape(2 * QB, P, P))
            for i in range(2):
                h = half * HALF + 4 * i
                k_part = kv_up[:, :, h:h + 4, :HD].reshape(KVB, P, 2, 2 * HD).transpose(2, 0, 1, 3)
                put(f"heads{half}", 4 + i, k_part.reshape(2 * KVB, P, P))
                put(f"heads{half}", 6 + i, kv_up[:, :, h:h + 4, HD:].reshape(KVB, P, 4 * HD))
            for i in range(FF_H):
                b = half * FF_H + i
                put(f"up{half}", 2 * i, cols(w_up, b * P))
                put(f"up{half}", 2 * i + 1, cols(w_up, (FF_B + b) * P))
                put(f"down{half}", i, w["w_down"][layer][b * P:(b + 1) * P].reshape(1, P, D))
    return tiles


def pack_ada(w):
    m = w["w_ada"].reshape(LAYERS, DB, P, SIDE, SIDE_TILES, P)
    return m.transpose(0, 3, 2, 4, 1, 5).reshape(LAYERS, SIDE, P, SIDE_TILES * 1024)


def pack_params(w):
    out = np.zeros((LAYERS, P, N_PARAMS), np.float32)

    def put(name, value):
        at, n = PARAMS[name]
        out[:, :, at:at + n] = value.transpose(1, 0, 2)

    def columns(v):
        return v.reshape(LAYERS, -1, P).transpose(2, 0, 1)
    for name in ("b_ada", "g_pre_mix", "g_post_mix", "g_pre_ffn", "g_post_ffn", "b_gate"):
        put(name, columns(w[name]))
    put("g_ssd", columns(w["g_ssd_norm"]))
    put("g_q", columns(w["g_q_norm"]))
    put("g_kv", columns(w["g_kv_norm"]))
    put("conv_b", columns(w["conv_ssd_b"]))
    put("conv_w", w["conv_ssd_w"].reshape(LAYERS, 3, XBC_B, P).transpose(3, 0, 2, 1).reshape(P, LAYERS, -1))
    put("ffn_b", w["conv_ffn_b"].reshape(LAYERS, 2, FF_B, P).transpose(3, 0, 2, 1).reshape(P, LAYERS, -1))
    put("ffn_w", w["conv_ffn_w"].reshape(LAYERS, 3, 2, FF_B, P).transpose(4, 0, 3, 2, 1).reshape(P, LAYERS, -1))
    put("d_skip", columns(np.repeat(w["d_skip"], HD, axis=1)))
    put("dt_bias", np.broadcast_to(w["dt_bias"].reshape(1, LAYERS, 32), (P, LAYERS, 32)))
    put("a_log", np.broadcast_to(w["a_log"].reshape(1, LAYERS, 32), (P, LAYERS, 32)))
    return out


def feature_major(v):
    return v.reshape(v.shape[0], -1, P).transpose(2, 1, 0)


def kernel(**inputs):
    import concourse.bacc as bacc
    from concourse.bass_utils import run_bass_kernel_spmd

    w = {k: np.ascontiguousarray(v) for k, v in inputs.items()}
    arrays = {
        "in_x": feature_major(np.concatenate([w["x_prompt"][0], w["x_sample"][0]], 0)),
        "in_cond": feature_major(np.stack([w["c_ctx"], w["c"][0]])),
        "in_state": w["state_ssm"][0].transpose(0, 4, 1, 2, 3).reshape(LAYERS, STATE, 2, D),
        "in_ckv": w["cache_ckv"][0].reshape(LAYERS, PAST, KVB, P).transpose(0, 3, 2, 1),
        "in_kpe": w["cache_kpe"][0].transpose(0, 2, 1),
        "in_params": pack_params(w),
        "in_consts": constant_tables(),
        "in_weights": pack_weights(w),
        "in_ada": pack_ada(w),
    }
    arrays = {k: np.ascontiguousarray(v) for k, v in arrays.items()}
    outs = {
        "out_x": (P, DB, T),
        "out_ckv": (LAYERS, P, KVB, CTX),
        "out_kpe": (LAYERS, ROPE, CTX),
        "out_state": (LAYERS, 2, STATE, D),
    }
    nc = bacc.Bacc("TRN2", target_bir_lowering=False, num_devices=1)
    args = [nc.dram_tensor(k, v.shape, F32, kind="ExternalInput").ap() for k, v in arrays.items()]
    args += [nc.dram_tensor(k, s, F32, kind="ExternalOutput").ap() for k, s in outs.items()]
    build_program(nc, *args)
    r = run_bass_kernel_spmd(nc, [arrays], core_ids=[0]).results[0]
    y = r["out_x"].transpose(2, 1, 0).reshape(T, D)
    return (
        y[None, :CTX], y[None, CTX:],
        r["out_ckv"].transpose(0, 3, 2, 1).reshape(1, LAYERS, CTX, KVL),
        r["out_kpe"].transpose(0, 2, 1)[None],
        r["out_state"].reshape(LAYERS, 2, STATE, HEADS, HD).transpose(0, 1, 3, 4, 2)[None],
    )
```

```python
from contextlib import ExitStack

import numpy as np

import concourse.bass as bass
from concourse import mybir

F32 = mybir.dt.float32
F32R = mybir.dt.float32r
BF16 = mybir.dt.bfloat16
ALU = mybir.AluOpType
ACT = mybir.ActivationFunctionType
AX = mybir.AxisListType

P = 128
LAYERS = 2
CTX, LAT, PAST = 128, 256, 128
T = CTX + LAT
KEYS = T + PAST
D = 1024
DB = D // P
HEADS = 16
HALF = HEADS // 2
HD = 64
STATE = 128
ROPE = 32
QL, KVL = 384, 256
QB, KVB = QL // P, KVL // P
XBC_B = 12
FF_B = 22
FF_H = FF_B // 2
GROUP_W = 256
GROUPS = 4
EPS = 1e-6
ATTN_SCALE = float((HD + ROPE) ** -0.5)
SEGS = ((0, CTX), (CTX, T))
CHUNKS = T // P
PROB = 3 * LAT + CTX

RING = 4
AHEAD = 2
STAGES = {}
TILES = 0
for _name, _count in (("proj", 18), ("z", 8), ("out_ssd", 16), ("heads0", 8), ("heads1", 8),
                      ("out_mla", 16), ("f", 8), ("out_fft", 16), ("w_o", 8),
                      ("up0", 22), ("down0", 11), ("up1", 22), ("down1", 11)):
    STAGES[_name] = (TILES, _count)
    TILES += _count
TURNS = TILES // RING
assert TILES % RING == 0

SIDE = 12
SIDE_TILES = 4
SIDE_ARRIVED = [16, 16, 32, 32, 64, 64, 80, 80, 96, 96, 112, 112]

PARAMS = {}
N_PARAMS = 0
for _name, _count in (("b_ada", 48), ("g_pre_mix", 8), ("g_post_mix", 8), ("g_pre_ffn", 8), ("g_post_ffn", 8),
                      ("b_gate", 24), ("conv_w", 36), ("conv_b", 12), ("ffn_w", 132), ("ffn_b", 44),
                      ("d_skip", 8), ("g_ssd", 8), ("g_q", 3), ("g_kv", 2), ("dt_bias", 32), ("a_log", 32)):
    PARAMS[_name] = (N_PARAMS, _count)
    N_PARAMS += _count

CONSTS = {}
N_CONSTS = 0
for _name, _count in (("ident", 128), ("tri", 256), ("ones", 128), ("rope", T), ("dft_ch", 2 * 512),
                      ("dft_lat", 2 * 2 * 256), ("dft_ctx", 2 * 128)):
    CONSTS[_name] = (N_CONSTS, _count)
    N_CONSTS += _count
N_KEPT = CONSTS["dft_ch"][0]
N_DFT = N_CONSTS - N_KEPT


class Signal:

    def __init__(self, sem, per_layer):
        self.sem, self.per_layer = sem, per_layer

    def at(self, layer, n):
        return layer * self.per_layer + n


NORM_BLOCKS = (DB, KVB, QB, DB, DB, DB, DB)
DOWN_ORDER = (7, 0, 1, 2, 3, 4, 5, 6)

DVE_LINKS = 57


def build_program(nc, a_x, a_cond, a_state, a_ckv, a_kpe, a_params, a_consts, a_weights, a_ada,
                  o_x, o_ckv, o_kpe, o_state):
    ctx = ExitStack()
    with ctx:
        def sb(name, shape, dt=F32):
            return ctx.enter_context(nc.sbuf_tensor(name, shape, dt))

        def sem(name):
            return ctx.enter_context(nc.semaphore(name))

        def signal(name, per_layer):
            return Signal(sem(name), per_layer)

        consts = sb("consts", [P, N_KEPT])
        params = sb("params", [P, N_PARAMS])
        raw = sb("raw", [P, RING, 1024])
        w_hi = sb("w_hi", [P, AHEAD, 1024], F32R)
        w_lo = sb("w_lo", [P, AHEAD, 1024], F32R)
        x = sb("x", [P, DB, T])
        cond = sb("cond", [P, DB, 2])
        cond_pad = sb("cond_pad", [P, DB, 14])
        mod = sb("mod", [P, DB, 2])
        coef = sb("coef", [P, 6, DB, 2])
        h_hi = sb("h_hi", [P, DB, T], F32R)
        h_lo = sb("h_lo", [P, DB, T], F32R)
        in_hi = sb("in_hi", [P, DB * T + KVB * KEYS + QB * T], F32R)
        in_lo = sb("in_lo", [P, DB * T + KVB * KEYS + QB * T], F32R)
        y_hi, y_lo = (v[:, 0:FF_H * T].rearrange("p (k n) -> p k n", k=FF_H) for v in (in_hi, in_lo))
        kvq_hi, kvq_lo = (v[:, DB * T:] for v in (in_hi, in_lo))
        wide = sb("wide", [P, DB, T])
        mix = sb("mix", [P, DB, T])
        root = sb("root", [P, T])
        rstd = sb("rstd", [P, T])
        conv = sb("conv", [P, AHEAD, T])
        gate = sb("gate", [P, T])
        gated = sb("gated", [P, T])
        kpe = sb("kpe", [96, KEYS])
        low = mix[:, 0:KVB + QB, :]
        ckv = sb("ckv", [P, KVB, KEYS])
        stat = sb("stat", [P, 64])
        region = sb("region", [P, 12 * 1024])

        def view(at, shape):
            n = int(np.prod(shape))
            v = region[:, at:at + n]
            names = [chr(97 + i) for i in range(len(shape))]
            if len(shape) == 1:
                return v
            return v.rearrange(f"p ({' '.join(names)}) -> p {' '.join(names)}",
                               **dict(zip(names[1:], shape[1:])))

        tok_major = "p k n -> p (k n)"
        side_slot = [view(0, [SIDE_TILES, 1024]), view(4096, [SIDE_TILES, 1024])]
        mod_rows = region[0:8, 12032:12032 + 2 * P].rearrange("p (i n) -> p i n", i=2)
        side_three = {4: wide[:, :, :].rearrange(tok_major), 5: view(0, [3 * 1024])}
        side_last = view(11008, [1024])
        xbc = view(0, [XBC_B, T])
        b_tok = view(4608, [CHUNKS, 256])
        cb = view(5376, [CHUNKS * 2, P])
        kpe_raw = region[:, 6144:6144 + CTX]
        xdt = view(6912, [2, D])
        decay = view(8960, [2 * HALF, P])
        h_state = view(8960, [2, D])
        x_end = view(6912, [2, D])
        off_tok = view(6912, [2, D])
        xs_tok = mix[:, :, :].rearrange(tok_major).rearrange("p (c n) -> p c n", c=CHUNKS)
        wide_tok = wide[:, :, :].rearrange(tok_major).rearrange("p (c n) -> p c n", c=CHUNKS)
        ctx_states = wide_tok
        scaled = wide_tok[:, 2, :]
        q_t = view(0, [HALF, T])
        k_t = view(3072, [HALF, KEYS])
        v_tok = view(7168, [4, HALF // 2, 3, HD])
        prob_t = view(10240, [2, PROB])
        rot = conv
        f_ch = view(0, [CHUNKS, GROUPS, 512])
        dft = view(12288 - N_DFT, [N_DFT])

        dts = sb("dts", [P, 9, CHUNKS * 32])
        dta_parts = sb("dta_parts", [P, 3, CHUNKS * 32], BF16)
        tri_bf = sb("tri_bf", [P, 2, P], BF16)
        far_bf = sb("far_bf", [P, 2, P], BF16)
        ident_bf = sb("ident_bf", [P, P], BF16)
        dt_t = gated[0:32, :]

        ps = ctx.enter_context(nc.psum_tensor("ps", [P, 8, 512], F32))
        flat = ps[:, :, :].rearrange("p b n -> p (b n)")
        acum_ps = ps[:, 6, 96:96 + 192]

        def const(name):
            at, n = CONSTS[name]
            return consts[:, at:at + n] if at < N_KEPT else dft[:, at - N_KEPT:at - N_KEPT + n]

        def param(name, i=0, n=1):
            at = PARAMS[name][0]
            return params[:, at + i:at + i + n]

        ident = const("ident")
        ones = const("ones")
        tri = [const("tri")[:, 0:P], const("tri")[:, P:2 * P]]
        dft_ch = const("dft_ch").rearrange("p (k n) -> p k n", k=2)
        dft_lat = const("dft_lat").rearrange("p (k s n) -> p k s n", k=2, s=2)
        dft_ctx = const("dft_ctx").rearrange("p (s n) -> p s n", s=2)
        rope = const("rope")
        ckv_hi = kvq_hi[:, 0:KVB * KEYS].rearrange("p (k n) -> p k n", k=KVB)
        ckv_lo = kvq_lo[:, 0:KVB * KEYS].rearrange("p (k n) -> p k n", k=KVB)
        q_hi = kvq_hi[:, KVB * KEYS:].rearrange("p (k n) -> p k n", k=QB)
        q_lo = kvq_lo[:, KVB * KEYS:].rearrange("p (k n) -> p k n", k=QB)

        loaded = sem("loaded")
        stored = sem("stored")
        arrived = [Signal(sem(f"arrived{j}"), 16 * TURNS) for j in range(RING)]
        hi_made = signal("hi_made", TILES)
        lo_made = signal("lo_made", TILES)
        used = signal("used", TILES)
        taken = signal("taken", TILES)
        ready = sem("ready")
        cond_ready = sem("cond_ready")
        pool_marks, pe_marks, dve_marks = sem("pool_marks"), sem("pe_marks"), sem("dve_marks")
        squares = signal("squares", sum(NORM_BLOCKS))
        added = signal("added", 2 * (DB - 1))
        sums = signal("sums", 7)
        roots = signal("roots", 7)
        side_in = [Signal(sem(f"side_in{i}"), 112) for i in range(2)]
        side_used = signal("side_used", SIDE)
        rows_out = signal("rows_out", SIDE)
        cols_made = signal("cols_made", SIDE // 2)
        cols_taken = signal("cols_taken", SIDE // 2)
        cols_used = signal("cols_used", 2)
        scaled_by = signal("scaled_by", 4 * DB)
        h_value = signal("h_value", 2 * DB)
        h_latent = signal("h_latent", 2 * DB)
        h_hi_made = signal("h_hi_made", 2 * DB)
        h_lo_made = signal("h_lo_made", 2 * DB)
        kvq_value = signal("kvq_value", 5)
        kvq_hi_made = signal("kvq_hi_made", 5)
        kvq_lo_made = signal("kvq_lo_made", 5)
        y_value = signal("y_value", 2 * DB)
        y_hi_made = signal("y_hi_made", 4 * DB + FF_B)
        y_lo_made = signal("y_lo_made", 4 * DB + FF_B)
        conv_mid = signal("conv_mid", XBC_B + 2 * FF_B)
        conv_left = signal("conv_left", XBC_B + 2 * FF_B)
        conv_done = signal("conv_done", XBC_B + 2 * FF_B)
        silu_done = signal("silu_done", XBC_B + FF_B + DB)
        ag_value = signal("ag_value", FF_B)
        misc_copied = signal("misc_copied", 1)
        cache_in = signal("cache_in", 32)
        params_in = signal("params_in", 16)
        caches_free = signal("caches_free", 1)
        kpe_ready = signal("kpe_ready", 3)
        kpe_spread = signal("kpe_spread", 3)
        ckv_ready = signal("ckv_ready", 1)
        transposed = signal("transposed", CHUNKS)
        tok_ready = signal("tok_ready", CHUNKS)
        dt_turned = signal("dt_turned", 1)
        dt_in = signal("dt_in", 1)
        dt_ready = signal("dt_ready", 1)
        acum_sums = signal("acum_sums", 1)
        cb_made = signal("cb_made", 1)
        xdt_ready = signal("xdt_ready", 4 * CHUNKS)
        rows_made = signal("rows_made", 4 * CHUNKS)
        decay_ready = signal("decay_ready", 4 * CHUNKS)
        weighted = signal("weighted", 4 * CHUNKS)
        y_diag = signal("y_diag", 4 * CHUNKS)
        y_added = signal("y_added", 2 * CHUNKS)
        state_in = signal("state_in", 16)
        ends_ready = signal("ends_ready", 4)
        states_made = signal("states_made", 4)
        new_state = signal("new_state", 2)
        state_out = signal("state_out", 32)
        state_next = signal("state_next", 2)
        off_made = signal("off_made", 4)
        off_ready = signal("off_ready", 4)
        off_turned = signal("off_turned", 2)
        off_back = signal("off_back", 2)
        gate_made = signal("gate_made", 3 * DB)
        q_plain = signal("q_plain", HALF)
        q_rot = signal("q_rot", 3 * HALF)
        k_even = signal("k_even", 4)
        k_odd = signal("k_odd", 4)
        v_ready = signal("v_ready", 4)
        scored = signal("scored", HEADS)
        maxed = signal("maxed", HEADS)
        max_turned = signal("max_turned", HEADS)
        max_in = signal("max_in", HEADS)
        scored_t = signal("scored_t", HEADS)
        exped = signal("exped", HEADS)
        o_made = signal("o_made", HEADS)
        o_ready = signal("o_ready", HEADS)
        dft_in = signal("dft_in", 16)
        f_ready = signal("f_ready", DB)
        ch_made = signal("ch_made", CHUNKS * GROUPS)
        ch_taken = signal("ch_taken", CHUNKS * GROUPS)
        pos_made = signal("pos_made", DB)
        wo_ready = signal("wo_ready", DB)
        down_made = signal("down_made", 2)
        down_taken = signal("down_taken", 1 + DB)
        down_taken_act = signal("down_taken_act", 1)
        x_ready = signal("x_ready", DB)
        x_mid = signal("x_mid", DB)
        dt_abs = signal("dt_abs", 1)
        dt_exp = signal("dt_exp", 2)
        to_end = signal("to_end", 1)
        mixed = signal("mixed", 1 + 2 * DB)
        dve_chain = signal("dve_chain", DVE_LINKS)

        def through(eng, stage, body):
            t, count = STAGES[stage]
            first, end = t, t + count
            while t % RING and t < end:
                body(t, t // RING, t % RING, t - first)
                t += 1
            turns = (end - t) // RING
            if turns > 1:
                with eng.Fori(0, turns) as r:
                    for j in range(RING):
                        body(r * RING + (t + j), r + t // RING, j, r * RING + (t + j - first))
                t += turns * RING
            while t < end:
                body(t, t // RING, t % RING, t - first)
                t += 1

        def anew(eng, L):
            number = eng.alloc_register()
            eng.reg_mov(number, L)
            return eng.snap(number, min_val=0, max_val=LAYERS - 1)

        def tile_bank(j, banks=2):
            return j % 4 if banks == 4 else 2 * (j % 2)

        def squares_at(L, n, i):
            return squares.at(L, sum(NORM_BLOCKS[:n - 1]) + i)

        def settle(eng, mark):
            eng.sem_inc(mark, 1)

        def after(dve):
            settle(dve, dve_marks)
            return dve.engine_nop()

        def spread(ap, n):
            return ap.unsqueeze(2).broadcast_to([ap.shape[0], ap.shape[1], n])

        def repeat(ap, n):
            return ap.unsqueeze(1).broadcast_to([ap.shape[0], n, ap.shape[1]])

        def dt_turn(pe, L):
            pe.wait_ge(misc_copied.sem, misc_copied.at(L, 1))
            settle(pe, pe_marks)
            for c in range(CHUNKS):
                m = pe.transpose(ps[:, 6, c * 32:(c + 1) * 32], dt_t[:, c * P:(c + 1) * P], ident[0:32, 0:32])
            m.then_inc(dt_turned.sem, 1)

        def cumulate(pe, L):
            pe.wait_ge(dt_ready.sem, dt_ready.at(L, 1))
            dta = dts[:, 1, :].rearrange("p (c d h) -> p c d h", c=CHUNKS, d=2)
            for d in range(2):
                pe.matmul(acum_ps[:, d * 48:(d + 1) * 48], tri[d], dta[:, :, d, :], start=True, stop=True)
            pe.matmul(acum_ps[:, 96:192], ones, dts[:, 1, :], start=True, stop=True).then_inc(acum_sums.sem, 1)

        TOKEN_ORDER = [(2, 0), (0, 3), (1, 0)]

        def ssd(pe, L):
            for n, (c, at) in enumerate(TOKEN_ORDER):
                at *= 512
                if n == 2:
                    cumulate(pe, L)
                    pe.wait_ge(tok_ready.sem, tok_ready.at(L, 1))
                if n == 1:
                    pe.wait_ge(rows_out.sem, rows_out.at(L, 5))
                cols = slice(c * P, (c + 1) * P)
                for b in range(10):
                    m = pe.transpose(flat[:, at + b * P:at + (b + 1) * P], xbc[:, b, cols], ident)
                    if b == 9:
                        m.then_inc(transposed.sem, 1)
            pe.wait_ge(dt_exp.sem, dt_exp.at(L, 2))
            for c in range(CHUNKS):
                cols = slice(c * P, (c + 1) * P)
                for g in range(2):
                    m = pe.matmul(flat[:, 6 * 512 + (2 * c + g) * P:6 * 512 + (2 * c + g + 1) * P],
                                  xbc[:, 8 + g, cols], xbc[:, 10 + g, cols], start=True, stop=True)
            m.then_inc(cb_made.sem, 1)
            pe.wait_ge(tok_ready.sem, tok_ready.at(L, CHUNKS))

            def state(n):
                d, c = STATES[n]
                pe.wait_ge(ends_ready.sem, ends_ready.at(L, n + 1))
                if n >= 2:
                    pe.wait_ge(new_state.sem, new_state.at(L, n - 1))
                for g in range(2):
                    m = pe.matmul(ps[:, 2 * (n % 2) + g, :], b_tok[:, c, g * P:(g + 1) * P],
                                  x_end[:, n % 2, g * 512:(g + 1) * 512], start=True, stop=True)
                m.then_inc(states_made.sem, 1)

            def entering(n):
                d, c = ENTERING[n]
                if n < 2:
                    pe.wait_ge(state_in.sem, state_in.at(L, 16))
                else:
                    pe.wait_ge(state_next.sem, state_next.at(L, n - 1))
                    pe.wait_ge(off_ready.sem, off_ready.at(L, n - 1))
                for g in range(2):
                    m = pe.matmul(ps[:, 4 + 2 * (n % 2) + g, :], xbc[:, 10 + g, c * P:(c + 1) * P],
                                  h_state[:, d, g * 512:(g + 1) * 512], start=True, stop=True)
                m.then_inc(off_made.sem, 1)
            for n in range(4):
                state(n)
            for n in range(4):
                entering(n)
            def rows(u):
                c, g, d = UNITS[u]
                if u >= 2:
                    pe.wait_ge(decay_ready.sem, decay_ready.at(L, u - 1))
                for h in range(HALF):
                    bank = ps[:, 4 + 2 * (u % 2) + h // 4, :]
                    if h % 4 == 0:
                        pe.matmul(bank, ident_bf[:, :], repeat(far_bf[:, d, :], 4), start=True, stop=False)
                    at = c * 32 + d * 16 + g * HALF + h
                    for i in range(3):
                        m = pe.matmul(bank[:, h % 4 * P:(h % 4 + 1) * P],
                                      dta_parts[:, i, at:at + 1].broadcast_to([P, P]), tri_bf[:, d, :],
                                      start=False, stop=(h % 4 == 3 and i == 2))
                m.then_inc(rows_made.sem, 1)

            pe.wait_ge(off_ready.sem, off_ready.at(L, 3))
            rows(0)
            pe.wait_ge(off_ready.sem, off_ready.at(L, 4))
            for c in range(2):
                for b in range(DB):
                    m = pe.transpose(ps[:, 2 * c + b // 4, b % 4 * P:(b % 4 + 1) * P], off_tok[:, c, b * P:(b + 1) * P],
                                     ident)
                m.then_inc(off_turned.sem, 1)
            for u, (c, g, d) in enumerate(UNITS):
                if u + 1 < len(UNITS):
                    rows(u + 1)
                if u == 0:
                    pe.wait_ge(off_back.sem, off_back.at(L, 2))
                if d == 0 and u >= 8:
                    pe.wait_ge(y_added.sem, y_added.at(L, u // 2 - 3))
                pe.wait_ge(xdt_ready.sem, xdt_ready.at(L, u + 1))
                pe.wait_ge(weighted.sem, weighted.at(L, u + 1))
                for h in range(HALF):
                    half = h % 2 * HD
                    m = pe.matmul(ps[half:half + HD, (u // 2) % 4, h // 2 * P:(h // 2 + 1) * P],
                                  xdt[:, d, (g * HALF + h) * HD:(g * HALF + h + 1) * HD], decay[:, u % 2 * HALF + h, :],
                                  start=(d == 0 and h < 2), stop=(d == 1), skip_group_check=True)
                m.then_inc(y_diag.sem, 1)

        def attention(pe, L, half, product, weights, tile_in):
            t0 = STAGES[f"heads{half}"][0]
            for i in range(4):
                t = t0 + i
                tile_in(L, t)
                if half == 0 and i == 0:
                    pe.wait_ge(kvq_lo_made.sem, kvq_lo_made.at(L, 5))
                for hh in range(2):
                    m = product(ps[:, 2 * (t % AHEAD) + hh, 0:T],
                                [(*weights(t, hh * QB + kk), q_hi[:, kk, :], q_lo[:, kk, :]) for kk in range(QB)])
                m.then_inc(used.sem, 1)
            for i in range(2):
                t = t0 + 4 + i
                tile_in(L, t)
                for b in range(2):
                    m = product(ps[:, 2 * (t % AHEAD) + b, :],
                                [(*weights(t, b * KVB + kk), ckv_hi[:, kk, :], ckv_lo[:, kk, :]) for kk in range(KVB)])
                m.then_inc(used.sem, 1)
            for i in range(2):
                t = t0 + 6 + i
                tile_in(L, t)
                for s in range(KEYS // P):
                    cols = slice(s * P, (s + 1) * P)
                    parts = []
                    for kk in range(KVB):
                        wh, wl = weights(t, 0, n=256, at=kk * 256)
                        parts.append((ckv_hi[:, kk, cols], ckv_lo[:, kk, cols], wh, wl))
                    m = product(ps[:, 2 * (t % AHEAD) + s // 2, (s % 2) * 256:(s % 2 + 1) * 256], parts)
                m.then_inc(used.sem, 1)
            pe.wait_ge(taken.sem, taken.at(L, t0 + 8 + AHEAD))
            pe.wait_ge(v_ready.sem, v_ready.at(L, 2 * half + 2))
            pe.wait_ge(kpe_spread.sem, kpe_spread.at(L, 3))
            pe.wait_ge(q_rot.sem, q_rot.at(L, 12 * (half + 1)))

            base = half * HALF

            def scores(h):
                if h:
                    pe.wait_ge(maxed.sem, maxed.at(L, base + h))
                for qt in range(CHUNKS):
                    keys, at = (slice(0, CTX), 0) if qt == 0 else (slice(CTX, KEYS), CTX + (qt - 1) * T)
                    m = pe.matmul(flat[:, at:at + keys.stop - keys.start], q_t[0:96, h, qt * P:(qt + 1) * P],
                                  k_t[0:96, h, keys], start=True, stop=True)
                m.then_inc(scored.sem, 1)

            def maxima(h):
                pe.wait_ge(maxed.sem, maxed.at(L, base + h + 1))
                for qt in range(CHUNKS):
                    m = pe.matmul(ps[96:97, 6, qt * P:(qt + 1) * P], stat[:, 3 * (h % 2) + qt:3 * (h % 2) + qt + 1], ident,
                                  start=True, stop=True)
                m.then_inc(max_turned.sem, 1)

            def scores_t(h):
                pe.wait_ge(max_in.sem, max_in.at(L, base + h + 1))
                if h:
                    pe.wait_ge(exped.sem, exped.at(L, base + h))
                for i in range(4):
                    keys, queries = (i + 1, slice(CTX, T)) if i < 3 else (0, slice(0, CTX))
                    at = 1024 + i * LAT
                    m = pe.matmul(flat[:, at:at + queries.stop - queries.start], k_t[0:97, h, keys * P:(keys + 1) * P],
                                  q_t[0:97, h, queries], start=True, stop=True)
                m.then_inc(scored_t.sem, 1)

            def output(h):
                pe.wait_ge(exped.sem, exped.at(L, base + h + 1))
                if base + h >= 2:
                    pe.wait_ge(o_ready.sem, o_ready.at(L, base + h - 1))

                def v_ones(tile):
                    return v_tok[:, tile, h // 2, h % 2:h % 2 + 2, :]
                p = prob_t[:, h % 2, :]
                pe.matmul(ps[:, 4 + h % 2, 0:CTX], v_ones(0), p[:, 3 * LAT:PROB], start=True, stop=True)
                for i in range(3):
                    m = pe.matmul(ps[:, 4 + h % 2, CTX:T], v_ones(1 + i), p[:, i * LAT:(i + 1) * LAT],
                                  start=(i == 0), stop=(i == 2))
                m.then_inc(o_made.sem, 1)

            scores(0)
            maxima(0)
            for h in range(HALF):
                if h + 1 < HALF:
                    scores(h + 1)
                scores_t(h)
                if h + 1 < HALF:
                    maxima(h + 1)
                if h:
                    output(h - 1)
            output(HALF - 1)

        def fourier(pe, L):
            pe.wait_ge(f_ready.sem, f_ready.at(L, DB))
            pe.wait_ge(dft_in.sem, dft_in.at(L, 16))
            for i in range(CHUNKS * GROUPS):
                c, g = i // GROUPS, i % GROUPS
                if i >= 4:
                    pe.wait_ge(ch_taken.sem, ch_taken.at(L, i - 3))
                for kk in range(2):
                    m = pe.matmul(ps[:, 4 + i % 4, :], wide[:, 2 * g + kk, c * P:(c + 1) * P], dft_ch[:, kk, :],
                                  start=(kk == 0), stop=(kk == 1))
                m.then_inc(ch_made.sem, 1)
            pe.wait_ge(ch_taken.sem, ch_taken.at(L, CHUNKS * GROUPS))
            for b in range(DB):
                g, w = b // 2, (b % 2) * P
                if b >= 4:
                    pe.wait_ge(y_lo_made.sem, y_lo_made.at(L, 2 * DB + b - 3))
                for s in range(2):
                    pe.matmul(ps[:, 4 + b % 4, 0:CTX], f_ch[:, 0, g, s * 256 + w:s * 256 + w + P], dft_ctx[:, s, :],
                              start=(s == 0), stop=(s == 1))
                for i in range(4):
                    c, s = i // 2, i % 2
                    m = pe.matmul(ps[:, 4 + b % 4, CTX:T], f_ch[:, 1 + c, g, s * 256 + w:s * 256 + w + P],
                                  dft_lat[:, c, s, :], start=(i == 0), stop=(i == 3))
                m.then_inc(pos_made.sem, 1)

        STATES = [(0, 0), (1, 0), (0, 1), (1, 2)]
        ENTERING = [(0, 1), (1, 2), (0, 2), (1, 1)]
        UNITS = [(c, g, d) for c in range(CHUNKS) for g in range(2) for d in range(2)]

        def up_stage(eng, half, body):
            t, count = STAGES[f"up{half}"]
            first, end = t, t + count
            def one(t, turn, j, k, par, i):
                body(t, turn, j, k, par == 0, i)
            while t % RING and t < end:
                one(t, t // RING, t % RING, t - first, (t - first) % 2, (t - first) // 2)
                t += 1
            turns = (end - t) // RING
            with eng.Fori(0, turns) as r:
                for j in range(RING):
                    k0 = t + j - first
                    one(r * RING + (t + j), r + t // RING, j, r * RING + k0, k0 % 2, r * (RING // 2) + k0 // 2)
            t += turns * RING
            while t < end:
                one(t, t // RING, t % RING, t - first, (t - first) % 2, (t - first) // 2)
                t += 1

        def sub_stage(eng, first, count, body):
            t, end = first, first + count
            while t % RING and t < end:
                body(t, t // RING, t % RING, t - first)
                t += 1
            turns = (end - t) // RING
            if turns:
                with eng.Fori(0, turns) as r:
                    for j in range(RING):
                        body(r * RING + (t + j), r + t // RING, j, r * RING + (t + j - first))
                t += turns * RING
            while t < end:
                body(t, t // RING, t % RING, t - first)
                t += 1

        def lagged(eng, first, count, body):
            for t in range(first, first + RING):
                body(t, t // RING, t % RING, t - first)
            sub_stage(eng, first + RING, count - RING, lambda t, turn, j, k: body(t, turn, j, k + RING))

        def param_at(name, k, step, i):
            at = PARAMS[name][0]
            start = k * step + (at + i)
            return params[:, bass.ds(start, 1)]

        def gates(L, act, refill, stage, branch):
            def body(t, turn, j, k, i, is_gate):
                refill(L, t, turn, j)
                if is_gate:
                    act.wait_ge(taken.sem, taken.at(L, t + AHEAD))
                    act.activation(gate[:, :], ps[:, 2 * (j % 2), 0:T], ACT.Sigmoid,
                                   bias=param_at("b_gate", i + branch * DB, 1, 0)).then_inc(gate_made.sem, 1)
            pairs(act, stage, body)

        def pairs(eng, stage, body):
            t, count = STAGES[stage]
            first, end = t, t + count
            while t % RING and t < end:
                body(t, t // RING, t % RING, t - first, (t - first) // 2, (t - first) % 2 == 0)
                t += 1
            turns = (end - t) // RING
            with eng.Fori(0, turns) as r:
                for j in range(RING):
                    k0 = t + j - first
                    body(r * RING + (t + j), r + t // RING, j, r * RING + k0, r * (RING // 2) + k0 // 2, k0 % 2 == 0)
            t += turns * RING
            while t < end:
                body(t, t // RING, t % RING, t - first, (t - first) // 2, (t - first) % 2 == 0)
                t += 1

        def ssd_act(L, act):
            def token_major(n):
                c, at = TOKEN_ORDER[n]
                at *= 512
                act.wait_ge(transposed.sem, transposed.at(L, n + 1))
                act.activation(xs_tok[:, c, :], flat[:, at:at + 1024], ACT.Copy)
                act.activation(b_tok[:, c, :], flat[:, at + 1024:at + 1280], ACT.Copy).then_inc(tok_ready.sem, 1)

            token_major(0)
            act.wait_ge(kvq_value.sem, kvq_value.at(L, 5))
            for k in range(QB):
                act.activation(q_hi[:, k, :], low[:, KVB + k, :], ACT.Copy).then_inc(kvq_hi_made.sem, 1)
            act.wait_ge(to_end.sem, to_end.at(L, 1))
            act.activation(dts[:, 6, :], dts[:, 5, :], ACT.Exp)
            act.activation(dts[:, 4, :], dts[:, 2, :], ACT.Exp)
            act.activation(dts[:, 7, :], acum_ps[:, 96:192], ACT.Exp).then_inc(dt_exp.sem, 1)
            act.wait_ge(kvq_lo_made.sem, kvq_lo_made.at(L, 5))
            token_major(1)
            token_major(2)
            for n in range(2):
                act.wait_ge(states_made.sem, states_made.at(L, n + 1))
                act.activation(ctx_states[:, n, :], flat[:, n * 1024:(n + 1) * 1024], ACT.Copy)\
                   .then_inc(new_state.sem, 1)
            for u, (c, g, d) in enumerate(UNITS):
                act.wait_ge(rows_made.sem, rows_made.at(L, u + 1))
                if u == 0:
                    act.wait_ge(off_made.sem, off_made.at(L, 4))
                if u >= 2:
                    act.wait_ge(y_diag.sem, y_diag.at(L, u - 1))
                for h in range(HALF):
                    at = c * 32 + d * 16 + g * HALF + h
                    m = act.activation(decay[:, u % 2 * HALF + h, :],
                                       ps[:, 4 + 2 * (u % 2) + h // 4, h % 4 * P:(h % 4 + 1) * P], ACT.Exp,
                                       bias=dts[:, 3, at:at + 1])
                m.then_inc(decay_ready.sem, 1)

        def attention_act(L, act, refill, half):
            t0 = STAGES[f"heads{half}"][0]
            for i in range(4):
                t = t0 + i
                refill(L, t, t // RING, t % RING)
                act.activation(q_t[0:64, 2 * i:2 * i + 2, :], ps[0:64, 2 * (t % 2):2 * (t % 2) + 2, 0:T], ACT.Copy)\
                   .then_inc(q_plain.sem, 1)
            for i in range(2):
                t = t0 + 4 + i
                refill(L, t, t // RING, t % RING)
                act.activation(k_t[0:64, 4 * i:4 * i + 4:2, :], ps[0:64, 2 * (t % 2):2 * (t % 2) + 2, :], ACT.Copy)\
                   .then_inc(k_even.sem, 1)
            for i in range(2):
                t = t0 + 6 + i
                refill(L, t, t // RING, t % RING)
                b = 2 * (t % 2)
                for s in range(4):
                    m = act.activation(v_tok[:, s, 2 * i:2 * i + 2, 0:3:2, :],
                                       flat[:, b * 512 + s * 256:b * 512 + (s + 1) * 256]
                                       .rearrange("p (h e n) -> p h e n", h=2, e=2), ACT.Copy)
                m.then_inc(v_ready.sem, 1)
            if half:
                for b in (2, 3):
                    o_hi(L, b)
            base = half * HALF

            def max_row(h):
                act.wait_ge(max_turned.sem, max_turned.at(L, base + h + 1))
                act.activation(q_t[96:97, h, :], ps[96:97, 6, 0:T], ACT.Copy, scale=-1.0).then_inc(max_in.sem, 1)

            max_row(0)
            for h in range(HALF):
                act.wait_ge(scored_t.sem, scored_t.at(L, base + h + 1))
                if base + h >= 2:
                    act.wait_ge(o_made.sem, o_made.at(L, base + h - 1))
                act.activation(prob_t[:, h % 2, :], flat[:, 1024:1024 + PROB], ACT.Exp, scale=ATTN_SCALE)\
                   .then_inc(exped.sem, 1)
                if h + 1 < HALF:
                    max_row(h + 1)
                if h in (4, 6):
                    o_hi(L, 4 * half + h // 2 - 2)
            if half:
                for b in (6, 7):
                    o_hi(L, b)

        def o_hi(L, b):
            nc.scalar.wait_ge(o_ready.sem, o_ready.at(L, 2 * b + 2))
            nc.scalar.activation(y_hi[:, b, :], wide[:, b, :], ACT.Copy).then_inc(y_hi_made.sem, 1)

        def y_los(L, n, value):
            dve = nc.vector
            for k in range(DB):
                dve.wait_ge(y_hi_made.sem, y_hi_made.at(L, n * DB + k + 1))
                dve.tensor_tensor(y_lo[:, k, :], value(k), y_hi[:, k, :].bitcast(F32), ALU.subtract)\
                   .then_inc(y_lo_made.sem, 1)

        def merge(L, stage, branch):
            dve = nc.vector

            def body(t, turn, j, k, i, is_gate):
                dve.wait_ge(hi_made.sem, hi_made.at(L, t + AHEAD + 1))
                dve.tensor_tensor(w_lo[:, j % AHEAD, :], raw[:, (j + AHEAD) % RING, :],
                                  w_hi[:, j % AHEAD, :].bitcast(F32), ALU.subtract).then_inc(lo_made.sem, 1)
                if is_gate:
                    dve.wait_ge(gate_made.sem, gate_made.at(L, i + branch * DB + 1))
                    after(dve).then_inc(taken.sem, 1)
                    return
                dve.wait_ge(used.sem, used.at(L, t + 1))
                bank = ps[:, 2 * (j % 2), 0:T]
                if branch == 0:
                    dve.tensor_tensor(mix[:, i, :], gate[:, :], bank, ALU.mult).then_inc(taken.sem, 1)
                else:
                    dve.wait_ge(mixed.sem, mixed.at(L, i + (1 + (branch - 1) * DB)))
                    dve.tensor_tensor(gated[:, :], gate[:, :], bank, ALU.mult).then_inc(taken.sem, 1)
                    dve.wait_ge(taken.sem, taken.at(L, t + 1 + AHEAD))
                    dve.tensor_tensor(mix[:, i, :], mix[:, i, :], gated[:, :], ALU.add).then_inc(mixed.sem, 1)
            pairs(dve, stage, body)
            if branch == 0:
                after(dve).then_inc(mixed.sem, 1)

        def per_chunk(ap):
            return ap.rearrange("p (c n) -> p c n", c=CHUNKS)

        def dt_magnitude(L, dve, link):
            dt, mag = dts[:, 0, :], dts[:, 2, :]
            dve.wait_ge(dt_in.sem, dt_in.at(L, 1))
            link(L, dve.tensor_tensor(per_chunk(dt), per_chunk(dt), repeat(param("dt_bias", 0, 32), CHUNKS), ALU.add))
            link(L, dve.tensor_scalar(mag, dt, -1.0, None, ALU.mult))
            dve.tensor_tensor(mag, mag, dt, ALU.max).then_inc(dt_abs.sem, 1)

        def step_sizes(L, dve, link):
            dt, dta, _, e, ea_log, s2 = (dts[:, i, :] for i in range(6))
            poly = dts[:, 8, :]
            dve.wait_ge(dt_exp.sem, dt_exp.at(L, 1))
            link(L, dve.tensor_scalar(s2, e, 2.0, None, ALU.add))
            link(L, dve.reciprocal(s2, s2))
            link(L, dve.tensor_tensor(e, e, s2, ALU.mult))
            link(L, dve.tensor_tensor(s2, e, e, ALU.mult))
            link(L, dve.tensor_scalar(poly, s2, 1.0 / 17, None, ALU.mult))
            for q in (15, 13, 11, 9, 7, 5, 3):
                link(L, dve.scalar_tensor_tensor(out=poly, in0=poly, scalar=1.0 / q, in1=s2, op0=ALU.add, op1=ALU.mult))
            link(L, dve.scalar_tensor_tensor(out=poly, in0=poly, scalar=1.0, in1=e, op0=ALU.add, op1=ALU.mult))
            link(L, dve.tensor_scalar(dt, dt, 0.0, None, ALU.max))
            link(L, dve.scalar_tensor_tensor(out=dt, in0=poly, scalar=2.0, in1=dt, op0=ALU.mult, op1=ALU.add))
            dve.scalar_tensor_tensor(out=per_chunk(dta), in0=per_chunk(dt), scalar=-1.0,
                                     in1=repeat(ea_log[:, 0:32], CHUNKS), op0=ALU.mult, op1=ALU.mult)\
               .then_inc(dt_ready.sem, 1)
            dve.wait_ge(dt_ready.sem, dt_ready.at(L, 1))
            link(L, dve.tensor_copy(dta_parts[:, 0, :], dta))
            link(L, dve.tensor_tensor(s2, dta, dta_parts[:, 0, :], ALU.subtract))
            link(L, dve.tensor_copy(dta_parts[:, 1, :], s2))
            link(L, dve.tensor_tensor(dta_parts[:, 2, :], s2, dta_parts[:, 1, :], ALU.subtract))

        def cumulated(L, dve, link):
            acum, minus_acum, end = dts[:, 2, :], dts[:, 3, :], dts[:, 5, :]
            dve.wait_ge(acum_sums.sem, acum_sums.at(L, 1))
            for d in range(2):
                m = dve.tensor_copy(acum.rearrange("p (c d h) -> p c d h", c=CHUNKS, d=2)[:, :, d, :],
                                    acum_ps[:, d * 48:(d + 1) * 48].rearrange("p (c h) -> p c h", c=CHUNKS))
            link(L, m)
            dve.tensor_scalar(minus_acum, acum, -1.0, None, ALU.mult)
            dve.tensor_tensor(end, acum_ps[:, 96:192], acum, ALU.subtract).then_inc(to_end.sem, 1)

        def ssd_dve(L, dve, link):
            dt = dts[:, 0, :]
            acum, minus_acum, exp_a, end = (dts[:, i, :] for i in (2, 3, 4, 5))
            exp_end, exp_all, poly = (dts[:, i, :] for i in (6, 7, 8))
            dve.wait_ge(dt_exp.sem, dt_exp.at(L, 2))

            def heads(v):
                return v.rearrange("p (h n) -> p h n", n=HD)

            def at_heads(table, d, c):
                return spread(table[:, c * 32 + d * 16:c * 32 + d * 16 + 16], HD)

            link(L, dve.tensor_tensor(poly, dt, exp_end, ALU.mult))
            for n, (d, c) in enumerate(STATES):
                if n == 0:
                    dve.wait_ge(tok_ready.sem, tok_ready.at(L, 2))
                if n == 2:
                    dve.wait_ge(cb_made.sem, cb_made.at(L, 1))
                    link(L, dve.tensor_copy(cb[:, :, :], flat[:, 6 * 512:6 * 512 + 768]
                                            .rearrange("p (i n) -> p i n", n=P)))
                    dve.wait_ge(tok_ready.sem, tok_ready.at(L, CHUNKS))
                if n >= 2:
                    dve.wait_ge(states_made.sem, states_made.at(L, n - 1))
                dve.tensor_tensor(heads(x_end[:, n % 2, :]), heads(xs_tok[:, c, :]), at_heads(poly, d, c), ALU.mult)\
                   .then_inc(ends_ready.sem, 1)
            dve.wait_ge(states_made.sem, states_made.at(L, 4))
            for n, (d, c) in enumerate(ENTERING):
                off = flat[:, 2048 + 1024 * (n % 2):3072 + 1024 * (n % 2)]
                dve.wait_ge(off_made.sem, off_made.at(L, n + 1))
                if n < 2:
                    dve.tensor_tensor(heads(off_tok[:, c - 1, :]), heads(off), at_heads(exp_a, d, c), ALU.mult)\
                       .then_inc(off_ready.sem, 1)
                    link(L, dve.tensor_tensor(heads(h_state[:, d, :]), heads(h_state[:, d, :]), at_heads(exp_all, d, c),
                                              ALU.mult))
                    dve.tensor_tensor(h_state[:, d, :], h_state[:, d, :], flat[:, 1024 * n:1024 * (n + 1)], ALU.add)\
                       .then_inc(state_next.sem, 1)
                else:
                    link(L, dve.tensor_tensor(heads(scaled), heads(off), at_heads(exp_a, d, c), ALU.mult))
                    dve.tensor_tensor(off_tok[:, c - 1, :], off_tok[:, c - 1, :], scaled, ALU.add)\
                       .then_inc(off_ready.sem, 1)
                    dve.wait_ge(off_ready.sem, off_ready.at(L, n + 1))
            dve.wait_ge(state_out.sem, state_out.at(L, 32))
            for c in range(2):
                dve.wait_ge(off_turned.sem, off_turned.at(L, c + 1))
                cols = slice((1 + c) * P, (2 + c) * P)
                for b in range(DB):
                    m = dve.scalar_tensor_tensor(out=wide[:, b, cols], in0=xbc[:, b, cols], scalar=param("d_skip", b),
                                                 in1=ps[:, 2 * c + b // 4, b % 4 * P:(b % 4 + 1) * P],
                                                 op0=ALU.mult, op1=ALU.add)
                m.then_inc(off_back.sem, 1)

            def x_dt(u):
                c, g, d = UNITS[u]
                cols = slice(g * 512, (g + 1) * 512)
                at = c * 32 + d * 16 + g * HALF
                dve.tensor_tensor(heads(xdt[:, d, cols]), heads(xs_tok[:, c, cols]), spread(dt[:, at:at + HALF], HD),
                                  ALU.mult).then_inc(xdt_ready.sem, 1)

            def add_y(n):
                c, g = n // 2, n % 2
                cols = slice(c * P, (c + 1) * P)
                dve.wait_ge(y_diag.sem, y_diag.at(L, 2 * n + 2))
                sums_ = ps[:, n % 4, :].rearrange("p (b n) -> p b n", b=4)
                if c == 0:
                    for b in range(4):
                        m = dve.scalar_tensor_tensor(out=wide[:, 4 * g + b, cols], in0=xbc[:, 4 * g + b, cols],
                                                     scalar=param("d_skip", 4 * g + b), in1=sums_[:, b, :],
                                                     op0=ALU.mult, op1=ALU.add)
                else:
                    m = dve.tensor_tensor(wide[:, 4 * g:4 * g + 4, cols], wide[:, 4 * g:4 * g + 4, cols], sums_, ALU.add)
                m.then_inc(y_added.sem, 1)

            x_dt(0)
            for u, (c, g, d) in enumerate(UNITS):
                dve.wait_ge(decay_ready.sem, decay_ready.at(L, u + 1))
                buf = decay[:, u % 2 * HALF:(u % 2 + 1) * HALF, :]
                dve.tensor_tensor(buf, buf, repeat(cb[:, 2 * c + g, :], HALF), ALU.mult).then_inc(weighted.sem, 1)
                if u == 0:
                    for i in range(1, 4):
                        x_dt(i)
                elif u + 3 < len(UNITS):
                    dve.wait_ge(y_diag.sem, y_diag.at(L, u))
                    x_dt(u + 3)
                if u >= 3 and u % 2 == 1:
                    add_y(u // 2 - 1)
            add_y(len(UNITS) // 2 - 1)
            dve.wait_ge(y_added.sem, y_added.at(L, 2 * CHUNKS))

        def attention_dve(L, dve, link, split, tick_taken, half):
            t0 = STAGES[f"heads{half}"][0]
            for i in range(4):
                t = t0 + i
                split(L, t, t // RING, t % RING)
                dve.wait_ge(q_plain.sem, q_plain.at(L, 4 * half + i + 1))
                b = 2 * (t % 2)
                n = 3 * (4 * half + i)
                if n:
                    dve.wait_ge(q_rot.sem, q_rot.at(L, n))
                dve.tensor_tensor(rot[64:96, :, :], ps[96:128, b:b + 2, 0:T], repeat(rope[96:128, :], 2), ALU.mult)\
                   .then_inc(q_rot.sem, 1)
                dve.tensor_tensor(q_t[64:96, 2 * i:2 * i + 2, :], ps[64:96, b:b + 2, 0:T], repeat(rope[64:96, :], 2),
                                  ALU.mult).then_inc(q_rot.sem, 1)
                dve.wait_ge(q_rot.sem, q_rot.at(L, n + 2))
                tick_taken()
            for i in range(2):
                t = t0 + 4 + i
                split(L, t, t // RING, t % RING)
                dve.wait_ge(k_even.sem, k_even.at(L, 2 * half + i + 1))
                b = 2 * (t % 2)
                dve.tensor_copy(k_t[0:64, 4 * i + 1:4 * i + 4:2, :], ps[64:128, b:b + 2, :]).then_inc(taken.sem, 1)
            for i in range(2):
                t = t0 + 6 + i
                split(L, t, t // RING, t % RING)
                dve.wait_ge(v_ready.sem, v_ready.at(L, 2 * half + i + 1))
                tick_taken()
            base = half * HALF

            def o_lo(b):
                dve.wait_ge(y_hi_made.sem, y_hi_made.at(L, DB + b + 1))
                dve.tensor_tensor(y_lo[:, b, :], wide[:, b, :], y_hi[:, b, :].bitcast(F32), ALU.subtract)\
                   .then_inc(y_lo_made.sem, 1)

            def maxima(h):
                dve.wait_ge(scored.sem, scored.at(L, base + h + 1))
                at = 3 * (h % 2)
                dve.tensor_reduce(stat[:, at:at + 1], ps[:, 0, 0:CTX], AX.X, ALU.max)
                dve.tensor_reduce(stat[:, at + 1:at + 3], flat[:, CTX:CTX + 2 * T].rearrange("p (i n) -> p i n", i=2),
                                  AX.X, ALU.max).then_inc(maxed.sem, 1)

            def normalise(h):
                dve.wait_ge(o_made.sem, o_made.at(L, base + h + 1))
                bank = ps[:, 4 + h % 2, 0:T]
                at = h % 2 * HD
                own, other = slice(at, at + HD), slice(HD - at, P - at)
                link(L, dve.reciprocal(gated[own, :], bank[other, :]))
                dve.tensor_tensor(wide[own, (base + h) // 2, :], bank[own, :], gated[own, :], ALU.mult)\
                   .then_inc(o_ready.sem, 1)

            if half:
                for b in (2, 3):
                    o_lo(b)
            maxima(0)
            for h in range(HALF):
                if h + 1 < HALF:
                    maxima(h + 1)
                if h >= 2:
                    normalise(h - 2)
                if h in (6, 7):
                    o_lo(4 * half + h - 6)
            normalise(HALF - 2)
            normalise(HALF - 1)
            if half:
                for b in (6, 7):
                    o_lo(b)

        block = ctx.enter_context(nc.Block())


        @block.sync
        def _(sp):
            total = LAYERS * TILES
            sp.wait_ge(loaded, 48)
            for t in range(RING):
                sp.dma_start(raw[:, t, :], a_weights[t]).then_inc(arrived[t].sem, 16)
            with sp.Fori(0, total // RING - 1) as r:
                for j in range(RING):
                    sp.wait_ge(lo_made.sem, r * RING + (j + 1))
                    sp.dma_start(raw[:, j, :], a_weights[r * RING + (RING + j)]).then_inc(arrived[j].sem, 16)
            for j in range(AHEAD):
                sp.wait_ge(lo_made.sem, total - RING + j + 1)
                sp.dma_start(raw[:, j, :], a_weights[j]).then_inc(arrived[j].sem, 16)

        @block.gpsimd
        def _(pool):
            pool.dma_start(cond[:, :, :], a_cond).then_inc(loaded, 16)
            pool.dma_start(consts[:, :], a_consts[:, 0:N_KEPT]).then_inc(loaded, 16)
            pool.dma_start(x[:, :, :], a_x).then_inc(loaded, 16)
            def side_load(L, g):
                if g == 4:
                    pool.wait_ge(h_lo_made.sem, h_lo_made.at(L, DB))
                elif g == 5:
                    pool.wait_ge(y_added.sem, y_added.at(L, 2 * CHUNKS))
                elif g == 6:
                    pool.wait_ge(pos_made.sem, pos_made.at(L, DB))
                else:
                    pool.wait_ge(side_used.sem, side_used.at(L, g + 1))
                settle(pool, pool_marks)
                into = side_in[g % 2].sem
                if g in (4, 5):
                    pool.dma_start(side_three[g], a_ada[L, g, :, 0:3072]).then_inc(into, 16)
                    pool.dma_start(side_last, a_ada[L, g, :, 3072:4096]).then_inc(into, 16)
                else:
                    pool.dma_start(side_slot[g % 2], a_ada[L, g].rearrange("p (i n) -> p i n", i=SIDE_TILES))\
                        .then_inc(into, 16)

            with pool.Fori(0, LAYERS) as L:
                side_load(L, 0)
                side_load(L, 1)
                pool.wait_ge(caches_free.sem, caches_free.at(L, 1))
                settle(pool, pool_marks)
                pool.dma_start(params[:, :], a_params[L]).then_inc(params_in.sem, 16)
                pool.dma_start(h_state[:, :, :], a_state[L]).then_inc(state_in.sem, 16)
                pool.dma_start(ckv[:, :, T:KEYS], a_ckv[L]).then_inc(cache_in.sem, 16)
                pool.dma_start(kpe[64:96, T:KEYS], a_kpe[L]).then_inc(cache_in.sem, 16)
                side_load(L, 2)
                side_load(L, 3)
                side_load(L, 4)
                pool.wait_ge(misc_copied.sem, misc_copied.at(L, 1))
                settle(pool, pool_marks)
                pool.dma_start(o_kpe[L], kpe_raw[64:96, :]).then_inc(stored, 16)
                pool.wait_ge(ckv_ready.sem, ckv_ready.at(L, 1))
                settle(pool, pool_marks)
                pool.dma_start(o_ckv[L], ckv[:, :, 0:CTX]).then_inc(stored, 16)
                for d in range(2):
                    pool.wait_ge(new_state.sem, new_state.at(L, d + 1))
                    settle(pool, pool_marks)
                    pool.dma_start(o_state[L, d], ctx_states[:, d, :]).then_inc(state_out.sem, 16)
                side_load(L, 5)
                pool.wait_ge(y_added.sem, y_added.at(L, 2 * CHUNKS))
                pool.wait_ge(kpe_ready.sem, kpe_ready.at(L, 3))
                pool.wait_ge(cache_in.sem, cache_in.at(L, 32))
                pool.wait_ge(stored, (L + 1) * 32)
                settle(pool, pool_marks)
                pool.memset(k_t[96:97, :, :], 1.0).then_inc(kpe_spread.sem, 1)
                pool.wait_ge(kpe_spread.sem, kpe_spread.at(L, 1))
                settle(pool, pool_marks)
                pool.memset(v_tok[:, :, :, 1, :], 1.0).then_inc(kpe_spread.sem, 1)
                pool.wait_ge(kpe_spread.sem, kpe_spread.at(L, 2))
                settle(pool, pool_marks)
                pool.tensor_copy(k_t[64:96, :, :], repeat(kpe[64:96, :], HALF)).then_inc(kpe_spread.sem, 1)
                for i in range(HALF):
                    pool.wait_ge(q_rot.sem, q_rot.at(L, 3 * i + 2))
                    settle(pool, pool_marks)
                    q_pe = q_t[64:96, 2 * (i % 4):2 * (i % 4) + 2, :]
                    pool.tensor_tensor(q_pe, q_pe, rot[64:96, :, :], ALU.add).then_inc(q_rot.sem, 1)
                pool.wait_ge(o_made.sem, o_made.at(L, HEADS))
                settle(pool, pool_marks)
                pool.dma_start(dft, a_consts[:, N_KEPT:]).then_inc(dft_in.sem, 16)
                for g in range(6, SIDE):
                    side_load(L, g)
            pool.wait_ge(x_ready.sem, x_ready.at(LAYERS, DB))
            pool.dma_start(o_x, x[:, :, :]).then_inc(stored, 16)
            pool.wait_ge(stored, 16 * (2 * LAYERS + 1))
            pool.wait_ge(state_out.sem, LAYERS * 32)
            for j in range(AHEAD):
                pool.wait_ge(arrived[j].sem, 16 * (LAYERS * TURNS + 1))

        @block.tensor
        def _(pe):
            def product(out, blocks, first=True, last=True):
                for i, (ah, al, bh, bl) in enumerate(blocks):
                    start, stop = first and i == 0, last and i == len(blocks) - 1
                    pe.matmul(out, ah, bh, start=start, stop=False)
                    pe.matmul(out, ah, bl, start=False, stop=False)
                    m = pe.matmul(out, al, bh, start=False, stop=stop)
                return m

            def weights(j, k, n=P, at=None):
                lo = k * P if at is None else at
                return w_hi[:, j % AHEAD, lo:lo + n], w_lo[:, j % AHEAD, lo:lo + n]

            def tile_in(L, t, ago=2):
                pe.wait_ge(lo_made.sem, lo_made.at(L, t + 1))
                pe.wait_ge(taken.sem, taken.at(L, t + 3 - ago))

            def tile_product(t, j, hi, lo, parts=None, banks=2):
                for kk in range(DB):
                    if parts:
                        pe.wait_ge(parts[0].sem, parts[1] + kk)
                    m = product(ps[:, tile_bank(j, banks), 0:T], [(*weights(j, kk), hi[:, kk, :], lo[:, kk, :])],
                                first=(kk == 0), last=(kk == DB - 1))
                m.then_inc(used.sem, 1)

            def project(L, stage, hi, lo, parts=None, banks=2):
                def body(t, turn, j, k):
                    tile_in(L, t, 2 if isinstance(k, int) else banks)
                    tile_product(t, j, hi, lo, parts if isinstance(k, int) and k == 0 else None, banks)
                if parts and STAGES[stage][0] % RING == 0:
                    lagged(pe, *STAGES[stage], body)
                else:
                    through(pe, stage, body)

            def added_sum(L, which):
                pe.wait_ge(added.sem, added.at(L, (which + 1) * (DB - 1)))
                pe.matmul(ps[:, 7, 0:T], ones, mix[:, 0, :], start=True, stop=True).then_inc(sums.sem, 1)

            def norm_sum(L, n, sq, order=None):
                blocks = NORM_BLOCKS[n - 1]
                order = order or range(blocks)
                for i in range(blocks):
                    pe.wait_ge(squares.sem, squares_at(L, n, i + 1))
                    m = pe.matmul(ps[:, 7, 0:T], ones, sq[:, order[i], :], start=(i == 0), stop=(i == blocks - 1))
                    if i == blocks - 1:
                        m.then_inc(sums.sem, 1)

            def out_project(L, stage, branch):
                def body(t, turn, j, k):
                    tile_in(L, t)
                    first = isinstance(k, int) and k == 1
                    tile_product(t, j, *((h_hi, h_lo) if j % 2 == 0 else (y_hi, y_lo)),
                                 (y_lo_made, y_lo_made.at(L, branch * DB + 1)) if first else None)
                assert STAGES[stage][0] % 2 == 0
                through(pe, stage, body)

            def side(L, g, between=None):
                pe.wait_ge(side_in[g % 2].sem, side_in[g % 2].at(L, SIDE_ARRIVED[g]))
                for i in range(SIDE_TILES):
                    if g in (4, 5):
                        tile = side_three[g][:, i * 1024:(i + 1) * 1024] if i < 3 else side_last
                    else:
                        tile = side_slot[g % 2][:, i, :]
                    for kk in range(DB):
                        m = pe.matmul(ps[0:8, 5 + g % 2, 0:P], cond_pad[:, kk, 6 - 2 * i:14 - 2 * i],
                                      tile[:, kk * P:(kk + 1) * P], start=(i == 0 and kk == 0),
                                      stop=(i == SIDE_TILES - 1 and kk == DB - 1))
                    if between and i == 1:
                        between()
                m.then_inc(side_used.sem, 1)

            def columns(L, v):
                pe.wait_ge(rows_out.sem, rows_out.at(L, 2 * v + 2))
                if v:
                    pe.wait_ge(cols_taken.sem, cols_taken.at(L, v))
                for p in range(2):
                    m = pe.matmul(ps[:, 4, 8 * p:8 * p + 8], mod_rows[:, p, :], ident[0:8, 0:8], start=True, stop=True)
                m.then_inc(cols_made.sem, 1)

            pe.wait_ge(loaded, 48)
            pe.wait_ge(cond_ready, 2)
            pe.wait_ge(side_used.sem, 2)
            with pe.Fori(0, LAYERS) as L:
                side(L, 0)
                side(L, 1)
                norm_sum(L, 1, wide)
                columns(L, 0)
                side(L, 2)
                side(L, 3)
                columns(L, 1)
                project(L, "proj", h_hi, h_lo, (h_lo_made, h_lo_made.at(L, 1)), banks=4)
                dt_turn(pe, L)
                norm_sum(L, 2, mix[:, KVB + QB:, :])
                side(L, 4)
                norm_sum(L, 3, mix[:, KVB + QB:, :])
                ssd(pe, L)
                pe.wait_ge(y_added.sem, y_added.at(L, 2 * CHUNKS - 1))
                project(L, "z", h_hi, h_lo)
                side(L, 5, lambda: added_sum(L, 0))
                out_project(L, "out_ssd", 0)
                columns(L, 2)
                pe.wait_ge(cols_taken.sem, cols_taken.at(L, 3))
                attention(pe, L, 0, product, weights, tile_in)
                attention(pe, L, 1, product, weights, tile_in)
                out_project(L, "out_mla", 1)
                project(L, "f", h_hi, h_lo)
                fourier(pe, L)
                out_project(L, "out_fft", 2)
                side(L, 6)
                project(L, "w_o", y_hi, y_lo, (y_lo_made, y_lo_made.at(L, 3 * DB + 1)))
                side(L, 7, lambda: added_sum(L, 1))
                columns(L, 3)
                side(L, 8)
                norm_sum(L, 6, mix)
                side(L, 9)
                columns(L, 4)
                for half in range(2):
                    if half:
                        pe.wait_ge(down_taken.sem, down_taken.at(L, 1))
                        pe.wait_ge(down_taken_act.sem, down_taken_act.at(L, 1))
                    project(L, f"up{half}", h_hi, h_lo, None if half else (h_lo_made, h_lo_made.at(L, DB + 1)),
                            banks=4)
                    side(L, 10 + half)
                    pe.wait_ge(rows_out.sem, rows_out.at(L, 11 + half))
                    if half == 0:
                        pe.wait_ge(cols_taken.sem, cols_taken.at(L, 5))
                    pe.wait_ge(taken.sem, taken.at(L, STAGES[f"down{half}"][0] + AHEAD))

                    def down(t, turn, j, k, half=half):
                        pe.wait_ge(lo_made.sem, lo_made.at(L, t + 1))
                        pe.wait_ge(y_lo_made.sem, y_lo_made.at(L, 4 * DB + half * FF_H + 1 + k))
                        for b in range(DB):
                            wh, wl = weights(j, b)
                            m = product(ps[:, b, 0:T], [(wh, wl, y_hi[:, k, :], y_lo[:, k, :])],
                                        first=(k == 0), last=(k == FF_H - 1))
                        m.then_inc(used.sem, 1)
                    t0 = STAGES[f"down{half}"][0]
                    for k in range(FF_H):
                        down(t0 + k, (t0 + k) // RING, (t0 + k) % RING, k)
                    m = pe.matmul(ps[0:1, 7, 510:511], ones[:, 0:1], ones[:, 0:1], start=True, stop=True)
                    m.then_inc(down_made.sem, 1)
                norm_sum(L, 7, mix, DOWN_ORDER)
                columns(L, 5)

        @block.scalar
        def _(act):
            def refill(L, t, turn, j):
                act.wait_ge(used.sem, used.at(L, t + 1))
                nxt = (j + AHEAD) % RING
                act.wait_ge(arrived[nxt].sem, arrived[nxt].at(L, 16 * (turn + (j + AHEAD) // RING + 1)))
                act.activation(w_hi[:, j % AHEAD, :], raw[:, nxt, :], ACT.Copy).then_inc(hi_made.sem, 1)

            def rows(L, g):
                act.wait_ge(side_used.sem, side_used.at(L, g + 3))
                if g >= 2:
                    act.wait_ge(cols_made.sem, cols_made.at(L, g // 2))
                act.activation(mod_rows[:, g % 2, :], ps[0:8, 5 + g % 2, 0:P], ACT.Copy).then_inc(rows_out.sem, 1)

            def square(sq, src):
                act.activation(sq, src, ACT.Square).then_inc(squares.sem, 1)

            def norm(L, n, width):
                act.wait_ge(sums.sem, sums.at(L, n))
                act.activation(root[:, :], ps[:, 7, 0:T], ACT.Sqrt, scale=1.0 / width, bias=eps[:, 0:1])\
                   .then_inc(roots.sem, 1)

            def modulate(L, which):
                def hi(k):
                    n = which * DB + k + 1
                    act.wait_ge(h_value.sem, h_value.at(L, n))
                    act.wait_ge(h_latent.sem, h_latent.at(L, n))
                    act.activation(h_hi[:, k, :], wide[:, k, :], ACT.Copy).then_inc(h_hi_made.sem, 1)
                for k in range(DB):
                    act.wait_ge(scaled_by.sem, scaled_by.at(L, 2 * which * DB + k + 1))
                    if k == 0:
                        act.wait_ge(cols_used.sem, cols_used.at(L, which + 1))
                    act.activation(wide[:, k, CTX:T], wide[:, k, CTX:T], ACT.Identity,
                                   scale=coef[:, 3 * which, k, 1:2], bias=coef[:, 3 * which + 1, k, 1:2])\
                       .then_inc(h_latent.sem, 1)
                    if k:
                        hi(k - 1)
                hi(DB - 1)

            eps = stat[:, 63:64]
            act.wait_ge(loaded, 48)
            act.wait_ge(ready, 1)
            act.activation(cond_pad[:, :, 6:8], cond[:, :, :], ACT.Silu).then_inc(cond_ready, 1)
            for t in range(AHEAD):
                act.wait_ge(arrived[t].sem, 16)
                act.activation(w_hi[:, t, :], raw[:, t, :], ACT.Copy).then_inc(hi_made.sem, 1)
            with act.Fori(0, LAYERS) as L:
                for k in range(DB):
                    act.wait_ge(x_ready.sem, x_ready.at(L, k + 1))
                    square(wide[:, k, :], x[:, k, :])
                rows(L, 0)
                rows(L, 1)
                norm(L, 1, D)
                rows(L, 2)
                rows(L, 3)
                act.wait_ge(params_in.sem, params_in.at(L, 16))
                modulate(L, 0)

                def centre(L, j, w_name, b_name, k):
                    act.activation(conv[:, j % 2, :], ps[:, tile_bank(j, 4), 0:T], ACT.Identity,
                                   scale=param_at(w_name, k, 3, 1), bias=param_at(b_name, k, 1, 0))\
                       .then_inc(conv_mid.sem, 1)

                def xbc_silu(j, k):
                    act.wait_ge(conv_done.sem, conv_done.at(L, k + 1))
                    act.activation(xbc[:, k, :], conv[:, j % 2, :], ACT.Silu).then_inc(silu_done.sem, 1)

                def proj(t, turn, j, k):
                    refill(L, t, turn, j)
                    if not (isinstance(k, int) and k < 2):
                        act.wait_ge(silu_done.sem, silu_done.at(L, k - 1))
                    centre(L, j, "conv_w", "conv_b", k)
                    if not (isinstance(k, int) and k == 0):
                        xbc_silu(j + 1, k - 1)
                t0 = STAGES["proj"][0]
                lagged(act, t0, XBC_B, proj)
                for k in range(XBC_B, 18):
                    t = t0 + k
                    refill(L, t, t // RING, t % RING)
                    if k == XBC_B:
                        xbc_silu(k - 1, k - 1)
                        bank = ps[:, tile_bank(t, 4), :]
                        act.activation(dt_t[:, :], bank[0:32, 0:T], ACT.Copy)
                        act.activation(kpe_raw[64:96, :], bank[64:96, 0:CTX], ACT.Copy).then_inc(misc_copied.sem, 1)
                act.wait_ge(taken.sem, taken.at(L, t0 + 18 + AHEAD))
                for k in range(KVB):
                    square(mix[:, KVB + QB + k, :], low[:, k, :])
                act.wait_ge(dt_turned.sem, dt_turned.at(L, 1))
                act.activation(dts[:, 0, :], ps[:, 6, 0:96], ACT.Copy).then_inc(dt_in.sem, 1)
                norm(L, 2, KVL)
                act.wait_ge(dt_abs.sem, dt_abs.at(L, 1))
                act.activation(dts[:, 3, :], dts[:, 2, :], ACT.Exp, scale=-1.0)
                act.activation(dts[:, 4, 0:32], param("a_log", 0, 32), ACT.Exp).then_inc(dt_exp.sem, 1)
                act.wait_ge(kvq_value.sem, kvq_value.at(L, 2))
                act.wait_ge(cache_in.sem, cache_in.at(L, 32))
                for k in range(KVB):
                    act.activation(ckv_hi[:, k, :], ckv[:, k, :], ACT.Copy).then_inc(kvq_hi_made.sem, 1)
                for k in range(QB):
                    square(mix[:, KVB + QB + k, :], low[:, KVB + k, :])
                rows(L, 4)
                norm(L, 3, QL)
                ssd_act(L, act)

                def z_tile(t, turn, j, k):
                    refill(L, t, turn, j)
                    act.activation(conv[:, j % 2, :], ps[:, 2 * (j % 2), 0:T], ACT.Silu).then_inc(silu_done.sem, 1)
                    if k:
                        z_square(k - 1)

                def z_square(k):
                    act.wait_ge(y_value.sem, y_value.at(L, k + 1))
                    square(mix[:, k, :], wide[:, k, :])
                through(act, "z", z_tile)
                z_square(DB - 1)
                norm(L, 4, D)
                for k in range(DB):
                    act.wait_ge(y_value.sem, y_value.at(L, DB + k + 1))
                    act.activation(y_hi[:, k, :], wide[:, k, :], ACT.Copy).then_inc(y_hi_made.sem, 1)
                rows(L, 5)
                gates(L, act, refill, "out_ssd", 0)

                L = anew(act, L)
                attention_act(L, act, refill, 0)
                attention_act(L, act, refill, 1)
                gates(L, act, refill, "out_mla", 1)

                def f_tile(t, turn, j, k):
                    refill(L, t, turn, j)
                    act.activation(wide[:, k, :], ps[:, 2 * (j % 2), 0:T], ACT.Copy).then_inc(f_ready.sem, 1)
                through(act, "f", f_tile)
                for i in range(CHUNKS * GROUPS):
                    act.wait_ge(ch_made.sem, ch_made.at(L, i + 1))
                    act.activation(f_ch[:, i // GROUPS, i % GROUPS, :], ps[:, 4 + i % 4, :], ACT.Copy)\
                       .then_inc(ch_taken.sem, 1)
                for b in range(DB):
                    act.wait_ge(pos_made.sem, pos_made.at(L, b + 1))
                    act.activation(y_hi[:, b, :], ps[:, 4 + b % 4, 0:T], ACT.Copy).then_inc(y_hi_made.sem, 1)
                gates(L, act, refill, "out_fft", 2)
                for k in range(DB):
                    act.wait_ge(mixed.sem, mixed.at(L, 1 + DB + k + 1))
                    if k == 0:
                        act.wait_ge(used.sem, used.at(L, STAGES["w_o"][0]))
                    act.activation(y_hi[:, k, :], mix[:, k, :], ACT.Copy).then_inc(y_hi_made.sem, 1)

                rows(L, 6)

                def wo_tile(t, turn, j, k):
                    refill(L, t, turn, j)
                    if k == 0:
                        act.wait_ge(y_lo_made.sem, y_lo_made.at(L, 4 * DB))
                    square(mix[:, k, :], ps[:, 2 * (j % 2), 0:T])
                    act.activation(wide[:, k, :], ps[:, 2 * (j % 2), 0:T], ACT.Copy).then_inc(wo_ready.sem, 1)
                through(act, "w_o", wo_tile)
                L = anew(act, L)
                norm(L, 5, D)
                rows(L, 7)
                for k in range(DB):
                    act.wait_ge(x_mid.sem, x_mid.at(L, k + 1))
                    square(mix[:, k, :], x[:, k, :])
                rows(L, 8)
                norm(L, 6, D)
                rows(L, 9)
                modulate(L, 1)
                for half in range(2):
                    base = half * FF_B

                    def finish(j, k, a, i, half=half, base=base):
                        if a:
                            act.wait_ge(conv_done.sem, conv_done.at(L, k + (XBC_B + base + 1)))
                            act.activation(gate[:, :], conv[:, j % 2, :], ACT.Silu).then_inc(silu_done.sem, 1)
                        else:
                            act.wait_ge(ag_value.sem, ag_value.at(L, i + (half * FF_H + 1)))
                            act.activation(y_hi[:, i, :], gated[:, :], ACT.Copy).then_inc(y_hi_made.sem, 1)

                    def up(t, turn, j, k, a, i, half=half, base=base):
                        refill(L, t, turn, j)
                        first = isinstance(k, int)
                        if a and not (first and k < 2):
                            act.wait_ge(silu_done.sem, silu_done.at(L, i + (XBC_B + DB + half * FF_H)))
                        if not a and not (first and k < 2):
                            act.wait_ge(ag_value.sem, ag_value.at(L, i + half * FF_H))
                        centre(L, j, "ffn_w", "ffn_b", k + base)
                        if not (first and k == 0):
                            finish(j + 1, k - 1, not a, i if not a else i - 1)
                    up_stage(act, half, up)
                    finish(STAGES[f"up{half}"][0] + FF_B - 1, FF_B - 1, False, FF_H - 1)
                    rows(L, 10 + half)
                    t0 = STAGES[f"down{half}"][0]
                    for k in range(FF_H):
                        refill(L, t0 + k, (t0 + k) // RING, (t0 + k) % RING)
                    if half == 0:
                        act.wait_ge(down_made.sem, down_made.at(L, 1))
                        act.activation(wide[:, 4:8, :], ps[:, 4:8, 0:T], ACT.Copy).then_inc(down_taken_act.sem, 1)
                for i, b in enumerate(DOWN_ORDER):
                    act.wait_ge(down_taken.sem, down_taken.at(L, i + 2))
                    square(mix[:, b, :], wide[:, b, :])
                norm(L, 7, D)

        @block.vector
        def _(dve):
            steps = [0]

            def link(L, ins):
                steps[0] += 1
                ins.then_inc(dve_chain.sem, 1)
                dve.wait_ge(dve_chain.sem, dve_chain.at(L, steps[0]))

            def split(L, t, turn, j):
                dve.wait_ge(hi_made.sem, hi_made.at(L, t + AHEAD + 1))
                dve.tensor_tensor(w_lo[:, j % AHEAD, :], raw[:, (j + AHEAD) % RING, :],
                                  w_hi[:, j % AHEAD, :].bitcast(F32), ALU.subtract).then_inc(lo_made.sem, 1)

            def lo_part(out, value, hi):
                return dve.tensor_tensor(out, value, hi.bitcast(F32), ALU.subtract)

            def tick_taken():
                after(dve).then_inc(taken.sem, 1)

            def norm(L, n):
                dve.wait_ge(roots.sem, roots.at(L, n))
                link(L, dve.reciprocal(rstd[:, :], root[:, :]))

            def times_rstd(n, k, src):
                dve.tensor_tensor(wide[:, k, :], src[:, k, :], rstd[:, :], ALU.mult).then_inc(scaled_by.sem, 1)

            def modulate(L, which):
                def lo(k):
                    dve.wait_ge(h_hi_made.sem, h_hi_made.at(L, which * DB + k + 1))
                    lo_part(h_lo[:, k, :], wide[:, k, :], h_hi[:, k, :]).then_inc(h_lo_made.sem, 1)
                for k in range(DB):
                    dve.wait_ge(scaled_by.sem, scaled_by.at(L, 2 * which * DB + k + 1))
                    dve.tensor_scalar(wide[:, k, 0:CTX], wide[:, k, 0:CTX], coef[:, 3 * which, k, 0:1],
                                      coef[:, 3 * which + 1, k, 0:1], ALU.mult, ALU.add).then_inc(h_value.sem, 1)
                    if k >= 2:
                        lo(k - 2)
                lo(DB - 2)
                lo(DB - 1)

            def vector(L, v):
                which, kind = v // 3, v % 3
                dve.wait_ge(cols_made.sem, cols_made.at(L, v + 1))
                out = coef[:, 3 * which + (1, 0, 2)[kind], :, :]
                m = dve.tensor_tensor(out if kind == 0 else mod[:, :, :],
                                      ps[:, 4, 0:16].rearrange("p (k s) -> p k s", s=2),
                                      spread(param("b_ada", v * DB, DB), 2), ALU.add)
                m.then_inc(cols_taken.sem, 1)
                dve.wait_ge(cols_taken.sem, cols_taken.at(L, v + 1))
                if kind == 1:
                    link(L, dve.scalar_tensor_tensor(
                        out=out, in0=mod[:, :, :], scalar=1.0,
                        in1=spread(param(("g_pre_mix", "g_pre_ffn")[which], 0, DB), 2), op0=ALU.add, op1=ALU.mult))
                elif kind == 2:
                    link(L, dve.tensor_tensor(out, mod[:, :, :],
                                              spread(param(("g_post_mix", "g_post_ffn")[which], 0, DB), 2), ALU.mult))

            def add_squares(L, which, k):
                dve.wait_ge(squares.sem, squares_at(L, 4 + which, k + 1))
                if k > 1:
                    dve.wait_ge(added.sem, added.at(L, which * (DB - 1) + k - 1))
                dve.tensor_tensor(mix[:, 0, :], mix[:, 0, :], mix[:, k, :], ALU.add).then_inc(added.sem, 1)

            def residual(L, which, signal_):
                times_rstd(L, 0, wide)
                for k in range(DB):
                    if k + 1 < DB:
                        times_rstd(L, k + 1, wide)
                    dve.wait_ge(scaled_by.sem, scaled_by.at(L, (2 * which + 1) * DB + k + 1))
                    for s, (lo, hi) in enumerate(SEGS):
                        m = dve.scalar_tensor_tensor(out=x[:, k, lo:hi], in0=wide[:, k, lo:hi],
                                                     scalar=coef[:, 3 * which + 2, k, s:s + 1], in1=x[:, k, lo:hi],
                                                     op0=ALU.mult, op1=ALU.add)
                    m.then_inc(signal_.sem, 1)

            def taps(L, n, j, w_name, k, last):
                dve.wait_ge(conv_mid.sem, conv_mid.at(L, n + 1))
                bank, buf = ps[:, tile_bank(j, 4), :], conv[:, j % 2, :]
                for lo, hi in SEGS:
                    m = dve.scalar_tensor_tensor(out=buf[:, lo + 1:hi], in0=bank[:, lo:hi - 1],
                                                 scalar=param_at(w_name, k, 3, 0), in1=buf[:, lo + 1:hi],
                                                 op0=ALU.mult, op1=ALU.add)
                m.then_inc(conv_left.sem, 1)
                dve.wait_ge(conv_left.sem, conv_left.at(L, n + 1))
                for lo, hi in SEGS:
                    m = dve.scalar_tensor_tensor(out=buf[:, lo:hi - 1], in0=bank[:, lo + 1:hi],
                                                 scalar=param_at(w_name, k, 3, 2), in1=buf[:, lo:hi - 1],
                                                 op0=ALU.mult, op1=ALU.add)
                m.then_inc(conv_done.sem, 1)
                dve.wait_ge(conv_done.sem, conv_done.at(L, n + 1))
                tick_taken()

            for _ in range(2):
                after(dve).then_inc(side_used.sem, 1)
            after(dve).then_inc(caches_free.sem, 1)
            dve.wait_ge(loaded, 48)
            dve.memset(cond_pad[:, :, 0:6], 0.0)
            dve.memset(cond_pad[:, :, 8:14], 0.0).then_inc(cond_ready, 1)
            dve.memset(stat[:, 63:64], EPS).then_inc(ready, 1)
            for d in range(2):
                dve.tensor_copy(tri_bf[:, d, :], tri[d])
                dve.tensor_scalar(far_bf[:, d, :], tri[d], 1.0, 1e30, ALU.subtract, ALU.mult)
            dve.tensor_copy(ident_bf[:, :], ident)
            for t in range(AHEAD):
                dve.wait_ge(hi_made.sem, t + 1)
                dve.tensor_tensor(w_lo[:, t, :], raw[:, t, :], w_hi[:, t, :].bitcast(F32), ALU.subtract)\
                   .then_inc(lo_made.sem, 1)
            for _ in range(AHEAD):
                tick_taken()
            for _ in range(DB):
                after(dve).then_inc(x_ready.sem, 1)

            with dve.Fori(0, LAYERS) as L:
                dve.wait_ge(params_in.sem, params_in.at(L, 16))
                settle(dve, dve_marks)

                norm(L, 1)
                for k in range(DB):
                    times_rstd(L, k, x)
                vector(L, 0)
                vector(L, 1)
                after(dve).then_inc(cols_used.sem, 1)
                modulate(L, 0)

                def conv_tile(t, turn, j, k):
                    split(L, t, turn, j)
                    taps(L, k, j, "conv_w", k, None)
                t0 = STAGES["proj"][0]
                sub_stage(dve, t0, XBC_B, conv_tile)
                t = t0 + XBC_B
                j = t % RING
                split(L, t, t // RING, j)
                dve.wait_ge(misc_copied.sem, misc_copied.at(L, 1))
                bank = ps[:, tile_bank(j, 4), :]
                dve.tensor_tensor(gated[64:96, :], bank[32:64, 0:T], rope[32:64, :], ALU.mult).then_inc(kpe_ready.sem, 1)
                dve.tensor_tensor(kpe[64:96, 0:T], bank[64:96, 0:T], rope[64:96, :], ALU.mult).then_inc(kpe_ready.sem, 1)
                dve.wait_ge(kpe_ready.sem, kpe_ready.at(L, 2))
                tick_taken()
                dve.tensor_tensor(kpe[64:96, 0:T], kpe[64:96, 0:T], gated[64:96, :], ALU.add).then_inc(kpe_ready.sem, 1)
                for k in range(KVB + QB):
                    t = t0 + XBC_B + 1 + k
                    j = t % RING
                    split(L, t, t // RING, j)
                    dve.wait_ge(used.sem, used.at(L, t + 1))
                    dve.tensor_copy(low[:, k, :], ps[:, tile_bank(j, 4), 0:T]).then_inc(taken.sem, 1)
                dt_magnitude(L, dve, link)
                norm(L, 2)
                for k in range(KVB):
                    link(L, dve.scalar_tensor_tensor(out=ckv[:, k, 0:T], in0=low[:, k, :], scalar=param("g_kv", k),
                                             in1=rstd[:, :], op0=ALU.mult, op1=ALU.mult))
                after(dve).then_inc(ckv_ready.sem, 1)
                for k in range(KVB):
                    after(dve).then_inc(kvq_value.sem, 1)
                for k in range(KVB):
                    dve.wait_ge(kvq_hi_made.sem, kvq_hi_made.at(L, k + 1))
                    lo_part(ckv_lo[:, k, :], ckv[:, k, :], ckv_hi[:, k, :]).then_inc(kvq_lo_made.sem, 1)
                step_sizes(L, dve, link)
                norm(L, 3)
                for k in range(QB):
                    dve.scalar_tensor_tensor(out=low[:, KVB + k, :], in0=low[:, KVB + k, :], scalar=param("g_q", k),
                                             in1=rstd[:, :], op0=ALU.mult, op1=ALU.mult).then_inc(kvq_value.sem, 1)
                cumulated(L, dve, link)
                for k in range(QB):
                    dve.wait_ge(kvq_hi_made.sem, kvq_hi_made.at(L, KVB + k + 1))
                    lo_part(q_lo[:, k, :], low[:, KVB + k, :], q_hi[:, k, :]).then_inc(kvq_lo_made.sem, 1)
                ssd_dve(L, dve, link)

                def z_tile(t, turn, j, k):
                    split(L, t, turn, j)
                    dve.wait_ge(silu_done.sem, silu_done.at(L, XBC_B + k + 1))
                    dve.tensor_tensor(wide[:, k, :], wide[:, k, :], conv[:, j % 2, :], ALU.mult).then_inc(y_value.sem, 1)
                    tick_taken()
                    if k >= 2:
                        add_squares(L, 0, k - 1)
                through(dve, "z", z_tile)
                add_squares(L, 0, DB - 1)
                norm(L, 4)
                for k in range(DB):
                    dve.scalar_tensor_tensor(out=wide[:, k, :], in0=wide[:, k, :], scalar=param("g_ssd", k),
                                             in1=rstd[:, :], op0=ALU.mult, op1=ALU.mult).then_inc(y_value.sem, 1)
                y_los(L, 0, lambda k: wide[:, k, :])
                merge(L, "out_ssd", 0)
                vector(L, 2)

                attention_dve(L, dve, link, split, tick_taken, 0)
                attention_dve(L, dve, link, split, tick_taken, 1)
                merge(L, "out_mla", 1)
                through(dve, "f", lambda t, turn, j, k: (split(L, t, turn, j),
                                                        dve.wait_ge(f_ready.sem, f_ready.at(L, k + 1)),
                                                        tick_taken()))
                y_los(L, 2, lambda k: ps[:, 4 + k % 4, 0:T])
                merge(L, "out_fft", 2)
                y_los(L, 3, lambda k: mix[:, k, :])

                def wo_tile(t, turn, j, k):
                    split(L, t, turn, j)
                    dve.wait_ge(wo_ready.sem, wo_ready.at(L, k + 1))
                    tick_taken()
                    if k:
                        add_squares(L, 1, k)
                through(dve, "w_o", wo_tile)
                norm(L, 5)
                residual(L, 0, x_mid)
                dve.wait_ge(x_mid.sem, x_mid.at(L, DB))
                vector(L, 3)
                norm(L, 6)
                for k in range(DB):
                    times_rstd(L, k, x)
                vector(L, 4)
                after(dve).then_inc(cols_used.sem, 1)
                modulate(L, 1)

                for half in range(2):
                    def ag_lo(i, half=half):
                        dve.wait_ge(y_hi_made.sem, y_hi_made.at(L, i + (4 * DB + half * FF_H + 1)))
                        lo_part(y_lo[:, i, :], gated[:, :], y_hi[:, i, :]).then_inc(y_lo_made.sem, 1)

                    def up(t, turn, j, k, a, i, half=half):
                        split(L, t, turn, j)
                        taps(L, k + (XBC_B + half * FF_B), j, "ffn_w", k + half * FF_B, None)
                        if a:
                            if not (isinstance(i, int) and i == 0):
                                ag_lo(i - 1)
                        else:
                            if not (isinstance(i, int) and i == 0):
                                dve.wait_ge(y_lo_made.sem, y_lo_made.at(L, i + (4 * DB + half * FF_H)))
                            dve.wait_ge(silu_done.sem, silu_done.at(L, i + (XBC_B + DB + half * FF_H + 1)))
                            dve.tensor_tensor(gated[:, :], gate[:, :], conv[:, j % 2, :], ALU.mult)\
                               .then_inc(ag_value.sem, 1)
                    up_stage(dve, half, up)
                    ag_lo(FF_H - 1)
                    t0 = STAGES[f"down{half}"][0]
                    for k in range(FF_H):
                        split(L, t0 + k, (t0 + k) // RING, (t0 + k) % RING)
                        tick_taken()
                    dve.wait_ge(down_made.sem, down_made.at(L, half + 1))
                    if half == 0:
                        dve.tensor_copy(wide[:, 0:4, :], ps[:, 0:4, 0:T]).then_inc(down_taken.sem, 1)
                        dve.wait_ge(down_taken.sem, down_taken.at(L, 1))
                        dve.wait_ge(down_taken_act.sem, down_taken_act.at(L, 1))
                    else:
                        for b in DOWN_ORDER:
                            dve.tensor_tensor(wide[:, b, :], wide[:, b, :], ps[:, b, 0:T], ALU.add)\
                               .then_inc(down_taken.sem, 1)
                dve.wait_ge(down_taken.sem, down_taken.at(L, 1 + DB))
                norm(L, 7)
                vector(L, 5)
                residual(L, 1, x_ready)
                dve.wait_ge(x_ready.sem, x_ready.at(L, 2 * DB))
                after(dve).then_inc(caches_free.sem, 1)
            assert steps[0] == DVE_LINKS, steps


def dft(n, scale):
    i = np.arange(n)
    angle = 2 * np.pi * ((i[:, None] * i[None, :]) % n) / n
    return np.cos(angle) * scale, np.sin(angle) * scale


def rope_swap():
    q = ROPE // 4
    i = np.arange(ROPE)
    second = (i // q) % 2 == 1
    return np.where(second, i - q, i + q), np.where(second, 1.0, -1.0)


def constant_tables():
    out = np.zeros((P, N_CONSTS), np.float32)

    def put(name, value):
        at, n = CONSTS[name]
        out[:, at:at + n] = np.asarray(value, np.float64).reshape(P, n)
    i = np.arange(P)
    put("ident", np.eye(P))
    put("tri", np.concatenate([i[:, None] <= i[None, :], i[:, None] >= i[None, :]], 1))
    put("ones", np.ones((P, P)))
    c, s = dft(GROUP_W, GROUP_W ** -0.5)
    put("dft_ch", np.concatenate([c, s], 1).reshape(2, P, 512).transpose(1, 0, 2))
    c, s = dft(LAT, LAT ** -0.5)
    put("dft_lat", np.stack([c, -s], 1).reshape(2, P, 2, LAT).transpose(1, 0, 2, 3))
    c, s = dft(CTX, CTX ** -0.5)
    put("dft_ctx", np.stack([c, -s], 1))
    quarter = ROPE // 4
    inv = (10000.0 ** (-np.arange(quarter, dtype=np.float32) / quarter)).astype(np.float32)
    t = np.arange(LAT)
    pos = np.stack([t // 64, t % 64]).astype(np.float32)
    f = np.arange(ROPE)
    angle = (pos[f // (2 * quarter)] * inv[f % quarter][:, None]).astype(np.float32).astype(np.float64)
    _, sign = rope_swap()
    table = np.zeros((P, T))
    cos = np.concatenate([np.ones((ROPE, CTX)), np.cos(angle)], 1)
    sin = np.concatenate([np.zeros((ROPE, CTX)), np.sin(angle) * sign[:, None]], 1)
    table[32:64], table[64:96], table[96:128] = sin, cos, sin
    put("rope", table)
    return out


def pack_weights(w):
    tiles = np.zeros((LAYERS * TILES, P, 1024), np.float32)
    swap, _ = rope_swap()
    o_xbc, o_dt, o_q, o_kv, o_f = 1024, 1024 + 1536, 1024 + 1536 + 32, 1024 + 1536 + 32 + QL, \
        1024 + 1536 + 32 + QL + KVL + ROPE
    for layer in range(LAYERS):
        w_in, w_gate, w_up = w["w_in"][layer], w["w_gate"][layer], w["w_up"][layer]

        def put(stage, k, m):
            tile = tiles[layer * TILES + STAGES[stage][0] + k]
            m = m.transpose(1, 0, 2).reshape(P, -1)
            tile[:, :m.shape[1]] = m

        def cols(matrix, at, n=P):
            return matrix[:, at:at + n].reshape(-1, P, n)
        for k in range(XBC_B):
            put("proj", k, cols(w_in, o_xbc + k * P))
        pe = w_in[:, o_kv + KVL:o_kv + KVL + ROPE]
        put("proj", XBC_B, np.concatenate([w_in[:, o_dt:o_dt + 32], pe[:, swap], pe, pe], 1).reshape(-1, P, P))
        for k in range(KVB):
            put("proj", XBC_B + 1 + k, cols(w_in, o_kv + k * P))
        for k in range(QB):
            put("proj", XBC_B + 1 + KVB + k, cols(w_in, o_q + k * P))
        for k in range(DB):
            put("z", k, cols(w_in, k * P))
            put("f", k, cols(w_in, o_f + k * P))
            put("w_o", k, cols(w["w_o"][layer], k * P))
            for b, name in enumerate(("ssd", "mla", "fft")):
                put(f"out_{name}", 2 * k, cols(w_gate, b * D + k * P))
                put(f"out_{name}", 2 * k + 1, cols(w[f"w_{name}_out"][layer], k * P))
        q_up = w["w_q_up"][layer].reshape(QB, P, HEADS, HD + ROPE)
        q_up = np.concatenate([q_up, q_up[..., HD:][..., swap]], 3)
        kv_up = w["w_kv_up"][layer].reshape(KVB, P, HEADS, 2 * HD)
        for half in range(2):
            for i in range(4):
                h = half * HALF + 2 * i
                put(f"heads{half}", i, q_up[:, :, h:h + 2].transpose(2, 0, 1, 3).reshape(2 * QB, P, P))
            for i in range(2):
                h = half * HALF + 4 * i
                k_part = kv_up[:, :, h:h + 4, :HD].reshape(KVB, P, 2, 2 * HD).transpose(2, 0, 1, 3)
                put(f"heads{half}", 4 + i, k_part.reshape(2 * KVB, P, P))
                put(f"heads{half}", 6 + i, kv_up[:, :, h:h + 4, HD:].reshape(KVB, P, 4 * HD))
            for i in range(FF_H):
                b = half * FF_H + i
                put(f"up{half}", 2 * i, cols(w_up, b * P))
                put(f"up{half}", 2 * i + 1, cols(w_up, (FF_B + b) * P))
                put(f"down{half}", i, w["w_down"][layer][b * P:(b + 1) * P].reshape(1, P, D))
    return tiles


def pack_ada(w):
    m = w["w_ada"].reshape(LAYERS, DB, P, SIDE, SIDE_TILES, P)
    return m.transpose(0, 3, 2, 4, 1, 5).reshape(LAYERS, SIDE, P, SIDE_TILES * 1024)


def pack_params(w):
    out = np.zeros((LAYERS, P, N_PARAMS), np.float32)

    def put(name, value):
        at, n = PARAMS[name]
        out[:, :, at:at + n] = value.transpose(1, 0, 2)

    def columns(v):
        return v.reshape(LAYERS, -1, P).transpose(2, 0, 1)
    for name in ("b_ada", "g_pre_mix", "g_post_mix", "g_pre_ffn", "g_post_ffn", "b_gate"):
        put(name, columns(w[name]))
    put("g_ssd", columns(w["g_ssd_norm"]))
    put("g_q", columns(w["g_q_norm"]))
    put("g_kv", columns(w["g_kv_norm"]))
    put("conv_b", columns(w["conv_ssd_b"]))
    put("conv_w", w["conv_ssd_w"].reshape(LAYERS, 3, XBC_B, P).transpose(3, 0, 2, 1).reshape(P, LAYERS, -1))
    put("ffn_b", w["conv_ffn_b"].reshape(LAYERS, 2, FF_B, P).transpose(3, 0, 2, 1).reshape(P, LAYERS, -1))
    put("ffn_w", w["conv_ffn_w"].reshape(LAYERS, 3, 2, FF_B, P).transpose(4, 0, 3, 2, 1).reshape(P, LAYERS, -1))
    put("d_skip", columns(np.repeat(w["d_skip"], HD, axis=1)))
    put("dt_bias", np.broadcast_to(w["dt_bias"].reshape(1, LAYERS, 32), (P, LAYERS, 32)))
    put("a_log", np.broadcast_to(w["a_log"].reshape(1, LAYERS, 32), (P, LAYERS, 32)))
    return out


def feature_major(v):
    return v.reshape(v.shape[0], -1, P).transpose(2, 1, 0)


def kernel(**inputs):
    import concourse.bacc as bacc
    from concourse.bass_utils import run_bass_kernel_spmd

    w = {k: np.ascontiguousarray(v) for k, v in inputs.items()}
    arrays = {
        "in_x": feature_major(np.concatenate([w["x_prompt"][0], w["x_sample"][0]], 0)),
        "in_cond": feature_major(np.stack([w["c_ctx"], w["c"][0]])),
        "in_state": w["state_ssm"][0].transpose(0, 4, 1, 2, 3).reshape(LAYERS, STATE, 2, D),
        "in_ckv": w["cache_ckv"][0].reshape(LAYERS, PAST, KVB, P).transpose(0, 3, 2, 1),
        "in_kpe": w["cache_kpe"][0].transpose(0, 2, 1),
        "in_params": pack_params(w),
        "in_consts": constant_tables(),
        "in_weights": pack_weights(w),
        "in_ada": pack_ada(w),
    }
    arrays = {k: np.ascontiguousarray(v) for k, v in arrays.items()}
    outs = {
        "out_x": (P, DB, T),
        "out_ckv": (LAYERS, P, KVB, CTX),
        "out_kpe": (LAYERS, ROPE, CTX),
        "out_state": (LAYERS, 2, STATE, D),
    }
    nc = bacc.Bacc("TRN2", target_bir_lowering=False, num_devices=1)
    args = [nc.dram_tensor(k, v.shape, F32, kind="ExternalInput").ap() for k, v in arrays.items()]
    args += [nc.dram_tensor(k, s, F32, kind="ExternalOutput").ap() for k, s in outs.items()]
    build_program(nc, *args)
    r = run_bass_kernel_spmd(nc, [arrays], core_ids=[0]).results[0]
    y = r["out_x"].transpose(2, 1, 0).reshape(T, D)
    return (
        y[None, :CTX], y[None, CTX:],
        r["out_ckv"].transpose(0, 3, 2, 1).reshape(1, LAYERS, CTX, KVL),
        r["out_kpe"].transpose(0, 2, 1)[None],
        r["out_state"].reshape(LAYERS, 2, STATE, HEADS, HD).transpose(0, 1, 3, 4, 2)[None],
    )
```
